# Optimizing a Trainium2 kernel written in Bass

```python
import jax, jax.numpy as jnp
from jax import lax
import numpy as np

D_MODEL = 1024
BATCH = 1
SEQ = 512
DEPTH = 1

RWKV_HEAD_DIM = 64
RWKV_WIDTH = D_MODEL // 2
RWKV_HEADS = RWKV_WIDTH // RWKV_HEAD_DIM
RWKV_DECAY_LORA = 64
RWKV_AAA_LORA = 64
RWKV_GATE_LORA = 128
RWKV_LN_EPS = 64e-5

HGRN_HEAD_DIM = 128
HGRN_WIDTH = D_MODEL // 2
HGRN_HEADS = HGRN_WIDTH // HGRN_HEAD_DIM
HGRN_VALUE_DIM = HGRN_WIDTH // HGRN_HEADS
HGRN_CHUNK = 64
F_FLOOR = 1e-30

MLA_HEADS = 8
MLA_Q_RANK = D_MODEL // 4
MLA_KV_RANK = D_MODEL // 8
MLA_NOPE_DIM = 64
MLA_ROPE_DIM = 32
MLA_V_DIM = 64
MLA_WIDTH = MLA_HEADS * MLA_V_DIM
MLA_SCALE = (MLA_NOPE_DIM + MLA_ROPE_DIM) ** -0.5
Q_BLOCK = 128
ROPE_THETA = 10000.0
NEG_BIG = -1e30

N_BRANCHES = 3
D_FF = 2816
CONV_WIDTH = 3
NORM_EPS = 1e-6

RW_SIZES = (RWKV_WIDTH, RWKV_WIDTH, RWKV_WIDTH, RWKV_DECAY_LORA, RWKV_AAA_LORA, RWKV_GATE_LORA)
HG_SIZES = (HGRN_WIDTH, HGRN_WIDTH, HGRN_WIDTH, HGRN_WIDTH)
MLA_SIZES = (MLA_Q_RANK, MLA_KV_RANK, MLA_ROPE_DIM)
RW_COLS = sum(RW_SIZES)
HG_COLS = sum(HG_SIZES)
MLA_COLS = sum(MLA_SIZES)
GATE_COLS = N_BRANCHES * D_MODEL
IN_SIZES = (RW_COLS, HG_COLS, MLA_COLS, GATE_COLS)
IN_WIDTH = sum(IN_SIZES)

kernel_name = 'hybrid_rwkv7_hgrn2_mla_adaln_trunk'

def _split(u, sizes):
    cuts, acc = [], 0
    for s in sizes[:-1]:
        acc += s
        cuts.append(acc)
    return jnp.split(u, cuts, axis=-1)

def _rmsnorm(x, eps=NORM_EPS):
    x32 = x.astype(jnp.float32)
    y = x32 * lax.rsqrt(jnp.mean(x32 * x32, axis=-1, keepdims=True) + eps)
    return y.astype(x.dtype)

def _modulate(x, shift, scale):
    return _rmsnorm(x) * (1.0 + scale[:, None, :]) + shift[:, None, :]

def _token_shift(u):
    return jnp.pad(u[:, :-1], ((0, 0), (1, 0), (0, 0)))

def _rope_tables(positions):
    inv_freq = ROPE_THETA ** (-jnp.arange(0, MLA_ROPE_DIM, 2, dtype=jnp.float32) / MLA_ROPE_DIM)
    ang = positions.astype(jnp.float32)[..., None] * inv_freq
    return jnp.cos(ang), jnp.sin(ang)

def _apply_rope(x, cos, sin):
    x1, x2 = jnp.split(x, 2, axis=-1)
    return jnp.concatenate([x1 * cos - x2 * sin, x2 * cos + x1 * sin], axis=-1).astype(x.dtype)

def _rwkv7_scan(r, w, k, v, a, b):
    B, S, H, N = r.shape
    xs = tuple(jnp.moveaxis(t.astype(jnp.float32), 1, 0) for t in (r, w, k, v, a, b))

    def step(St, inp):
        r_t, w_t, k_t, v_t, a_t, b_t = inp
        sa = jnp.einsum('bhij,bhj->bhi', St, a_t)
        St = St * w_t[:, :, None, :] + sa[..., None] * b_t[:, :, None, :] + v_t[..., None] * k_t[:, :, None, :]
        return St, jnp.einsum('bhij,bhj->bhi', St, r_t)

    _, y = lax.scan(step, jnp.zeros((B, H, N, N), jnp.float32), xs)
    return jnp.moveaxis(y, 0, 1).astype(r.dtype)

def _rwkv7_branch(u, mu, w0, w2, a0, a2, g2, k_k, k_a, r_k, ln_w, ln_b):
    B, S, _ = u.shape
    H, N = RWKV_HEADS, RWKV_HEAD_DIM
    u = u + (_token_shift(u) - u) * mu
    r, k, v, wl, al, gl = _split(u, RW_SIZES)
    w = -jax.nn.softplus(-(w0 + jnp.tanh(wl) @ w2)) - 0.5
    decay = jnp.exp(-jnp.exp(w.astype(jnp.float32)))
    a = jax.nn.sigmoid(a0 + al @ a2)
    g = jax.nn.sigmoid(gl) @ g2
    heads = lambda t: t.reshape(B, S, H, N)
    r, k, v, a, decay = heads(r), heads(k), heads(v), heads(a), heads(decay)
    kk = (k * k_k.reshape(H, N)).astype(jnp.float32)
    kk = kk / jnp.maximum(jnp.sqrt(jnp.sum(kk * kk, axis=-1, keepdims=True)), 1e-12)
    kk = kk.astype(k.dtype)
    k = k * (1.0 + (a - 1.0) * k_a.reshape(H, N))
    y = _rwkv7_scan(r, decay, k, v, -kk, kk * a)
    y32 = y.astype(jnp.float32)
    mean = jnp.mean(y32, axis=-1, keepdims=True)
    var = jnp.mean((y32 - mean) ** 2, axis=-1, keepdims=True)
    y = ((y32 - mean) * lax.rsqrt(var + RWKV_LN_EPS)).astype(y.dtype)
    y = y * ln_w.reshape(H, N) + ln_b.reshape(H, N)
    y = y + jnp.sum(r * k * r_k, axis=-1, keepdims=True) * v
    return y.reshape(B, S, H * N) * g

def _gla_chunked(q, k, v, log_f):
    B, S, H, DK = q.shape
    NC = S // HGRN_CHUNK
    to_chunks = lambda t: t.astype(jnp.float32).reshape(B, NC, HGRN_CHUNK, H, -1).transpose(1, 0, 3, 2, 4)
    xs = (to_chunks(q), to_chunks(k), to_chunks(v), to_chunks(log_f))
    causal = jnp.tril(jnp.ones((HGRN_CHUNK, HGRN_CHUNK), bool))

    def step(St, inp):
        q_c, k_c, v_c, g_c = inp
        bcum = jnp.cumsum(g_c, axis=2)
        o_inter = jnp.einsum('bhtd,bhde->bhte', q_c * jnp.exp(bcum), St)
        diff = bcum[:, :, :, None, :] - bcum[:, :, None, :, :]
        dec = jnp.exp(jnp.where(causal[:, :, None], diff, NEG_BIG))
        A = jnp.einsum('bhtsd,bhsd->bhts', q_c[:, :, :, None, :] * dec, k_c)
        o_intra = jnp.einsum('bhts,bhse->bhte', A, v_c)
        b_last = bcum[:, :, -1:, :]
        St = jnp.exp(b_last[:, :, 0, :])[..., None] * St + jnp.einsum('bhsd,bhse->bhde', k_c * jnp.exp(b_last - bcum), v_c)
        return St, o_inter + o_intra

    _, o = lax.scan(step, jnp.zeros((B, H, DK, v.shape[-1]), jnp.float32), xs)
    return o.transpose(1, 0, 3, 2, 4).reshape(B, S, H, v.shape[-1])

def _hgrn2_branch(u, lb, norm_w):
    B, S, _ = u.shape
    H = HGRN_HEADS
    q, fz, i, og = _split(u, HG_SIZES)
    fz32 = fz.astype(jnp.float32).reshape(B, S, H, HGRN_HEAD_DIM)
    lb = lb.reshape(H, HGRN_HEAD_DIM)
    f = lb + (1.0 - lb) * jax.nn.sigmoid(fz32)
    log_f = jnp.log(jnp.maximum(f, F_FLOOR))
    key = (1.0 - lb) * jax.nn.sigmoid(-fz32)
    o = _gla_chunked(q.reshape(B, S, H, HGRN_HEAD_DIM), key, i.reshape(B, S, H, HGRN_VALUE_DIM), log_f)
    o = _rmsnorm(o).astype(u.dtype) * norm_w * jax.nn.silu(og.reshape(B, S, H, HGRN_VALUE_DIM))
    return o.reshape(B, S, H * HGRN_VALUE_DIM)

def _mla_branch(u, cos, sin, q_norm_w, w_uq, kv_norm_w, w_ukv):
    B, S, _ = u.shape
    H = MLA_HEADS
    cq, ckv, k_rope = _split(u, MLA_SIZES)
    q = ((_rmsnorm(cq) * q_norm_w) @ w_uq).reshape(B, S, H, MLA_NOPE_DIM + MLA_ROPE_DIM)
    q_nope, q_rope = jnp.split(q, [MLA_NOPE_DIM], axis=-1)
    kv = ((_rmsnorm(ckv) * kv_norm_w) @ w_ukv).reshape(B, S, H, MLA_NOPE_DIM + MLA_V_DIM)
    k_nope, v = jnp.split(kv, [MLA_NOPE_DIM], axis=-1)
    q_rope = _apply_rope(q_rope, cos[:, :, None, :], sin[:, :, None, :])
    k_rope = _apply_rope(k_rope, cos, sin)
    NB = S // Q_BLOCK
    to_blocks = lambda t: t.reshape(B, NB, Q_BLOCK, H, -1).swapaxes(0, 1)
    k_pos = jnp.arange(S, dtype=jnp.int32)

    def attend(args):
        blk, qn, qr = args
        s = jnp.einsum('bqhd,bkhd->bhqk', qn, k_nope) + jnp.einsum('bqhd,bkd->bhqk', qr, k_rope)
        s = s.astype(jnp.float32) * MLA_SCALE
        q_pos = blk * Q_BLOCK + jnp.arange(Q_BLOCK, dtype=jnp.int32)
        s = jnp.where(k_pos[None, :] <= q_pos[:, None], s, NEG_BIG)
        p = jax.nn.softmax(s, axis=-1).astype(v.dtype)
        return jnp.einsum('bhqk,bkhd->bqhd', p, v)

    o = lax.map(attend, (jnp.arange(NB, dtype=jnp.int32), to_blocks(q_nope), to_blocks(q_rope)))
    return o.swapaxes(0, 1).reshape(B, S, H * MLA_V_DIM)

def _hybrid_mixer(h, cos, sin, lb, w_in, rw_mu, rw_w0, rw_w2, rw_a0, rw_a2, rw_g2, rw_k_k, rw_k_a, rw_r_k,
                  rw_ln_w, rw_ln_b, hg_norm_w, q_norm_w, w_uq, kv_norm_w, w_ukv, proj_a, proj_b, proj_c, w_out):
    B, S, _ = h.shape
    u = h @ w_in
    u_rw, u_hg, u_mla, u_gate = _split(u, IN_SIZES)
    o_a = _rwkv7_branch(u_rw, rw_mu, rw_w0, rw_w2, rw_a0, rw_a2, rw_g2, rw_k_k, rw_k_a, rw_r_k, rw_ln_w, rw_ln_b)
    o_b = _hgrn2_branch(u_hg, lb, hg_norm_w)
    o_c = _mla_branch(u_mla, cos, sin, q_norm_w, w_uq, kv_norm_w, w_ukv)
    gates = jax.nn.sigmoid(u_gate).reshape(B, S, N_BRANCHES, D_MODEL)
    y = gates[:, :, 0] * (o_a @ proj_a) + gates[:, :, 1] * (o_b @ proj_b) + gates[:, :, 2] * (o_c @ proj_c)
    return y @ w_out

def _conv_glu_ffn(h, w_up, conv_w, conv_b, w_down):
    u = h @ w_up
    u = lax.conv_general_dilated(u, conv_w[:, None, :].astype(u.dtype), window_strides=(1,),
                                 padding=[(CONV_WIDTH - 1, 0)], dimension_numbers=('NWC', 'WIO', 'NWC'),
                                 feature_group_count=2 * D_FF) + conv_b
    val, gate = jnp.split(u, 2, axis=-1)
    return (jax.nn.silu(gate) * val) @ w_down

def setup_inputs(seed: int = 0) -> dict:
    key = jax.random.key(seed)
    ks = iter(jax.random.split(key, 40))

    def nrm(shape, scale):
        return jax.random.normal(next(ks), shape, jnp.float32) * scale

    L, D = DEPTH, D_MODEL
    x = nrm((BATCH, SEQ, D), 1.0)
    c = nrm((BATCH, D), 1.0)
    offsets = jax.random.randint(next(ks), (BATCH, 1), 0, 4096, dtype=jnp.int32)
    positions = offsets + jnp.arange(SEQ, dtype=jnp.int32)[None, :]
    return {
        'x': x, 'c': c, 'positions': positions,
        'ada_w': nrm((L, D, 6 * D), 0.5 * D ** -0.5),
        'ada_b': nrm((L, 6 * D), 0.05),
        'w_in': nrm((L, D, IN_WIDTH), D ** -0.5),
        'rwkv_mu': jax.random.uniform(next(ks), (L, RW_COLS), jnp.float32, 0.0, 1.0),
        'rwkv_w0': nrm((L, RWKV_WIDTH), 1.0),
        'rwkv_w2': nrm((L, RWKV_DECAY_LORA, RWKV_WIDTH), 0.5 * RWKV_DECAY_LORA ** -0.5),
        'rwkv_a0': nrm((L, RWKV_WIDTH), 0.5),
        'rwkv_a2': nrm((L, RWKV_AAA_LORA, RWKV_WIDTH), 0.5 * RWKV_AAA_LORA ** -0.5),
        'rwkv_g2': nrm((L, RWKV_GATE_LORA, RWKV_WIDTH), RWKV_GATE_LORA ** -0.5),
        'rwkv_k_k': 0.85 + nrm((L, RWKV_WIDTH), 0.05),
        'rwkv_k_a': 1.0 + nrm((L, RWKV_WIDTH), 0.05),
        'rwkv_r_k': nrm((L, RWKV_HEADS, RWKV_HEAD_DIM), 0.1),
        'rwkv_ln_w': 1.0 + nrm((L, RWKV_WIDTH), 0.05),
        'rwkv_ln_b': nrm((L, RWKV_WIDTH), 0.02),
        'hgrn_lb': 1.0 + nrm((L, HGRN_WIDTH), 0.1),
        'hgrn_norm_w': 1.0 + nrm((L, HGRN_VALUE_DIM), 0.05),
        'mla_q_norm_w': 1.0 + nrm((L, MLA_Q_RANK), 0.05),
        'mla_w_uq': nrm((L, MLA_Q_RANK, MLA_HEADS * (MLA_NOPE_DIM + MLA_ROPE_DIM)), MLA_Q_RANK ** -0.5),
        'mla_kv_norm_w': 1.0 + nrm((L, MLA_KV_RANK), 0.05),
        'mla_w_ukv': nrm((L, MLA_KV_RANK, MLA_HEADS * (MLA_NOPE_DIM + MLA_V_DIM)), MLA_KV_RANK ** -0.5),
        'branch_proj_a': nrm((L, RWKV_WIDTH, D), RWKV_WIDTH ** -0.5),
        'branch_proj_b': nrm((L, HGRN_WIDTH, D), HGRN_WIDTH ** -0.5),
        'branch_proj_c': nrm((L, MLA_WIDTH, D), MLA_WIDTH ** -0.5),
        'w_out': nrm((L, D, D), D ** -0.5),
        'ffn_w_up': nrm((L, D, 2 * D_FF), D ** -0.5),
        'ffn_conv_w': nrm((L, CONV_WIDTH, 2 * D_FF), 0.5),
        'ffn_conv_b': nrm((L, 2 * D_FF), 0.02),
        'ffn_w_down': nrm((L, D_FF, D), D_FF ** -0.5),
        'final_norm_w': 1.0 + nrm((D,), 0.05),
    }

def reference(x, c, positions, ada_w, ada_b, w_in, rwkv_mu, rwkv_w0, rwkv_w2, rwkv_a0, rwkv_a2, rwkv_g2,
              rwkv_k_k, rwkv_k_a, rwkv_r_k, rwkv_ln_w, rwkv_ln_b, hgrn_lb, hgrn_norm_w, mla_q_norm_w, mla_w_uq,
              mla_kv_norm_w, mla_w_ukv, branch_proj_a, branch_proj_b, branch_proj_c, w_out, ffn_w_up,
              ffn_conv_w, ffn_conv_b, ffn_w_down, final_norm_w):
    p = jax.nn.softmax(hgrn_lb.astype(jnp.float32), axis=0)
    lower_bounds = jnp.cumsum(p, axis=0) - p[0:1]
    cos, sin = _rope_tables(positions)
    cond = jax.nn.silu(c)
    B = x.shape[0]
    for l in range(DEPTH):
        mod = (cond @ ada_w[l] + ada_b[l]).reshape(B, 6, D_MODEL)
        sh1, sc1, g1, sh2, sc2, g2 = [mod[:, j] for j in range(6)]
        h = _modulate(x, sh1, sc1)
        x = x + g1[:, None, :] * _hybrid_mixer(
            h, cos, sin, lower_bounds[l], w_in[l], rwkv_mu[l], rwkv_w0[l], rwkv_w2[l], rwkv_a0[l], rwkv_a2[l],
            rwkv_g2[l], rwkv_k_k[l], rwkv_k_a[l], rwkv_r_k[l], rwkv_ln_w[l], rwkv_ln_b[l], hgrn_norm_w[l],
            mla_q_norm_w[l], mla_w_uq[l], mla_kv_norm_w[l], mla_w_ukv[l], branch_proj_a[l], branch_proj_b[l],
            branch_proj_c[l], w_out[l])
        h = _modulate(x, sh2, sc2)
        x = x + g2[:, None, :] * _conv_glu_ffn(h, ffn_w_up[l], ffn_conv_w[l], ffn_conv_b[l], ffn_w_down[l])
    return _rmsnorm(x) * final_norm_w


_drawn_inputs = setup_inputs


def setup_inputs(seed=0):
    import zlib

    import numpy as np

    out = dict(_drawn_inputs(seed))
    spreads = {}
    factors = {'rwkv_w2': 8.0,
     'rwkv_a2': 2.88,
     'rwkv_k_k': 64.0,
     'rwkv_k_a': 8.0,
     'rwkv_ln_w': 26.475,
     'rwkv_ln_b': 64.0,
     'hgrn_norm_w': 22.237,
     'mla_q_norm_w': 8.0,
     'mla_kv_norm_w': 8.0,
     'ffn_conv_b': 22.382}
    for name, (base, spread) in spreads.items():
        noise = np.random.default_rng([zlib.crc32(name.encode()), seed]).standard_normal(out[name].shape)
        drawn = base * np.exp(spread * noise) if base else spread * noise
        out[name] = __import__('jax').numpy.asarray(drawn.astype(out[name].dtype))
    for name, factor in factors.items():
        out[name] = (out[name] * factor).astype(out[name].dtype)
    return out
```

```python
from contextlib import ExitStack

import numpy as np

import concourse.bass as bass
from concourse import mybir

F32 = mybir.dt.float32
F32R = mybir.dt.float32r
I32 = mybir.dt.int32
ALU = mybir.AluOpType
ACT = mybir.ActivationFunctionType
AX = mybir.AxisListType

P = 128
T = 512
D = 1024
KD = D // P
FF = 2816
NF = FF // P
RW_TILES = 4
CH = 64
PAIRS = T // P
CHUNKS = T // CH
HG = 4
ML = 8
NOPE, ROPE = 64, 32
QK = NOPE + ROPE
MLA_SCALE = QK ** -0.5
NORM_EPS, RWKV_EPS = 1e-6, 64e-5
RW_COL, HG_COL, ML_COL, GATE_COL = 0, 1792, 3840, 4256
E_HALF = float(np.exp(-0.5))
GROUP = 2048

V_ADA, V_MU, V_W0, V_A0, V_KK, V_KA, V_RK, V_LNW, V_LNB = 0, 48, 62, 66, 70, 74, 78, 82, 86
V_LB, V_HN, V_QN, V_KV, V_FIN, V_C = 90, 94, 95, 97, 98, 106
V_ROWS = 114


def make_constants():
    s = np.arange(P)[:, None]
    t = np.arange(P)[None, :]
    same = (s // CH) == (t // CH)
    strict = (same & (s < t)).astype(np.float32)
    incl = (same & (s <= t)).astype(np.float32)
    c = {"ident": np.eye(P, dtype=np.float32), "rw_mask": np.concatenate([strict, incl, strict, incl], 1)}
    c["pair_t"] = ((s // 2 == t // 2) & (s < t)).astype(np.float32)
    levels = []
    for n in (2, 4, 8, 16, 32):
        first = [x for x in range(P) if (x // n) % 2 == 0]
        levels.append(np.array([[float((tt // (2 * n) == x // (2 * n)) and (tt // n) % 2 == 1) for x in first]
                                for tt in range(P)], np.float32))
    c["level"] = np.concatenate(levels, 1)
    c["ones"] = np.ones((P, P), np.float32)
    c["heads"] = ((s // CH) == (t // CH)).astype(np.float32)
    c["eye64"] = (s % CH == np.arange(CH)[None, :]).astype(np.float32)
    c["causal"] = np.where(t <= s, 0.0, -1e30).astype(np.float32)
    inv = (10000.0 ** (-np.arange(0, ROPE, 2, dtype=np.float32) / ROPE)).astype(np.float32)
    c["freq"] = np.tile(inv, P // 16)[:, None].astype(np.float32)
    c["rsign"] = np.where(np.arange(P) % ROPE < ROPE // 2, -1.0, 1.0)[:, None].astype(np.float32)
    hg = []
    for n in (1, 2, 4, 8, 16, 32, 64):
        second = [x for x in range(P) if (x // n) % 2 == 1]
        hg.append(np.array([[int((ss // (2 * n) == x // (2 * n)) and (ss // n) % 2 == 0) for x in second]
                            for ss in range(P)], np.int32))
    at, off = {}, 0
    for k, v in c.items():
        at[k] = (off, off + v.shape[1])
        off += v.shape[1]
    return np.concatenate(list(c.values()), 1), at, np.concatenate(hg, 1)


CONST_F, CONST_AT, CONST_I = make_constants()


def weight_groups(a):
    g = []
    kt = lambda w: w.rearrange("(k p) n -> p k n", p=P)
    ada, win = kt(a["ada_w"][0]), kt(a["w_in"][0])
    up, down = kt(a["ffn_w_up"][0]), kt(a["ffn_w_down"][0])
    for j in range(8):
        g.append(("raw", [(ada[:, :, 256 * j:256 * (j + 1)], 0, 256)], KD, 256))
    for c0 in (1536, 0, 256, 512, 768, 1024, 1280):
        g.append(("split", [(win[:, :, c0:c0 + 256], 0, 256)], KD, 256))
    for j in range(8, 24):
        g.append(("raw", [(ada[:, :, 256 * j:256 * (j + 1)], 0, 256)], KD, 256))
    for j in range(8):
        c0 = HG_COL + 256 * j
        g.append(("split", [(win[:, :, c0:c0 + 256], 0, 256)], KD, 256))
    g.append(("split", [(win[:, :, ML_COL:ML_COL + 256], 0, 256)], KD, 256))
    c0 = ML_COL + 256
    g.append(("split", [(win[:, :, c0:c0 + 160], 0, 160), (win[:, :, c0 + 144:c0 + 160], 160, 16),
                        (win[:, :, c0 + 128:c0 + 144], 176, 16)], KD, 192))
    proj = [kt(a[f"branch_proj_{b}"][0]) for b in "abc"]
    for half in range(2):
        for b in range(3):
            for q in range(2):
                c0 = GATE_COL + b * D + half * 512 + q * 256
                g.append(("split", [(win[:, :, c0:c0 + 256], 0, 256)], KD, 256))
            g.append(("split", [(proj[b][:, :, 512 * half:512 * (half + 1)], 0, 512)], 4, 512))
    wo = kt(a["w_out"][0])
    for q in range(4):
        g.append(("split", [(wo[:, :, 256 * q:256 * (q + 1)], 0, 256)], KD, 256))
    for j in range(NF):
        g.append(("split", [(up[:, :, P * j:P * (j + 1)], 0, P), (up[:, :, FF + P * j:FF + P * (j + 1)], P, P)], KD, 256))
    for q in range(4):
        for k0 in (0, 8, 16):
            nk = min(8, NF - k0)
            g.append(("split", [(down[:, k0:k0 + nk, 256 * q:256 * (q + 1)], 0, 256)], nk, 256))
    return g


G_ADA0, G_RW, G_ADA1, G_HG, G_ML, G_MIX, G_OUT, G_UP, G_DOWN = 0, 8, 15, 31, 39, 41, 59, 63, 85


def trunk(nc, a, out):
    groups = weight_groups(a)
    ctx = ExitStack()
    with ctx:
        def sb(name, shape, dt=F32, c=ctx):
            return c.enter_context(nc.sbuf_tensor(name, shape, dt))

        sems = {}

        def sem(name):
            if name not in sems:
                sems[name] = ctx.enter_context(nc.semaphore(name))
            return sems[name]

        wring = sb("wring", [P, 2, GROUP])
        whi = sb("whi", [P, 2, GROUP], F32R)
        wlo = sb("wlo", [P, 2, GROUP], F32R)
        hhi = sb("hhi", [P, KD, T], F32R)
        hlo = sb("hlo", [P, KD, T], F32R)
        const = sb("const", [P, CONST_F.shape[1]])
        consti = sb("consti", [P, 7, CH], I32)
        vec = sb("vec", [P, V_ROWS])
        convv = sb("convv", [P, 2, 88])
        mod = sb("mod", [P, 48])
        cond = sb("cond", [P, KD])
        small = sb("small", [P, 64])
        outs = sb("outs", [P, 12, T])
        scope = ExitStack()
        arena = sb("arena", [P, 46, T], c=scope)
        scope.close()
        scope = ExitStack()
        ohi = sb("ohi", [P, 4, T], F32R, c=scope)
        olo = sb("olo", [P, 4, T], F32R, c=scope)
        mix = sb("mix", [P, 37, T], c=scope)
        scope.close()
        scope = ExitStack()
        tail = sb("tail", [P, 2, T], c=scope)
        acthi = sb("acthi", [P, NF, T], F32R, c=scope)
        actlo = sb("actlo", [P, NF, T], F32R, c=scope)
        scope.close()
        scope = ExitStack()
        fin = sb("fin", [P, 12, T], c=scope)
        scope.close()
        SQF = fin[:, 2:10, :]
        ps = [ctx.enter_context(nc.psum_tensor(f"bank{b}", [P, T], F32))[:] for b in range(8)]

        def cst(name):
            lo, hi = CONST_AT[name]
            return const[:, lo:hi]

        ident = cst("ident")
        ones = cst("ones")
        heads = cst("heads")

        def col(row, n=1):
            return vec[:, row:row + n]

        EPS, REPS, ONE = small[:, 0:1], small[:, 1:2], small[:, 2:3]
        LBV, OMLB = small[:, 4:8], small[:, 8:12]
        NEG_W0 = small[:, 12:16]
        ONE_MU = small[:, 16:30]

        xtok = arena[:, 0:8, :].rearrange("p a t -> p (a t)").rearrange("p (a d) -> p a d", a=4)
        xT = arena[:, 8:16, :]
        sqT = arena[:, 16:24, :]
        rstd = arena[:, 24, :]
        vrows = arena[:, 25, 0:P]
        crow = arena[:, 26, 0:2 * P].rearrange("p (a b) -> p a b", a=2)
        R, K, V, DEC, AA, KK = (arena[:, 4 * i:4 * i + 4, :] for i in range(6))
        LORA = arena[:, 24, :]
        GL = arena[:, 25, :]
        LW = arena[:, 26, :]
        GW = arena[:, 27, :]
        ABR = arena[:, 28:36, :]
        TM = arena[:, 36:38, :].rearrange("p a t -> p (a t)").rearrange("p (i t) -> p i t", i=8)
        TT = arena[:, 38:40, :].rearrange("p a t -> p (a t)").rearrange("p (i t) -> p i t", i=8)
        YH = arena[:, 40, :]
        AV = arena[:, 41:43, :].rearrange("p a t -> p (a t)").rearrange("p (i t) -> p i t", i=8)
        WY = arena[:, 43:45, :].rearrange("p a t -> p (a t)").rearrange("p (i t) -> p i t", i=8)
        VTK = arena[:, 45, :].rearrange("p (q f) -> p q f", q=PAIRS)
        MT, NN = arena[:, 41, :], arena[:, 42, :]
        PP, PINV = outs[:, 4, :], outs[:, 5, :]
        AR = outs[:, 6:8, :].rearrange("p a t -> p (a t)").rearrange("p (q w t) -> p q w t", q=PAIRS, w=2)
        BH, KH, SCR = outs[:, 8, :], outs[:, 9, :], outs[:, 10, :]
        KTOK = [outs[:, i, :].rearrange("p (q f) -> p q f", q=PAIRS) for i in (10, 11)]
        HQ, HF, HK, HV, HO, SUF = (arena[:, 4 * i:4 * i + 4, :] for i in range(6))
        QC = arena[:, 24:26, :].rearrange("p a t -> p (a t)").rearrange("p (h t) -> p h t", h=HG)
        KN = arena[:, 26:30, :]
        AT = arena[:, 30:34, :].rearrange("p h (c t) -> p h c t", c=4)
        HVT = arena[:, 34:38, :].rearrange("p h (c t) -> p h c t", c=4)
        HKT = arena[:, 38:42, :].rearrange("p h (c t) -> p h c t", c=4)
        HS = arena[:, 42:46, :].rearrange("p h (c t) -> p h c t", c=4)
        HSCR = outs[:, 8:12, :]
        CQ = arena[:, 0:2, :]
        CKV = arena[:, 2, :]
        KR = arena[:, 3, :]
        MSQ = arena[:, 4:7, :]
        MRS = arena[:, 7:9, :]
        WUQ = arena[:, 9:11, :]
        WUK, WUV = arena[:, 12, :], arena[:, 13, :]
        QH = arena[:, 14:22, :]
        KHD = arena[:, 22:30, :]
        VM = arena[:, 30:34, :]
        COS, SIN, ANG, RED = (arena[:, i, :] for i in (34, 35, 36, 37))
        WROT = arena[:, 38, :].rearrange("p (k n) -> p k n", k=2)
        PRB = arena[:, 39:41, :]
        PT = arena[:, 41:45, :]
        RT = arena[:, 45, :]
        WROPE = outs[:, 8, :].rearrange("p (k n) -> p k n", k=2)
        KRR = outs[:, 9, :]
        GATE = mix[:, 0:4, :]
        YT = mix[:, 4:12, :]
        XT2 = mix[:, 20:28, :]
        TMP = mix[:, 12:16, :]
        XTOK2 = mix[:, 28:36, :].rearrange("p a t -> p (a t)").rearrange("p (a d) -> p a d", a=4)
        X1 = outs[:, 0:8, :]
        SQ1 = mix[:, 28:36, :]
        CV = outs[:, 8:10, :]
        CG = outs[:, 10:12, :]

        def mm3(e, o, g, k, m0, m1, rhi, rlo, first, last, ncols):
            hi = whi[:, g % 2, :][:, k * ncols + m0:k * ncols + m1]
            lo = wlo[:, g % 2, :][:, k * ncols + m0:k * ncols + m1]
            e.matmul(o, hi, rhi, start=first, stop=False)
            e.matmul(o, hi, rlo, start=False, stop=False)
            return e.matmul(o, lo, rhi, start=False, stop=last)

        split_no, raw_no = {}, {}
        for i, gr in enumerate(groups):
            n = split_no if gr[0] == "split" else raw_no
            n[i] = len(n)

        landings = {}
        count = [0, 0]
        for g, gr in enumerate(groups):
            count[g % 2] += 16 * len(gr[1])
            landings[g] = count[g % 2]

        def RESULT(q):
            return wring[:, q // 2, (q % 2) * D:(q % 2 + 1) * D]

        def FREE_AT(n):
            return (n + 1) // 2, n // 2

        used, tiles = [], 0
        for g in split_no:
            if g < G_DOWN:
                tiles += 4 if G_MIX <= g < G_OUT and (g - G_MIX) % 3 == 2 else 2
                used.append((sem("tile_ready"), tiles))
            elif (g - G_DOWN) % 3 < 2:
                used.append((sem("down_part"), 2 * ((g - G_DOWN) // 3) + (g - G_DOWN) % 3 + 1))
            else:
                tiles += 2
                used.append((sem("tile_ready"), tiles))

        block = ctx.enter_context(nc.Block())

        @block.sync
        def _(sp):
            sp.dma_start(const[:], a["const_f"]).then_inc(sem("ld_const"), 16)
            sp.dma_start(xtok, a["x"][0].rearrange("(a p) d -> p a d", p=P)).then_inc(sem("ld_x"), 16)
            rows = [("ada_b", V_ADA, 48), ("rwkv_mu", V_MU, 14), ("rwkv_w0", V_W0, 4), ("rwkv_a0", V_A0, 4),
                    ("rwkv_k_k", V_KK, 4), ("rwkv_k_a", V_KA, 4), ("rwkv_r_k", V_RK, 4), ("rwkv_ln_w", V_LNW, 4),
                    ("rwkv_ln_b", V_LNB, 4), ("hgrn_lb", V_LB, 4), ("hgrn_norm_w", V_HN, 1),
                    ("mla_q_norm_w", V_QN, 2), ("mla_kv_norm_w", V_KV, 1), ("final_norm_w", V_FIN, 8), ("c", V_C, 8)]
            for name, r0, n in rows:
                sp.dma_start(vrows[r0:r0 + n, :], a[name].rearrange("(r p) -> r p", p=P)).then_inc(sem("ld_vec"), 16)
            cw = a["ffn_conv_w"].rearrange("(r p) -> r p", p=P)
            sp.dma_start(crow[0:88, 0, :], cw[0:88, :]).then_inc(sem("ld_vec"), 16)
            sp.dma_start(crow[0:44, 1, :], cw[88:132, :]).then_inc(sem("ld_vec"), 16)
            sp.dma_start(crow[44:88, 1, :], a["ffn_conv_b"].rearrange("(r p) -> r p", p=P)).then_inc(sem("ld_vec"), 16)
            sp.dma_start(consti[:].rearrange("p a b -> p (a b)"), a["const_i"]).then_inc(sem("ld_const"), 16)

            def load(g):
                kind, parts, nk, n = groups[g]
                if g - 2 in split_no:
                    sp.wait_ge(sem("w_lo"), split_no[g - 2] + 1)
                elif g >= 2:
                    sp.wait_ge(sem("ada_used"), raw_no[g - 2] + 1)
                dst = wring[:, g % 2, 0:nk * n].rearrange("p (k n) -> p k n", k=nk)
                for src, off, w in parts:
                    sp.dma_start(dst[:, :, off:off + w], src).then_inc(sem(f"w_landed{g % 2}"), 16)

            for g in range(len(groups)):
                load(g)
                if g == G_RW + 1:
                    sp.wait_ge(sem("vec_turned"), 1)
                    sp.wait_ge(sem("h_split"), 1)
                    sp.dma_start(LW[0:64, :], a["rwkv_w2"][0]).then_inc(sem("ld_lora"), 16)
                    sp.dma_start(LW[64:128, :], a["rwkv_a2"][0]).then_inc(sem("ld_lora"), 16)
                    sp.dma_start(GW, a["rwkv_g2"][0]).then_inc(sem("ld_lora"), 16)
                if g == G_ML + 1:
                    sp.wait_ge(sem("hg_out"), 1)
                    uq = a["mla_w_uq"][0].rearrange("(k p) (h n) -> p k h n", p=P, n=QK)
                    ukv = a["mla_w_ukv"][0].rearrange("p (h n) -> p h n", n=P)
                    by_head = lambda v, n: v.rearrange("p (h n) -> p h n", n=n)
                    for k in range(2):
                        sp.dma_start(by_head(WUQ[:, k, :], NOPE), uq[:, k, :, 0:NOPE]).then_inc(sem("ld_mla"), 16)
                        sp.dma_start(by_head(WROPE[:, k, :], ROPE), uq[:, k, :, NOPE:QK]).then_inc(sem("ld_mla"), 16)
                    sp.dma_start(by_head(WUK, NOPE), ukv[:, :, 0:NOPE]).then_inc(sem("ld_mla"), 16)
                    sp.dma_start(by_head(WUV, NOPE), ukv[:, :, NOPE:P]).then_inc(sem("ld_mla"), 16)
                    sp.dma_start(ANG.bitcast(I32), a["positions"][0].partition_broadcast(P)).then_inc(sem("ld_mla"), 16)
                if g == G_MIX + 2:
                    sp.wait_ge(sem("oc_done"), ML)
                    sp.dma_start(XTOK2, a["x"][0].rearrange("(a p) d -> p a d", p=P)).then_inc(sem("ld_x2"), 16)
            for q in range(4):
                sp.wait_ge(sem("rows_ready"), 2 * (q + 1))
                sp.dma_start(out[0, q * P:(q + 1) * P, :], RESULT(q)).then_inc(sem("stored"), 16)
            sp.wait_ge(sem("stored"), 64)

        @block.gpsimd
        def _(pool):
            for g, n in split_no.items():
                w = groups[g][2] * groups[g][3]
                s = g % 2
                pool.wait_ge(sem("w_hi"), n + 1)
                if n >= 2:
                    pool.wait_ge(*used[n - 2])
                pool.tensor_tensor(wlo[:, s, 0:w], wring[:, s, 0:w], whi[:, s, 0:w].bitcast(F32),
                                   ALU.subtract).then_inc(sem("w_lo"), 1)

        @block.tensor
        def _(pe):
            tile_no = [0]

            def bank():
                i = tile_no[0]
                tile_no[0] += 1
                if i >= 2:
                    pe.wait_ge(sem(f"bank_free{i % 2}"), i // 2)
                return ps[i % 2]

            def project(g, cuts, rhi, rlo):
                n = split_no[g]
                pe.wait_ge(sem("w_lo"), n + 1)
                nk, ncols = groups[g][2], groups[g][3]
                for m0, m1 in cuts:
                    o = bank()[0:m1 - m0, :]
                    for k in range(nk):
                        q = mm3(pe, o, g, k, m0, m1, rhi[:, k, :], rlo[:, k, :], k == 0, k == nk - 1, ncols)
                    q.then_inc(sem("tile_ready"), 1)

            PAIR = [(0, P), (P, 2 * P)]

            pe.wait_ge(sem("ld_const"), 32)
            pe.wait_ge(sem("ld_x"), 16)
            for d in range(KD):
                if d >= 4:
                    pe.wait_ge(sem("xt_copied"), d - 3)
                for t in range(4):
                    q = pe.transpose(ps[2 + d % 4][:, P * t:P * (t + 1)], xtok[:, t, P * d:P * (d + 1)], ident)
                q.then_inc(sem("xt_turned"), 1)
            pe.wait_ge(sem("ld_vec"), 18 * 16)
            pe.transpose(ps[6][:, 0:V_ROWS], vrows[0:V_ROWS, :], ident[0:V_ROWS, 0:V_ROWS])
            pe.transpose(ps[6][:, 128:216], crow[0:88, 0, :], ident[0:88, 0:88])
            pe.transpose(ps[6][:, 256:344], crow[0:88, 1, :], ident[0:88, 0:88]).then_inc(sem("vec_in_psum"), 1)

            def mean_square(src, nk, o, w=None):
                for k in range(nk):
                    q = pe.matmul(o, ones if w is None else w, src[:, k, :], start=k == 0, stop=k == nk - 1)
                return q

            pe.wait_ge(sem("x_squared"), 1)
            pe.wait_ge(sem("vec_turned"), 1)
            mean_square(sqT, KD, ps[6]).then_inc(sem("x_summed"), 1)

            def ada(g):
                pe.wait_ge(sem(f"w_landed{g % 2}"), landings[g])
                if raw_no[g] == 0:
                    pe.wait_ge(sem("cond_ready"), 1)
                for m in range(2):
                    c = 2 * raw_no[g] + m
                    for k in range(KD):
                        q = pe.matmul(ps[7][:, c:c + 1], wring[:, g % 2, 256 * k + P * m:256 * k + P * (m + 1)],
                                      cond[:, k:k + 1], start=k == 0, stop=k == KD - 1)
                q.then_inc(sem("ada_used"), 1)

            for g in range(G_ADA0, G_RW):
                ada(g)
            pe.wait_ge(sem("h_split"), 1)
            for g in range(G_RW, G_ADA1):
                project(g, PAIR, hhi, hlo)
            for g in range(G_ADA1, G_HG):
                ada(g)

            pe.wait_ge(sem("ld_lora"), 48)
            pe.wait_ge(sem("lora_in"), 2)
            for j in range(RW_TILES):
                if j >= 2:
                    pe.wait_ge(sem("lora_read"), 2 * (j - 1))
                pe.matmul(ps[2 + j % 2], LW[0:64, P * j:P * (j + 1)], LORA[0:64, :], start=True, stop=True
                          ).then_inc(sem("lora_out"), 1)
                pe.matmul(ps[4 + j % 2], LW[64:128, P * j:P * (j + 1)], LORA[64:128, :], start=True, stop=True
                          ).then_inc(sem("lora_out"), 1)
            for j in range(RW_TILES):
                pe.wait_ge(sem("kk_squared"), j + 1)
                if j == 0:
                    pe.wait_ge(sem("mod_read"), 1)
                if j >= 1:
                    pe.wait_ge(sem("kk_norm_read"), j)
                pe.matmul(ps[6], heads, outs[:, 8 + j, :], start=True, stop=True).then_inc(sem("kk_summed"), 1)

            for j in range(RW_TILES):
                pe.wait_ge(sem("rw_hats"), j + 1)
                if j == 0:
                    pe.wait_ge(sem("kk_norm_read"), RW_TILES)
                for i in range(8):
                    p, h = i // 2, i % 2
                    b = ps[2 + i % 4]
                    if i >= 4:
                        pe.wait_ge(sem("abr_copied"), 8 * j + i - 3)
                    rows = slice(64 * h, 64 * h + 64)
                    rhs = AR[rows, p, :, :].rearrange("p w t -> p (w t)")
                    pe.matmul(b[:, 0:256], BH[rows, P * p:P * (p + 1)], rhs, start=True, stop=True)
                    pe.matmul(b[:, 256:512], KH[rows, P * p:P * (p + 1)], rhs, start=True, stop=True
                              ).then_inc(sem("abr_done"), 1)
                pe.wait_ge(sem("rw_tildes"), j + 1)
                pe.wait_ge(sem("abr_copied"), 8 * j + 8)
                for n, src in enumerate((None, BH, KH, V[:, j, :])):
                    if n == 2:
                        pe.wait_ge(sem("tok_copied"), 4 * j + 1)
                    if n == 3:
                        pe.wait_ge(sem("tok_copied"), 4 * j + 2)
                    for p in range(PAIRS):
                        piece = AR[:, p, 0, :] if src is None else src[:, P * p:P * (p + 1)]
                        q = pe.transpose(ps[6 + n % 2][:, P * p:P * (p + 1)], piece, ident)
                    q.then_inc(sem("tok_turned"), 1)
                def turn(l):
                    for half in range(2):
                        pe.wait_ge(sem("t_added"), 2 * (6 * j + l) + half + 1)
                        for i in range(4):
                            q = pe.transpose(ps[2 + half][:, P * i:P * (i + 1)], (TT if l == 0 else TM)[:, 4 * half + i, :], ident)
                        q.then_inc(sem("t_turned"), 1)

                turn(0)
                for l, n in enumerate((2, 4, 8, 16, 32)):
                    for half in range(2):
                        pe.wait_ge(sem("t_copied"), 2 * (6 * j + l) + half + 1)
                        for i in range(4):
                            x = 4 * half + i
                            first = TM[:, x, :].rearrange("p (b w n) -> p b w n", w=2, n=n)[:, :, 0, :]
                            q = pe.matmul(ps[4 + half][:, 64 * i:64 * (i + 1)], ABR[:, x, 0:P], first, start=True, stop=True)
                        q.then_inc(sem("y_done"), 1)
                    for half in range(2):
                        pe.wait_ge(sem("y_masked"), 2 * (5 * j + l) + half + 1)
                        for i in range(4):
                            x = 4 * half + i
                            q = pe.matmul(ps[4 + half][:, 256 + 64 * i:256 + 64 * (i + 1)], TT[:, x, :], YH[:, 64 * x:64 * (x + 1)],
                                          start=True, stop=True)
                        q.then_inc(sem("ty_done"), 1)
                    turn(l + 1)
                pe.wait_ge(sem("tok_copied"), 4 * j + 4)
                for i in range(8):
                    p, h = i // 2, i % 2
                    q = pe.matmul(ps[6][:, 64 * i:64 * (i + 1)], ABR[:, i, 256:384], VTK[:, p, 64 * h:64 * (h + 1)],
                                  start=True, stop=True)
                q.then_inc(sem("akv_done"), 1)
                pe.wait_ge(sem("t_copied"), 2 * (6 * j + 6))
                pe.wait_ge(sem("akv_copied"), j + 1)
                for half in range(2):
                    for i in range(4):
                        x = 4 * half + i
                        q = pe.matmul(ps[2 + half][:, P * i:P * (i + 1)], TT[:, x, :], AV[:, x, :], start=True, stop=True)
                    q.then_inc(sem("wy_done"), 1)
                pe.wait_ge(sem("wy_copied"), 2 * j + 2)
                for h in range(2):
                    for p in range(PAIRS):
                        for c in range(2):
                            x, rows, b = 2 * p + h, slice(64 * c, 64 * c + 64), ps[4 + c]
                            hs = slice(64 * h, 64 * h + 64)
                            w, y2 = WY[rows, x, 0:64], WY[rows, x, 64:128]
                            pe.matmul(b[hs, 64 * p:64 * p + 64], w, KTOK[0][rows, p, hs], start=True, stop=True)
                            o = b[hs, 256 + 64 * p:320 + 64 * p]
                            pe.matmul(o, KTOK[0][rows, p, hs], y2, start=True, stop=False)
                            q = pe.matmul(o, KTOK[1][rows, p, hs], VTK[rows, p, hs], start=False, stop=True)
                q.then_inc(sem("mn_done"), 1)
                for p in range(PAIRS):
                    for h in range(2):
                        x = 2 * p + h
                        q = pe.matmul(ps[6][64 * h:64 * h + 64, P * p:P * (p + 1)], WY[:, x, 0:64], ABR[:, x, 128:256],
                                      start=True, stop=True)
                q.then_inc(sem("q_done"), 1)
                for c in range(1, CHUNKS - 1):
                    pe.wait_ge(sem("state_ready"), 8 * j + c + 1)
                    for h in range(2):
                        hs = slice(64 * h, 64 * h + 64)
                        q = pe.matmul(ps[2 + h][hs, 0:64], MT[hs, 64 * c:64 * c + 64], YH[hs, 64 * c:64 * c + 64],
                                      start=True, stop=True)
                    q.then_inc(sem("state_step"), 1)
                pe.wait_ge(sem("state_ready"), 8 * j + 8)
                pe.wait_ge(sem("q_ready"), j + 1)
                for p in range(PAIRS):
                    for h in range(2):
                        x, hs = 2 * p + h, slice(64 * h, 64 * h + 64)
                        b = ps[4 + h]
                        pe.matmul(b[hs, P * p:P * (p + 1)], WY[:, x, 64:128], ABR[:, x, 128:256], start=True, stop=False)
                        q = pe.matmul(b[hs, P * p:P * (p + 1)], VTK[:, p, hs], ABR[:, x, 384:512], start=False, stop=True)
                        for c in range(2):
                            o = b[hs, P * p + 64 * c:P * p + 64 * c + 64]
                            ch = 2 * p + c
                            q = pe.matmul(o, YH[hs, 64 * ch:64 * ch + 64], PINV[hs, 64 * ch:64 * ch + 64],
                                          start=False, stop=True, skip_group_check=True)
                q.then_inc(sem("y_out"), 1)
                pe.wait_ge(sem("y_in"), j + 1)
                pe.matmul(ps[2], heads, KH, start=True, stop=True).then_inc(sem("stat"), 1)
                pe.wait_ge(sem("rk_ready"), j + 1)
                pe.matmul(ps[6], heads, SCR, start=True, stop=True).then_inc(sem("bonus_sum"), 1)
                pe.matmul(ps[7], GW[:, P * j:P * (j + 1)], GL, start=True, stop=True).then_inc(sem("g_out"), 1)
                pe.wait_ge(sem("y_centred"), j + 1)
                pe.matmul(ps[3], heads, BH, start=True, stop=True).then_inc(sem("stat"), 1)

            for g in range(G_HG, G_ML):
                project(g, PAIR, hhi, hlo)
            for l, n in enumerate((0, 1, 2, 4, 8, 16, 32, 64)):
                pe.wait_ge(sem("hg_factors"), l + 1)
                if n == 0:
                    pe.wait_ge(sem("rw_out"), RW_TILES)
                    for h in range(HG):
                        for c in range(4):
                            t = slice(P * c, P * (c + 1))
                            q = pe.matmul(ps[2 + h][:, t], HK[:, h, t], HQ[:, h, t], start=True, stop=True)
                    q.then_inc(sem("hg_level"), 1)
                    continue
                b0 = 6 if l % 2 else 4
                if l == 2:
                    pe.wait_ge(sem("hg_masked"), 1)
                elif l > 2:
                    pe.wait_ge(sem("hg_masked"), l - 1)
                for h in range(HG):
                    for c in range(4):
                        i = 4 * h + c
                        q = pe.matmul(ps[b0 + i // 8][:, 64 * (i % 8):64 * (i % 8) + 64], KN[:, h, P * c:P * (c + 1)],
                                      QC[:, h, 64 * c:64 * (c + 1)], start=True, stop=True)
                q.then_inc(sem("hg_level"), 1)
            pe.wait_ge(sem("hg_tail"), 1)
            for n in range(8):
                src = (HV if n < 4 else HK)[:, n % 4, :]
                if n >= 2:
                    pe.wait_ge(sem("hg_tok_copied"), n - 1)
                for c in range(4):
                    q = pe.transpose(ps[2 + n % 2][:, P * c:P * (c + 1)], src[:, P * c:P * (c + 1)], ident)
                q.then_inc(sem("hg_tok_turned"), 1)
            pe.wait_ge(sem("hg_masked"), 8)
            pe.wait_ge(sem("hg_tok_copied"), 8)
            for h in range(HG):
                if h >= 2:
                    pe.wait_ge(sem("hg_state"), 3 * (h - 1))
                for c in range(3):
                    q = pe.matmul(ps[2 + h % 2][:, P * c:P * (c + 1)], HKT[:, h, c, :], HVT[:, h, c, :], start=True, stop=True)
                q.then_inc(sem("hg_added"), 1)
            for h in range(HG):
                pe.wait_ge(sem("hg_state"), 3 * (h + 1))
                for c in range(4):
                    o = ps[4 + h][:, P * c:P * (c + 1)]
                    q = pe.matmul(o, HVT[:, h, c, :], AT[:, h, c, :], start=True, stop=c == 0)
                    if c:
                        q = pe.matmul(o, HS[:, h, c, :], HQ[:, h, P * c:P * (c + 1)], start=False, stop=True)
                q.then_inc(sem("hg_o"), 1)
            for h in range(HG):
                pe.wait_ge(sem("hg_squared"), h + 1)
                if h >= 2:
                    pe.wait_ge(sem("hg_rooted"), h - 1)
                pe.matmul(ps[2 + h % 2], ones, HSCR[:, h, :], start=True, stop=True).then_inc(sem("hg_summed"), 1)

            project(G_ML, PAIR, hhi, hlo)
            project(G_ML + 1, [(0, P), (P, 192)], hhi, hlo)
            pe.wait_ge(sem("ml_squared"), 1)
            pe.wait_ge(sem("hg_rooted"), 4)
            mean_square(MSQ, 2, ps[2])
            pe.matmul(ps[3], ones, MSQ[:, 2, :], start=True, stop=True).then_inc(sem("ml_summed"), 1)
            pe.wait_ge(sem("ml_normed"), 1)
            pe.wait_ge(sem("ld_mla"), 7 * 16)
            pe.wait_ge(sem("hg_out"), 1)
            for j in range(4):
                if j >= 1:
                    pe.wait_ge(sem("qk_copied"), 4 * j)
                for k in range(2):
                    pe.matmul(ps[2], WUQ[:, k, P * j:P * (j + 1)],
                              CQ[:, k, :], start=k == 0, stop=k == 1)
                pe.matmul(ps[3], WUK[:, P * j:P * (j + 1)], CKV,
                          start=True, stop=True).then_inc(sem("qk_done"), 1)
            pe.wait_ge(sem("rope_weights"), 1)
            for j in range(2):
                if j:
                    pe.wait_ge(sem("rope_done"), 5)
                for w, b in ((WROPE, ps[4]), (WROT, ps[5])):
                    for k in range(2):
                        q = pe.matmul(b, w[:, k, P * j:P * (j + 1)], CQ[:, k, :], start=k == 0, stop=k == 1)
                q.then_inc(sem("qr_done"), 1)
            for t in range(4):
                if t >= 2:
                    pe.wait_ge(sem("vm_copied"), t - 1)
                pe.matmul(ps[6 + t % 2], CKV[:, P * t:P * (t + 1)], WUV, start=True, stop=True
                          ).then_inc(sem("vm_done"), 1)
            pe.wait_ge(sem("qk_copied"), 16)
            pe.wait_ge(sem("rope_done"), 9)
            pe.wait_ge(sem("vm_copied"), 4)
            def score(i):
                h, qb = i // 4, i % 4
                w = P * (qb + 1)
                if i >= 2:
                    pe.wait_ge(sem("prob"), i - 1)
                pe.matmul(ps[2 + i % 2][:, 0:w], QH[0:QK, h, P * qb:P * (qb + 1)], KHD[0:QK, h, 0:w],
                          start=True, stop=True).then_inc(sem("score"), 1)

            score(0)
            for i in range(4 * ML):
                h, qb = i // 4, i % 4
                if i + 1 < 4 * ML:
                    score(i + 1)
                pe.wait_ge(sem("prob_scaled"), i + 1)
                if i >= 2:
                    pe.wait_ge(sem("pt_copied"), i - 1)
                for kb in range(qb + 1):
                    q = pe.transpose(ps[4 + i % 2][:, P * kb:P * (kb + 1)], PRB[:, i % 2, P * kb:P * (kb + 1)], ident)
                q.then_inc(sem("prob_turned"), 1)
                if qb < 3:
                    continue
                pe.wait_ge(sem("pt_copied"), i + 1)
                if h >= 2:
                    pe.wait_ge(sem("oc_copied"), h - 1)
                b = ps[6 + h % 2][64 * (h % 2):64 * (h % 2) + 64, :]
                for kb in range(4):
                    q = pe.matmul(b[:, P * kb:T], VM[:, kb, 64 * h:64 * (h + 1)], PT[:, kb, P * kb:T],
                                  start=kb == 0, stop=kb == 3)
                q.then_inc(sem("oc_done"), 1)

            pe.wait_ge(sem("oc_copied"), ML)
            pe.wait_ge(sem("ld_x2"), 16)
            for d in range(KD):
                if d >= 4:
                    pe.wait_ge(sem("xt2_copied"), d - 3)
                for t in range(4):
                    q = pe.transpose(ps[2 + d % 4][:, P * t:P * (t + 1)], XTOK2[:, t, P * d:P * (d + 1)], ident)
                q.then_inc(sem("xt2_turned"), 1)
            for half in range(2):
                for b in range(3):
                    g = G_MIX + 9 * half + 3 * b
                    project(g, PAIR, hhi, hlo)
                    project(g + 1, PAIR, hhi, hlo)
                    pe.wait_ge(sem("o_split"), 3 * half + b + 1)
                    project(g + 2, [(P * m, P * (m + 1)) for m in range(4)], ohi, olo)
            pe.wait_ge(sem("y_split"), 1)
            for q_ in range(4):
                project(G_OUT + q_, PAIR, hhi, hlo)

            pe.wait_ge(sem("x1_squared"), 1)
            pe.wait_ge(sem("oc_copied"), ML)
            mean_square(SQ1, KD, ps[6]).then_inc(sem("x1_summed"), 1)
            pe.wait_ge(sem("h2_split"), 1)
            for j in range(NF):
                project(G_UP + j, PAIR, hhi, hlo)
            pe.wait_ge(sem("act_split"), NF)
            for q_ in range(4):
                o = [bank(), bank()]
                for part in range(3):
                    g = G_DOWN + 3 * q_ + part
                    pe.wait_ge(sem("w_lo"), split_no[g] + 1)
                    nk, ncols = groups[g][2], groups[g][3]
                    for m in range(2):
                        for k in range(nk):
                            kk = 8 * part + k
                            q = mm3(pe, o[m], g, k, P * m, P * (m + 1), acthi[:, kk, :], actlo[:, kk, :],
                                    kk == 0, kk == NF - 1, ncols)
                        if part == 2:
                            q.then_inc(sem("tile_ready"), 1)
                    if part < 2:
                        q.then_inc(sem("down_part"), 1)
            pe.wait_ge(sem("x2_squared"), 1)
            mean_square(SQF, KD, ps[6]).then_inc(sem("x2_summed"), 1)
            pe.wait_ge(sem("x2_normed"), 1)
            for t in range(4):
                for half in range(2):
                    i = 2 * t + half
                    if i >= 2:
                        pe.wait_ge(sem("rows_ready"), i - 1)
                    for d in range(4):
                        q = pe.transpose(ps[2 + i % 2][:, P * d:P * (d + 1)], SQF[:, 4 * half + d, P * t:P * (t + 1)], ident)
                    q.then_inc(sem("rows_turned"), 1)

        @block.scalar
        def _(act):
            chain = [0]

            def link(ins):
                chain[0] += 1
                ins.then_inc(sem("act_chain"), 1)
                act.wait_ge(sem("act_chain"), chain[0])

            split_order = list(split_no)
            staged = [0]

            def stage(upto):
                while staged[0] <= min(upto, len(split_order) - 1):
                    n, g = staged[0], split_order[staged[0]]
                    w = groups[g][2] * groups[g][3]
                    act.wait_ge(sem(f"w_landed{g % 2}"), landings[g])
                    if n >= 2:
                        act.wait_ge(*used[n - 2])
                        act.wait_ge(sem("w_lo"), n - 1)
                    act.activation(whi[:, g % 2, 0:w], wring[:, g % 2, 0:w], ACT.Copy).then_inc(sem("w_hi"), 1)
                    staged[0] += 1

            tile_no = [0]

            def tile():
                i = tile_no[0]
                tile_no[0] += 1
                act.wait_ge(sem("tile_ready"), i + 1)
                return ps[i % 2], sem(f"bank_free{i % 2}")

            act.wait_ge(sem("vec_in_psum"), 1)
            act.activation(vec[:], ps[6][:, 0:V_ROWS], ACT.Copy)
            act.activation(convv[:, 0, :], ps[6][:, 128:216], ACT.Copy)
            link(act.activation(convv[:, 1, :], ps[6][:, 256:344], ACT.Copy))
            act.activation(small[:, 32:40], col(V_C, 8), ACT.Sigmoid).then_inc(sem("vec_turned"), 1)
            act.wait_ge(sem("lb_zero"), 1)
            act.activation(small[:, 44:48], small[:, 40:44], ACT.Exp).then_inc(sem("lb_exp"), 1)
            act.wait_ge(sem("x_summed"), 1)
            act.activation(rstd, ps[6][:], ACT.Sqrt, bias=EPS, scale=1.0 / D).then_inc(sem("x_rooted"), 1)
            stage(1)
            for d in range(KD):
                act.wait_ge(sem("h_value"), d + 1)
                act.activation(hhi[:, d, :], sqT[:, d, :], ACT.Copy).then_inc(sem("h_hi"), 1)

            for n in range(7):
                stage(n + 1)
                if n == 0:
                    act.wait_ge(sem("rw_mixed"), 2)
                    act.activation(LORA[0:64, :], LORA[0:64, :], ACT.Tanh).then_inc(sem("lora_in"), 1)
                    act.activation(GL, GL, ACT.Sigmoid).then_inc(sem("lora_in"), 1)
                tile_no[0] += 2
            for j in range(RW_TILES):
                act.wait_ge(sem("lora_out"), 2 * j + 2)
                act.activation(DEC[:, j, :], ps[2 + j % 2][:], ACT.Sigmoid, bias=col(V_W0 + j)).then_inc(sem("lora_read"), 1)
                act.activation(AA[:, j, :], ps[4 + j % 2][:], ACT.Sigmoid, bias=col(V_A0 + j)).then_inc(sem("lora_read"), 1)
            act.wait_ge(sem("lora_read"), 8)
            act.activation(DEC, DEC, ACT.Exp, scale=-E_HALF).then_inc(sem("decay_ready"), 1)
            for j in range(RW_TILES):
                act.wait_ge(sem("kk_summed"), j + 1)
                act.activation(outs[:, 4 + j, :], ps[6][:], ACT.Sqrt).then_inc(sem("kk_norm_read"), 1)

            for j in range(RW_TILES):
                for n in range(4):
                    act.wait_ge(sem("tok_turned"), 4 * j + n + 1)
                    src = ps[6 + n % 2][:]
                    if n == 0:
                        dst, src = AV[:, :, 0:64], src.rearrange("p (i f) -> p i f", i=8)
                    else:
                        dst = (KTOK[0], KTOK[1], VTK)[n - 1]
                        src = src.rearrange("p (q f) -> p q f", q=PAIRS)
                    act.activation(dst, src, ACT.Copy).then_inc(sem("tok_copied"), 1)
                for l in range(6):
                    for half in range(2):
                        act.wait_ge(sem("t_turned"), 2 * (6 * j + l) + half + 1)
                        dst = (TM if l == 0 else TT)[:, 4 * half:4 * half + 4, :]
                        act.activation(dst, ps[2 + half][:].rearrange("p (i t) -> p i t", i=4), ACT.Copy
                                       ).then_inc(sem("t_copied"), 1)
                act.wait_ge(sem("akv_done"), j + 1)
                act.activation(AV[:, :, 64:128], ps[6][:].rearrange("p (i f) -> p i f", i=8), ACT.Copy
                               ).then_inc(sem("akv_copied"), 1)
                for half in range(2):
                    act.wait_ge(sem("wy_done"), 2 * j + half + 1)
                    act.activation(WY[:, 4 * half:4 * half + 4, :], ps[2 + half][:].rearrange("p (i t) -> p i t", i=4),
                                   ACT.Copy).then_inc(sem("wy_copied"), 1)
                act.wait_ge(sem("y_out"), j + 1)
                for h in range(2):
                    hs = slice(64 * h, 64 * h + 64)
                    q = act.activation(KH[hs, :], ps[4 + h][hs, :], ACT.Copy)
                q.then_inc(sem("y_in"), 1)
                act.wait_ge(sem("stat"), 2 * j + 2)
                act.activation(PP, ps[3][:], ACT.Sqrt, bias=REPS, scale=1.0 / CH).then_inc(sem("y_rooted"), 1)

            act.wait_ge(sem("rw_out"), RW_TILES)
            for n in range(8):
                stage(7 + n + 1)
                for m in range(2):
                    x = 2 * n + m
                    h = x % 4
                    bk, free = tile()
                    if x < 4:
                        act.activation(HQ[:, h, :], bk[:], ACT.Copy).then_inc(free, 1)
                    elif x < 8:
                        act.activation(HF[:, h, :], bk[:], ACT.Sigmoid).then_inc(sem("hg_f"), 1)
                        act.activation(HK[:, h, :], bk[:], ACT.Sigmoid, scale=-1.0).then_inc(free, 1)
                    elif x < 12:
                        act.activation(HV[:, h, :], bk[:], ACT.Copy).then_inc(free, 1)
                    else:
                        act.activation(HO[:, h, :], bk[:], ACT.Sigmoid).then_inc(sem("hg_og"), 1)
            for n in range(8):
                act.wait_ge(sem("hg_tok_turned"), n + 1)
                dst = (HVT if n < 4 else HKT)[:, n % 4, :, :]
                act.activation(dst, ps[2 + n % 2][:].rearrange("p (c t) -> p c t", c=4), ACT.Copy
                               ).then_inc(sem("hg_tok_copied"), 1)
            for h in range(HG):
                act.wait_ge(sem("hg_o"), h + 1)
                if h == 0:
                    act.wait_ge(sem("hg_masked"), 8)
                act.activation(HSCR[:, h, :], ps[4 + h][:], ACT.Square).then_inc(sem("hg_squared"), 1)
            for h in range(HG):
                act.wait_ge(sem("hg_summed"), h + 1)
                act.activation(HSCR[:, h, :], ps[2 + h % 2][:], ACT.Sqrt, bias=EPS, scale=1.0 / P
                               ).then_inc(sem("hg_rooted"), 1)

            stage(16)
            for k in range(3):
                bk, free = tile()
                if k == 2:
                    stage(17)
                if k == 0:
                    act.wait_ge(sem("hg_out"), 1)
                act.activation(CQ[:, k, :] if k < 2 else CKV, bk[:], ACT.Copy).then_inc(free, 1)
            bk, free = tile()
            act.activation(KR[0:32, :], bk[0:32, :], ACT.Copy)
            act.activation(KRR[0:32, :], bk[32:64, :], ACT.Copy).then_inc(free, 1)
            act.wait_ge(sem("bank_free0"), 17)
            act.wait_ge(sem("bank_free1"), 17)
            act.activation(MSQ[:, 0:2, :], CQ, ACT.Square)
            act.activation(MSQ[:, 2, :], CKV, ACT.Square).then_inc(sem("ml_squared"), 1)
            act.wait_ge(sem("ml_summed"), 1)
            act.activation(MRS[:, 0, :], ps[2][:], ACT.Sqrt, bias=EPS, scale=0.5 / P)
            act.activation(MRS[:, 1, :], ps[3][:], ACT.Sqrt, bias=EPS, scale=1.0 / P).then_inc(sem("ml_rooted"), 1)
            act.wait_ge(sem("angles"), 1)
            act.activation(SIN, SIN, ACT.Sin)
            act.activation(COS, COS, ACT.Sin).then_inc(sem("sines"), 1)
            for j in range(4):
                act.wait_ge(sem("qk_done"), j + 1)
                for i in range(2):
                    rows = slice(64 * i, 64 * i + 64)
                    act.activation(QH[0:64, 2 * j + i, :], ps[2][rows, :], ACT.Copy).then_inc(sem("qk_copied"), 1)
                    act.activation(KHD[0:64, 2 * j + i, :], ps[3][rows, :], ACT.Copy).then_inc(sem("qk_copied"), 1)
            for t in range(4):
                act.wait_ge(sem("vm_done"), t + 1)
                act.activation(VM[:, t, :], ps[6 + t % 2][:], ACT.Copy).then_inc(sem("vm_copied"), 1)

            def prob(i):
                w = P * (i % 4 + 1)
                act.wait_ge(sem("row_max"), i + 1)
                if i >= 2:
                    act.wait_ge(sem("prob_turned"), i - 1)
                act.activation(PRB[:, i % 2, 0:w], ps[2 + i % 2][:, 0:w], ACT.Exp, bias=small[:, 48 + i % 2:49 + i % 2],
                               scale=MLA_SCALE, accum_out=small[:, 50 + i % 2:51 + i % 2]).then_inc(sem("prob"), 1)

            prob(0)
            for i in range(4 * ML):
                h, qb = i // 4, i % 4
                if i + 1 < 4 * ML:
                    prob(i + 1)
                act.wait_ge(sem("prob_turned"), i + 1)
                if qb == 0 and h:
                    act.wait_ge(sem("oc_done"), h)
                act.activation(PT[:, 0:qb + 1, P * qb:P * (qb + 1)],
                               ps[4 + i % 2][:, 0:P * (qb + 1)].rearrange("p (k t) -> p k t", k=qb + 1), ACT.Copy
                               ).then_inc(sem("pt_copied"), 1)
            n = 17
            act.wait_ge(sem("oc_done"), ML)
            for half in range(2):
                for b in range(3):
                    for q_ in range(2):
                        stage(n + 1)
                        for m in range(2):
                            bk, free = tile()
                            k = 2 * (3 * half + b)
                            if k and q_ == 0 and m == 0:
                                act.wait_ge(sem("gates_used"), 3 * half + b)
                            act.activation(GATE[:, 2 * q_ + m, :], bk[:], ACT.Sigmoid).then_inc(free, 1)
                        n += 1
                    act.wait_ge(sem("o_value"), 1)
                    if 3 * half + b >= 1:
                        act.wait_ge(sem("tile_ready"), tile_no[0])
                    act.activation(ohi[:], outs[:, 4 * b:4 * b + 4, :], ACT.Copy).then_inc(sem("o_hi"), 1)
                    stage(n + 1)
                    tile_no[0] += 4
                    n += 1
            act.wait_ge(sem("y_value"), 1)
            act.wait_ge(sem("tile_ready"), tile_no[0])
            act.activation(hhi[:], YT, ACT.Copy).then_inc(sem("y_hi"), 1)
            for q_ in range(4):
                stage(n + 1)
                n += 1
                tile_no[0] += 2
                act.wait_ge(sem("x1_tile"), 2 * q_ + 2)
                for d in (2 * q_, 2 * q_ + 1):
                    q = act.activation(SQ1[:, d, :], X1[:, d, :], ACT.Square)
            q.then_inc(sem("x1_squared"), 1)
            act.wait_ge(sem("x1_summed"), 1)
            act.activation(tail[:, 0, :], ps[6][:], ACT.Sqrt, bias=EPS, scale=1.0 / D).then_inc(sem("x1_rooted"), 1)
            act.wait_ge(sem("h2_value"), 1)
            act.activation(hhi[:], SQ1, ACT.Copy).then_inc(sem("h2_hi"), 1)
            for j in range(NF):
                stage(n + 1)
                n += 1
                tile_no[0] += 2
                act.wait_ge(sem("conv_gate"), j + 1)
                act.activation(tail[:, 1, :], CG[:, j % 2, :], ACT.Sigmoid).then_inc(sem("gate_sig"), 1)
                act.wait_ge(sem("act_value"), j + 1)
                act.activation(acthi[:, j, :], CV[:, j % 2, :], ACT.Copy).then_inc(sem("act_hi"), 1)
            for q_ in range(4):
                for part in range(3):
                    stage(n + 1)
                    n += 1
            act.wait_ge(sem("x2_tile"), KD)
            act.activation(SQF, X1, ACT.Square).then_inc(sem("x2_squared"), 1)
            act.wait_ge(sem("x2_summed"), 1)
            act.activation(tail[:, 0, :], ps[6][:], ACT.Sqrt, bias=EPS, scale=1.0 / D).then_inc(sem("x2_rooted"), 1)

        @block.vector
        def _(dve):
            chain = [0]

            def link(ins):
                chain[0] += 1
                ins.then_inc(sem("dve_chain"), 1)
                dve.wait_ge(sem("dve_chain"), chain[0])

            tile_no = [0]

            def tile():
                i = tile_no[0]
                tile_no[0] += 1
                dve.wait_ge(sem("tile_ready"), i + 1)
                return ps[i % 2], sem(f"bank_free{i % 2}")

            mul, add, sub = ALU.mult, ALU.add, ALU.subtract
            dve.memset(small[:, 0:1], NORM_EPS)
            dve.memset(small[:, 1:2], RWKV_EPS)
            for d in range(KD):
                dve.wait_ge(sem("xt_turned"), d + 1)
                dve.tensor_copy(xT[:, d, :], ps[2 + d % 4][:]).then_inc(sem("xt_copied"), 1)
            dve.wait_ge(sem("xt_copied"), KD)
            dve.tensor_tensor(sqT, xT, xT, mul).then_inc(sem("x_squared"), 1)
            dve.wait_ge(sem("vec_turned"), 1)
            dve.tensor_tensor(cond[:], small[:, 32:40], col(V_C, 8), mul).then_inc(sem("cond_ready"), 1)
            dve.tensor_tensor(small[:, 40:44], col(V_LB, 4), col(V_LB, 4), sub).then_inc(sem("lb_zero"), 1)
            dve.wait_ge(sem("lb_exp"), 1)
            link(dve.reciprocal(small[:, 56:60], small[:, 44:48]))
            link(dve.tensor_tensor(small[:, 60:64], small[:, 56:60], small[:, 44:48], mul))
            link(dve.tensor_tensor(LBV, small[:, 60:64], small[:, 60:64], sub))
            link(dve.tensor_scalar(OMLB, LBV, -1.0, 1.0, mul, add))
            link(dve.tensor_scalar(ONE_MU, col(V_MU, 14), -1.0, 1.0, mul, add))
            link(dve.tensor_scalar(small[:, 12:16], col(V_KA, 4), -1.0, 1.0, mul, add))
            dve.wait_ge(sem("x_rooted"), 1)
            link(dve.reciprocal(rstd, rstd))
            dve.wait_ge(sem("ada_used"), 8)
            link(dve.tensor_tensor(mod[:, 0:16], ps[7][:, 0:16], vec[:, 0:16], add))
            link(dve.tensor_scalar(mod[:, 8:16], mod[:, 8:16], 1.0, None, add))
            for d in range(KD):
                link(dve.tensor_tensor(sqT[:, d, :], xT[:, d, :], rstd, mul))
                dve.tensor_scalar(sqT[:, d, :], sqT[:, d, :], mod[:, 8 + d:9 + d], mod[:, d:d + 1], mul, add
                                  ).then_inc(sem("h_value"), 1)
            for d in range(KD):
                dve.wait_ge(sem("h_hi"), d + 1)
                dve.wait_ge(sem("h_value"), d + 1)
                q = dve.tensor_tensor(hlo[:, d, :], sqT[:, d, :], hhi[:, d, :].bitcast(F32), sub)
            q.then_inc(sem("h_split"), 1)

            for x in (12, 13, 0, 1, 2, 3, 4, 5, 6, 7, 8, 9, 10, 11):
                bk, free = tile()
                dst = LORA if x == 12 else GL if x == 13 else (R, K, V)[x // 4][:, x % 4, :]
                if x == 12:
                    dve.wait_ge(sem("h_split"), 1)
                link(dve.tensor_scalar(dst, bk[:], ONE_MU[:, x:x + 1], None, mul))
                link(dve.scalar_tensor_tensor(dst[:, 1:T], bk[:, 0:T - 1], col(V_MU + x), dst[:, 1:T], mul, add))
                dve.sem_inc(free, 1)
                if x in (12, 13):
                    dve.sem_inc(sem("rw_mixed"), 1)
            dve.wait_ge(sem("ada_used"), 24)
            dve.tensor_tensor(mod[:, 16:48], ps[7][:, 16:48], vec[:, 16:48], add).then_inc(sem("mod_read"), 1)
            dve.wait_ge(sem("mod_read"), 1)
            link(dve.tensor_scalar(mod[:, 32:40], mod[:, 32:40], 1.0, None, add))
            for j in range(RW_TILES):
                link(dve.tensor_scalar(KK[:, j, :], K[:, j, :], col(V_KK + j), None, mul))
                dve.tensor_tensor(outs[:, 8 + j, :], KK[:, j, :], KK[:, j, :], mul).then_inc(sem("kk_squared"), 1)
            for j in range(RW_TILES):
                dve.wait_ge(sem("kk_norm_read"), j + 1)
                nrm = outs[:, 4 + j, :]
                link(dve.tensor_scalar(nrm, nrm, 1e-12, None, ALU.max))
                link(dve.reciprocal(nrm, nrm))
                link(dve.tensor_tensor(KK[:, j, :], KK[:, j, :], nrm, mul))
                dve.wait_ge(sem("lora_read"), 8)
                link(dve.tensor_scalar(nrm, AA[:, j, :], col(V_KA + j), small[:, 12 + j:13 + j], mul, add))
                link(dve.tensor_tensor(K[:, j, :], K[:, j, :], nrm, mul))
                link(dve.tensor_tensor(AA[:, j, :], AA[:, j, :], KK[:, j, :], mul))
                link(dve.tensor_scalar(KK[:, j, :], KK[:, j, :], -1.0, None, mul))

            def chunks(v):
                return v.rearrange("p (c t) -> p c t", c=CHUNKS)

            dve.wait_ge(sem("decay_ready"), 1)
            for j in range(RW_TILES):
                dec = chunks(DEC[:, j, :])
                link(dve.memset(SCR, 0.0))
                link(dve.tensor_copy(chunks(SCR)[:, :, 0:1], dec[:, :, 0:1]))
                link(dve.memset(dec[:, :, 0:1], 0.0))
                link(dve.tensor_tensor_scan(PP, DEC[:, j, :], SCR, 0.0, mul, add))
                link(dve.reciprocal(PINV, PP))
                rr = R[:, j, :].rearrange("p (q t) -> p q t", q=PAIRS)
                pp = PP.rearrange("p (q t) -> p q t", q=PAIRS)
                dve.tensor_tensor(AR[:, :, 1, :], rr, pp, mul)
                for c in range(2):
                    ar = AR[:, :, 0, 64 * c:64 * c + 64]
                    kk = KK[:, j, :].rearrange("p (q c t) -> p q c t", q=PAIRS, c=2)[:, :, c, :]
                    pc = PP.rearrange("p (q c t) -> p q c t", q=PAIRS, c=2)[:, :, c, :]
                    dve.tensor_tensor(ar[:, :, 1:64], kk[:, :, 1:64], pc[:, :, 0:63], mul)
                    dve.tensor_copy(ar[:, :, 0:1], kk[:, :, 0:1])
                dve.tensor_tensor(BH, AA[:, j, :], PINV, mul)
                dve.tensor_tensor(KH, K[:, j, :], PINV, mul).then_inc(sem("rw_hats"), 1)
                for i in range(8):
                    dve.wait_ge(sem("abr_done"), 8 * j + i + 1)
                    dve.tensor_tensor(ABR[:, i, :], ps[2 + i % 4][:], cst("rw_mask"), mul).then_inc(sem("abr_copied"), 1)
                last = chunks(PP)[:, :, 63:64].broadcast_to([P, CHUNKS, CH])
                dve.wait_ge(sem("rw_hats"), j + 1)
                dve.tensor_tensor(chunks(BH), chunks(BH), last, mul)
                dve.tensor_tensor(chunks(KH), chunks(KH), last, mul).then_inc(sem("rw_tildes"), 1)
                dve.wait_ge(sem("abr_copied"), 8 * j + 8)
                for half in range(2):
                    x = slice(4 * half, 4 * half + 4)
                    wide = [P, 4, P]
                    link(dve.tensor_tensor(TT[:, x, :], ABR[:, x, 0:P], cst("pair_t").unsqueeze(1).broadcast_to(wide), mul))
                    dve.tensor_tensor(TT[:, x, :], TT[:, x, :], ident.unsqueeze(1).broadcast_to(wide), add
                                      ).then_inc(sem("t_added"), 1)
                for l, n in enumerate((2, 4, 8, 16, 32)):
                    mask = cst("level")[:, 64 * l:64 * l + 64].unsqueeze(1).broadcast_to([P, 4, 64])
                    for half in range(2):
                        dve.wait_ge(sem("y_done"), 2 * (5 * j + l) + half + 1)
                        dve.tensor_tensor(YH[:, 256 * half:256 * half + 256].rearrange("p (i c) -> p i c", i=4),
                                          ps[4 + half][:, 0:256].rearrange("p (i c) -> p i c", i=4), mask, mul
                                          ).then_inc(sem("y_masked"), 1)
                    for half in range(2):
                        dve.wait_ge(sem("ty_done"), 2 * (5 * j + l) + half + 1)
                        dve.wait_ge(sem("t_copied"), 2 * (6 * j) + 2)
                        first = TM[:, 4 * half:4 * half + 4, :].rearrange("p i (b w n) -> p (i b) w n", w=2, n=n)[:, :, 0, :]
                        dve.tensor_tensor(first, first, ps[4 + half][:, 256:512].rearrange("p (b n) -> p b n", n=n), add
                                          ).then_inc(sem("t_added"), 1)
                dve.wait_ge(sem("mn_done"), j + 1)
                mt = MT.rearrange("p (q c f) -> p q c f", q=PAIRS, c=2)
                nn_ = NN.rearrange("p (q c f) -> p q c f", q=PAIRS, c=2)
                link(dve.tensor_tensor(chunks(MT), cst("eye64").unsqueeze(1).broadcast_to([P, CHUNKS, CH]), last, mul))
                for c in range(2):
                    b = ps[4 + c][:].rearrange("p (w q f) -> p w q f", w=2, q=PAIRS)
                    dve.tensor_tensor(mt[:, :, c, :], mt[:, :, c, :], b[:, 0, :, :], add)
                    link(dve.tensor_copy(nn_[:, :, c, :], b[:, 1, :, :]))
                dve.wait_ge(sem("q_done"), j + 1)
                dve.tensor_tensor(PINV.rearrange("p (q t) -> p q t", q=PAIRS), ps[6][:].rearrange("p (q t) -> p q t", q=PAIRS),
                                  AR[:, :, 1, :], add).then_inc(sem("q_ready"), 1)
                dve.memset(YH[:, 0:64], 0.0).then_inc(sem("state_ready"), 1)
                dve.tensor_copy(YH[:, 64:128], NN[:, 0:64]).then_inc(sem("state_ready"), 1)
                for c in range(1, CHUNKS - 1):
                    dve.wait_ge(sem("state_step"), 6 * j + c)
                    for h in range(2):
                        hs = slice(64 * h, 64 * h + 64)
                        q = dve.tensor_tensor(YH[hs, 64 * c + 64:64 * c + 128], ps[2 + h][hs, 0:64], NN[hs, 64 * c:64 * c + 64], add)
                    q.then_inc(sem("state_ready"), 1)
                dve.wait_ge(sem("y_out"), j + 1)
                link(dve.tensor_tensor(SCR, R[:, j, :], K[:, j, :], mul))
                dve.tensor_scalar(SCR, SCR, col(V_RK + j), None, mul).then_inc(sem("rk_ready"), 1)
                dve.wait_ge(sem("y_in"), j + 1)
                dve.wait_ge(sem("stat"), 2 * j + 1)
                link(dve.scalar_tensor_tensor(KH, ps[2][:], -1.0 / CH, KH, mul, add))
                dve.tensor_tensor(BH, KH, KH, mul).then_inc(sem("y_centred"), 1)
                dve.wait_ge(sem("bonus_sum"), j + 1)
                link(dve.tensor_tensor(outs[:, 11, :], ps[6][:], V[:, j, :], mul))
                dve.wait_ge(sem("y_rooted"), j + 1)
                link(dve.reciprocal(PP, PP))
                link(dve.tensor_tensor(KH, KH, PP, mul))
                link(dve.tensor_scalar(KH, KH, col(V_LNW + j), col(V_LNB + j), mul, add))
                link(dve.tensor_tensor(KH, KH, outs[:, 11, :], add))
                dve.wait_ge(sem("g_out"), j + 1)
                dve.tensor_tensor(outs[:, j, :], KH, ps[7][:], mul).then_inc(sem("rw_out"), 1)
                dve.wait_ge(sem("rw_out"), j + 1)

            tile_no[0] += 12
            for h in range(HG):
                bk, free = tile()
                dve.wait_ge(sem("hg_og"), h + 1)
                dve.tensor_tensor(HO[:, h, :], HO[:, h, :], bk[:], mul).then_inc(free, 1)
            for h in range(HG):
                link(dve.tensor_scalar(HF[:, h, :], HF[:, h, :], OMLB[:, h:h + 1], LBV[:, h:h + 1], mul, add))
                link(dve.tensor_scalar(HK[:, h, :], HK[:, h, :], OMLB[:, h:h + 1], None, mul))
            link(dve.tensor_scalar(HF, HF, 1e-30, None, ALU.max))
            dve.memset(KN, 0.0)
            dve.memset(SUF, 1.0).then_inc(sem("hg_factors"), 1)
            dve.wait_ge(sem("hg_factors"), 1)

            def halves(v, n):
                return v.rearrange("p h (b w n) -> p (h b) w n", w=2, n=n)

            def masked(l, n):
                b0 = 6 if l % 2 else 4
                dve.wait_ge(sem("hg_level"), l + 1)
                dve.wait_ge(sem("hg_masked"), l)
                for i in range(2):
                    mask = consti[:, l - 1, :].unsqueeze(1).broadcast_to([P, 8, 64]).rearrange("p i (b n) -> p i b n", n=n)
                    at = AT[:, 2 * i:2 * i + 2, :, :].rearrange("p h c (b w n) -> p (h c) b w n", w=2, n=n)[:, :, :, 1, :]
                    q = None
                    src = ps[b0 + i][:].rearrange("p (i b n) -> p i b n", i=8, n=n)
                    q = dve.copy_predicated(at, mask, src)
                q.then_inc(sem("hg_masked"), 1)

            for l, n in enumerate((1, 2, 4, 8, 16, 32, 64)):
                k_, q_, f_, s_ = halves(HK, n), halves(HQ, n), halves(HF, n), halves(SUF, n)
                kn = halves(KN, n)
                if l:
                    dve.wait_ge(sem("hg_level"), l + 1)
                qc = QC.rearrange("p h (b n) -> p (h b) n", n=n)
                dve.tensor_tensor(qc, q_[:, :, 1, :], f_[:, :, 1, :], mul)
                dve.tensor_tensor(kn[:, :, 0, :], k_[:, :, 0, :], s_[:, :, 0, :], mul).then_inc(sem("hg_factors"), 1)
                shape = [P, HG * T // (2 * n), n]
                link(dve.tensor_tensor(s_[:, :, 0, :], s_[:, :, 0, :], f_[:, :, 1, n - 1:n].broadcast_to(shape), mul))
                link(dve.tensor_tensor(f_[:, :, 1, :], f_[:, :, 1, :], f_[:, :, 0, n - 1:n].broadcast_to(shape), mul))
                if l == 0:
                    dve.wait_ge(sem("hg_level"), 1)
                    for h in range(HG):
                        q = dve.tensor_tensor(AT[:, h, :, :], ps[2 + h][:].rearrange("p (c t) -> p c t", c=4),
                                              ident.unsqueeze(1).broadcast_to([P, 4, P]), mul)
                    q.then_inc(sem("hg_masked"), 1)
                    dve.wait_ge(sem("hg_masked"), 1)
                else:
                    masked(l, n // 2)
            masked(7, 64)
            dve.tensor_tensor(HQ, HQ, HF, mul)
            dve.tensor_tensor(HK, HK, SUF, mul).then_inc(sem("hg_tail"), 1)
            for h in range(HG):
                dve.wait_ge(sem("hg_added"), h + 1)
                b = ps[2 + h % 2]
                dve.tensor_copy(HS[:, h, 1, :], b[:, 0:P]).then_inc(sem("hg_state"), 1)
                for c in (1, 2):
                    dve.wait_ge(sem("hg_state"), 3 * h + c)
                    dve.scalar_tensor_tensor(HS[:, h, c + 1, :], HS[:, h, c, :], HF[:, h, P * (c + 1) - 1:P * (c + 1)],
                                             b[:, P * c:P * (c + 1)], mul, add).then_inc(sem("hg_state"), 1)
            for h in range(HG):
                dve.wait_ge(sem("hg_rooted"), h + 1)
                sc = HSCR[:, h, :]
                link(dve.reciprocal(sc, sc))
                link(dve.tensor_tensor(sc, sc, HO[:, h, :], mul))
                q = dve.scalar_tensor_tensor(outs[:, 4 + h, :], ps[4 + h][:], col(V_HN), sc, mul, mul)
            q.then_inc(sem("hg_out"), 1)

            tile_no[0] += 4
            dve.wait_ge(sem("ml_rooted"), 1)
            link(dve.reciprocal(MRS, MRS))
            for k in range(2):
                dve.scalar_tensor_tensor(CQ[:, k, :], CQ[:, k, :], col(V_QN + k), MRS[:, 0, :], mul, mul)
            dve.scalar_tensor_tensor(CKV, CKV, col(V_KV), MRS[:, 1, :], mul, mul).then_inc(sem("ml_normed"), 1)
            dve.wait_ge(sem("ld_mla"), 7 * 16)
            for k in range(2):
                wr = WROPE[:, k, :].rearrange("p (h n) -> p h n", n=ROPE)
                wx = WROT[:, k, :].rearrange("p (h n) -> p h n", n=ROPE)
                dve.tensor_copy(wx[:, :, 0:16], wr[:, :, 16:32])
                q = dve.tensor_copy(wx[:, :, 16:32], wr[:, :, 0:16])
            q.then_inc(sem("rope_weights"), 1)
            magic, c1, c2 = 12582912.0, 6.28125, 0.0019350051879882812
            c3 = 2 * np.pi - c1 - c2
            link(dve.tensor_copy(RED, ANG.bitcast(I32)))
            link(dve.tensor_scalar(ANG, RED, cst("freq"), None, mul))
            for dst, quarter in ((SIN, 0.0), (COS, 0.25)):
                link(dve.tensor_scalar(RED, ANG, float(1 / (2 * np.pi)), quarter, mul, add))
                link(dve.tensor_scalar(RED, RED, magic, None, add))
                link(dve.tensor_scalar(RED, RED, magic, None, sub))
                link(dve.scalar_tensor_tensor(dst, RED, -c1, ANG, mul, add))
                link(dve.scalar_tensor_tensor(dst, RED, -c2, dst, mul, add))
                link(dve.scalar_tensor_tensor(dst, RED, -float(c3), dst, mul, add))
                if quarter:
                    link(dve.tensor_scalar(dst, dst, float(np.pi / 2), None, add))
                link(dve.tensor_scalar(dst, dst, 3.1415925, -3.1415925, ALU.min, ALU.max))
            dve.sem_inc(sem("angles"), 1)
            dve.wait_ge(sem("sines"), 1)
            link(dve.tensor_scalar(SIN, SIN, cst("rsign"), None, mul))
            q4 = slice(0, ROPE)
            link(dve.tensor_tensor(KR[q4, :], KR[q4, :], COS[q4, :], mul))
            link(dve.tensor_tensor(KRR[q4, :], KRR[q4, :], SIN[q4, :], mul))
            for h in range(ML):
                q = dve.tensor_tensor(KHD[NOPE:QK, h, :], KR[q4, :], KRR[q4, :], add)
            q.then_inc(sem("rope_done"), 1)
            for j in range(2):
                dve.wait_ge(sem("qr_done"), j + 1)
                link(dve.tensor_tensor(RT, ps[4][:], COS, mul))
                link(dve.tensor_tensor(RED, ps[5][:], SIN, mul))
                for i in range(4):
                    rows = slice(32 * i, 32 * i + 32)
                    q = dve.tensor_tensor(QH[NOPE:QK, 4 * j + i, :], RT[rows, :], RED[rows, :], add)
                    q.then_inc(sem("rope_done"), 1)
                dve.wait_ge(sem("rope_done"), 4 * j + 5)

            def row_max(i):
                w = P * (i % 4 + 1)
                b, s2 = ps[2 + i % 2], i % 2
                dve.wait_ge(sem("score"), i + 1)
                link(dve.tensor_tensor(b[:, w - P:w], b[:, w - P:w], cst("causal"), add))
                link(dve.reduce_max(small[:, 52 + s2:53 + s2], b[:, 0:w], AX.X))
                dve.tensor_scalar(small[:, 48 + s2:49 + s2], small[:, 52 + s2:53 + s2], -MLA_SCALE, None, mul
                                  ).then_inc(sem("row_max"), 1)

            row_max(0)
            for i in range(4 * ML):
                if i + 1 < 4 * ML:
                    row_max(i + 1)
                w, s2, h = P * (i % 4 + 1), i % 2, i // 4
                dve.wait_ge(sem("prob"), i + 1)
                link(dve.reciprocal(small[:, 54 + s2:55 + s2], small[:, 50 + s2:51 + s2]))
                dve.tensor_scalar(PRB[:, s2, 0:w], PRB[:, s2, 0:w], small[:, 54 + s2:55 + s2], None, mul
                                  ).then_inc(sem("prob_scaled"), 1)
                if i % 4 == 3:
                    dve.wait_ge(sem("oc_done"), h + 1)
                    rows = slice(64 * (h % 2), 64 * (h % 2) + 64)
                    dve.tensor_copy(outs[rows, 8 + h // 2, :], ps[6 + h % 2][rows, :]).then_inc(sem("oc_copied"), 1)
            dve.wait_ge(sem("oc_copied"), ML)
            dve.sem_inc(sem("o_value"), 1)

            for d in range(KD):
                dve.wait_ge(sem("xt2_turned"), d + 1)
                dve.tensor_copy(XT2[:, d, :], ps[2 + d % 4][:]).then_inc(sem("xt2_copied"), 1)
            for half in range(2):
                for b in range(3):
                    x = 3 * half + b + 1
                    dve.wait_ge(sem("o_hi"), x)
                    dve.tensor_tensor(olo[:], outs[:, 4 * b:4 * b + 4, :], ohi[:].bitcast(F32), sub).then_inc(sem("o_split"), 1)
                    tile_no[0] += 4
                    for m in range(4):
                        bk, free = tile()
                        y = YT[:, 4 * half + m, :]
                        if b == 0:
                            q = dve.tensor_tensor(y, GATE[:, m, :], bk[:], mul)
                            q.then_inc(free, 1)
                        else:
                            dve.tensor_tensor(TMP[:, m, :], GATE[:, m, :], bk[:], mul).then_inc(free, 1)
                    if b:
                        dve.wait_ge(sem("bank_free0"), FREE_AT(tile_no[0])[0])
                        dve.wait_ge(sem("bank_free1"), FREE_AT(tile_no[0])[1])
                        ys = YT[:, 4 * half:4 * half + 4, :]
                        q = dve.tensor_tensor(ys, ys, TMP, add)
                        link(q)
                        dve.sem_inc(sem("gates_used"), 1)
                    else:
                        dve.wait_ge(sem("bank_free0"), FREE_AT(tile_no[0])[0])
                        dve.wait_ge(sem("bank_free1"), FREE_AT(tile_no[0])[1])
                        dve.sem_inc(sem("gates_used"), 1)
            dve.sem_inc(sem("y_value"), 1)
            dve.wait_ge(sem("y_hi"), 1)
            dve.tensor_tensor(hlo[:], YT, hhi[:].bitcast(F32), sub).then_inc(sem("y_split"), 1)
            for d in range(KD):
                bk, free = tile()
                link(dve.scalar_tensor_tensor(X1[:, d, :], bk[:], mod[:, 16 + d:17 + d], XT2[:, d, :], mul, add))
                dve.sem_inc(free, 1)
                dve.sem_inc(sem("x1_tile"), 1)
            dve.wait_ge(sem("x1_rooted"), 1)
            link(dve.reciprocal(tail[:, 0, :], tail[:, 0, :]))
            for d in range(KD):
                link(dve.tensor_tensor(SQ1[:, d, :], X1[:, d, :], tail[:, 0, :], mul))
                link(dve.tensor_scalar(SQ1[:, d, :], SQ1[:, d, :], mod[:, 32 + d:33 + d], mod[:, 24 + d:25 + d], mul, add))
            dve.sem_inc(sem("h2_value"), 1)
            dve.wait_ge(sem("h2_hi"), 1)
            dve.tensor_tensor(hlo[:], SQ1, hhi[:].bitcast(F32), sub).then_inc(sem("h2_split"), 1)

            for j in range(NF):
                cur = None
                for f, buf in ((j, CV), (NF + j, CG)):
                    bk, free = tile()
                    o = buf[:, j % 2, :]
                    if j >= 2 and f == j:
                        dve.wait_ge(sem("act_hi"), j - 1)
                    link(dve.tensor_scalar(o, bk[:], convv[:, 1, f:f + 1], convv[:, 1, 44 + f:45 + f], mul, add))
                    link(dve.scalar_tensor_tensor(o[:, 1:T], bk[:, 0:T - 1], convv[:, 0, 44 + f:45 + f], o[:, 1:T], mul, add))
                    link(dve.scalar_tensor_tensor(o[:, 2:T], bk[:, 0:T - 2], convv[:, 0, f:f + 1], o[:, 2:T], mul, add))
                    dve.sem_inc(free, 1)
                dve.sem_inc(sem("conv_gate"), 1)
                dve.wait_ge(sem("gate_sig"), j + 1)
                cv, cg = CV[:, j % 2, :], CG[:, j % 2, :]
                link(dve.tensor_tensor(cg, cg, tail[:, 1, :], mul))
                link(dve.tensor_tensor(cv, cv, cg, mul))
                dve.sem_inc(sem("act_value"), 1)
                dve.wait_ge(sem("act_hi"), j + 1)
                dve.tensor_tensor(actlo[:, j, :], cv, acthi[:, j, :].bitcast(F32), sub).then_inc(sem("act_split"), 1)
            for d in range(KD):
                bk, free = tile()
                link(dve.scalar_tensor_tensor(X1[:, d, :], bk[:], mod[:, 40 + d:41 + d], X1[:, d, :], mul, add))
                dve.sem_inc(free, 1)
                dve.sem_inc(sem("x2_tile"), 1)
            dve.wait_ge(sem("x2_rooted"), 1)
            link(dve.reciprocal(tail[:, 0, :], tail[:, 0, :]))
            for d in range(KD):
                q = dve.scalar_tensor_tensor(SQF[:, d, :], X1[:, d, :], col(V_FIN + d), tail[:, 0, :], mul, mul)
            q.then_inc(sem("x2_normed"), 1)
            for t in range(4):
                for half in range(2):
                    i = 2 * t + half
                    dve.wait_ge(sem("rows_turned"), i + 1)
                    dve.tensor_copy(RESULT(t)[:, T * half:T * half + T], ps[2 + i % 2][:]).then_inc(sem("rows_ready"), 1)


_INS = ["x", "c", "positions", "ada_w", "ada_b", "w_in", "rwkv_mu", "rwkv_w0", "rwkv_w2", "rwkv_a0", "rwkv_a2", "rwkv_g2",
        "rwkv_k_k", "rwkv_k_a", "rwkv_r_k", "rwkv_ln_w", "rwkv_ln_b", "hgrn_lb", "hgrn_norm_w", "mla_q_norm_w", "mla_w_uq",
        "mla_kv_norm_w", "mla_w_ukv", "branch_proj_a", "branch_proj_b", "branch_proj_c", "w_out", "ffn_w_up",
        "ffn_conv_w", "ffn_conv_b", "ffn_w_down", "final_norm_w"]
_FLAT = {"c", "ada_b", "rwkv_mu", "rwkv_w0", "rwkv_a0", "rwkv_k_k", "rwkv_k_a", "rwkv_r_k", "rwkv_ln_w", "rwkv_ln_b",
         "hgrn_lb", "hgrn_norm_w", "mla_q_norm_w", "mla_kv_norm_w", "ffn_conv_w", "ffn_conv_b", "final_norm_w"}


def kernel(**inputs):
    import concourse.bacc as bacc
    from concourse.bass_utils import run_bass_kernel_spmd

    nc = bacc.Bacc("TRN2", target_bir_lowering=False, num_devices=1)
    arrays = {"const_f": CONST_F, "const_i": CONST_I.reshape(P, 7, CH).reshape(P, 7 * CH)}
    for name in _INS:
        v = np.ascontiguousarray(inputs[name])
        arrays[name] = v.reshape(-1) if name in _FLAT else v
    feed, aps = {}, {}
    for name, v in arrays.items():
        feed["in_" + name] = np.ascontiguousarray(v)
        aps[name] = nc.dram_tensor("in_" + name, v.shape, mybir.dt.from_np(v.dtype), kind="ExternalInput").ap()
    out = nc.dram_tensor("out_y", (1, T, D), F32, kind="ExternalOutput").ap()
    trunk(nc, aps, out)
    r = run_bass_kernel_spmd(nc, [feed], core_ids=[0])
    return r.results[0]["out_y"]
```

```python
from contextlib import ExitStack

import numpy as np

import concourse.bass as bass
from concourse import mybir

F32 = mybir.dt.float32
F32R = mybir.dt.float32r
I32 = mybir.dt.int32
ALU = mybir.AluOpType
ACT = mybir.ActivationFunctionType
AX = mybir.AxisListType

P = 128
T = 512
D = 1024
KD = D // P
FF = 2816
NF = FF // P
RW_TILES = 4
CH = 64
PAIRS = T // P
CHUNKS = T // CH
HG = 4
ML = 8
NOPE, ROPE = 64, 32
QK = NOPE + ROPE
MLA_SCALE = QK ** -0.5
NORM_EPS, RWKV_EPS = 1e-6, 64e-5
RW_COL, HG_COL, ML_COL, GATE_COL = 0, 1792, 3840, 4256
E_HALF = float(np.exp(-0.5))
GROUP = 2048

V_ADA, V_MU, V_W0, V_A0, V_KK, V_KA, V_RK, V_LNW, V_LNB = 0, 48, 62, 66, 70, 74, 78, 82, 86
V_LB, V_HN, V_QN, V_KV, V_FIN, V_C = 90, 94, 95, 97, 98, 106
V_ROWS = 114


def make_constants():
    s = np.arange(P)[:, None]
    t = np.arange(P)[None, :]
    same = (s // CH) == (t // CH)
    strict = (same & (s < t)).astype(np.float32)
    incl = (same & (s <= t)).astype(np.float32)
    c = {"ident": np.eye(P, dtype=np.float32), "rw_mask": np.concatenate([strict, incl, strict, incl], 1)}
    c["pair_t"] = ((s // 2 == t // 2) & (s < t)).astype(np.float32)
    levels = []
    for n in (2, 4, 8, 16, 32):
        first = [x for x in range(P) if (x // n) % 2 == 0]
        levels.append(np.array([[float((tt // (2 * n) == x // (2 * n)) and (tt // n) % 2 == 1) for x in first]
                                for tt in range(P)], np.float32))
    c["level"] = np.concatenate(levels, 1)
    c["ones"] = np.ones((P, P), np.float32)
    c["heads"] = ((s // CH) == (t // CH)).astype(np.float32)
    c["eye64"] = (s % CH == np.arange(CH)[None, :]).astype(np.float32)
    c["causal"] = np.where(t <= s, 0.0, -1e30).astype(np.float32)
    inv = (10000.0 ** (-np.arange(0, ROPE, 2, dtype=np.float32) / ROPE)).astype(np.float32)
    c["freq"] = np.tile(inv, P // 16)[:, None].astype(np.float32)
    c["rsign"] = np.where(np.arange(P) % ROPE < ROPE // 2, -1.0, 1.0)[:, None].astype(np.float32)
    hg = []
    for n in (1, 2, 4, 8, 16, 32, 64):
        second = [x for x in range(P) if (x // n) % 2 == 1]
        hg.append(np.array([[int((ss // (2 * n) == x // (2 * n)) and (ss // n) % 2 == 0) for x in second]
                            for ss in range(P)], np.int32))
    at, off = {}, 0
    for k, v in c.items():
        at[k] = (off, off + v.shape[1])
        off += v.shape[1]
    return np.concatenate(list(c.values()), 1), at, np.concatenate(hg, 1)


CONST_F, CONST_AT, CONST_I = make_constants()


def weight_groups(a):
    g = []
    kt = lambda w: w.rearrange("(k p) n -> p k n", p=P)
    ada, win = kt(a["ada_w"][0]), kt(a["w_in"][0])
    up, down = kt(a["ffn_w_up"][0]), kt(a["ffn_w_down"][0])
    for j in range(8):
        g.append(("raw", [(ada[:, :, 256 * j:256 * (j + 1)], 0, 256)], KD, 256))
    for c0 in (1536, 512, 768, 0, 256, 1024, 1280):
        g.append(("split", [(win[:, :, c0:c0 + 256], 0, 256)], KD, 256))
    def ada_group(j):
        g.append(("raw", [(ada[:, :, 256 * j:256 * (j + 1)], 0, 256)], KD, 256))

    def hgrn_group(u):
        h, c0 = u // 2, HG_COL + 2 * HG * P * (u % 2)
        g.append(("split", [(win[:, :, c0 + P * h:c0 + P * (h + 1)], 0, P),
                            (win[:, :, c0 + P * (HG + h):c0 + P * (HG + h + 1)], P, P)], KD, 256))

    for j in range(8, 24):
        if (j - 8) % 5 == 4:
            if j == 12:
                g.append(("split", [(win[:, :, ML_COL:ML_COL + 256], 0, 256)], KD, 256))
            else:
                hgrn_group((j - 8) // 5 - 1)
        ada_group(j)
    for u in range(2, 8):
        hgrn_group(u)
    c0 = ML_COL + 256
    g.append(("split", [(win[:, :, c0:c0 + 160], 0, 160), (win[:, :, c0 + 144:c0 + 160], 160, 16),
                        (win[:, :, c0 + 128:c0 + 144], 176, 16)], KD, 192))
    proj = [kt(a[f"branch_proj_{b}"][0]) for b in "abc"]
    for half, b in MIX_BLOCKS:
        for q in range(2):
            c0 = GATE_COL + b * D + half * 512 + q * 256
            g.append(("split", [(win[:, :, c0:c0 + 256], 0, 256)], KD, 256))
        g.append(("split", [(proj[b][:, :, 512 * half:512 * (half + 1)], 0, 512)], 4, 512))
    wo = kt(a["w_out"][0])
    for q in range(4):
        g.append(("split", [(wo[:, :, 256 * q:256 * (q + 1)], 0, 256)], KD, 256))
    for j in range(NF):
        g.append(("split", [(up[:, :, P * j:P * (j + 1)], 0, P), (up[:, :, FF + P * j:FF + P * (j + 1)], P, P)], KD, 256))
    for q in range(4):
        for k0 in (0, 8, 16):
            nk = min(8, NF - k0)
            g.append(("split", [(down[:, k0:k0 + nk, 256 * q:256 * (q + 1)], 0, 256)], nk, 256))
    return g


G_ADA0, G_RW, G_ADA1, G_KR, G_MIX, G_OUT, G_UP, G_DOWN = 0, 8, 15, 40, 41, 59, 63, 85
MIX_BLOCKS = [(0, 0), (0, 1), (1, 0), (1, 1), (0, 2), (1, 2)]
MIX_TILE = 34
G_FILL = [19, 25, 31, 34]
G_HG = [25, 31, 34, 35, 36, 37, 38, 39]


def trunk(nc, a, out):
    groups = weight_groups(a)
    ctx = ExitStack()
    with ctx:
        def sb(name, shape, dt=F32, c=ctx):
            return c.enter_context(nc.sbuf_tensor(name, shape, dt))

        sems = {}

        def sem(name):
            if name not in sems:
                sems[name] = ctx.enter_context(nc.semaphore(name))
            return sems[name]

        wring = sb("wring", [P, 2, GROUP])
        whi = sb("whi", [P, 2, GROUP], F32R)
        wlo = sb("wlo", [P, 2, GROUP], F32R)
        hhi = sb("hhi", [P, KD, T], F32R)
        hlo = sb("hlo", [P, KD, T], F32R)
        const = sb("const", [P, CONST_F.shape[1]])
        consti = sb("consti", [P, 7, CH], I32)
        vec = sb("vec", [P, V_ROWS])
        convv = sb("convv", [P, 2, 88])
        mod = sb("mod", [P, 48])
        cond = sb("cond", [P, KD])
        small = sb("small", [P, 64])
        outs = sb("outs", [P, 12, T])
        PAD = sb("padded", [P, 4, T])
        CQ = sb("cq", [P, 2, T])[:]
        scope = ExitStack()
        arena = sb("arena", [P, 46, T], c=scope)
        scope.close()
        scope = ExitStack()
        ohi = sb("ohi", [P, 4, T], F32R, c=scope)
        olo = sb("olo", [P, 4, T], F32R, c=scope)
        mix = sb("mix", [P, 38, T], c=scope)
        scope.close()
        scope = ExitStack()
        tail = sb("tail", [P, 2, T], c=scope)
        acthi = sb("acthi", [P, NF, T], F32R, c=scope)
        actlo = sb("actlo", [P, NF, T], F32R, c=scope)
        scope.close()
        scope = ExitStack()
        fin = sb("fin", [P, 12, T], c=scope)
        scope.close()
        SQF = fin[:, 2:10, :]
        ps = [ctx.enter_context(nc.psum_tensor(f"bank{b}", [P, T], F32))[:] for b in range(8)]

        def cst(name):
            lo, hi = CONST_AT[name]
            return const[:, lo:hi]

        ident = cst("ident")
        ones = cst("ones")
        heads = cst("heads")

        def col(row, n=1):
            return vec[:, row:row + n]

        EPS, REPS, ONE = small[:, 0:1], small[:, 1:2], small[:, 2:3]
        LBV, OMLB = small[:, 4:8], small[:, 8:12]
        NEG_W0 = small[:, 12:16]
        ONE_MU = small[:, 16:30]

        xtok = arena[:, 0:8, :].rearrange("p a t -> p (a t)").rearrange("p (a d) -> p a d", a=4)
        xT = arena[:, 8:16, :]
        sqT = arena[:, 16:24, :]
        rstd = arena[:, 24, :]
        vrows = arena[:, 25, 0:P]
        crow = arena[:, 26, 0:2 * P].rearrange("p (a b) -> p a b", a=2)
        R, K, V, DEC, AA, KK = (arena[:, 4 * i:4 * i + 4, :] for i in range(6))
        LORA = arena[:, 24, :]
        LW = arena[:, 25, :]
        GL = arena[:, 26, :]
        GW = arena[:, 27, :]
        ABR = arena[:, 28:36, :]
        TM = arena[:, 36:38, :].rearrange("p a t -> p (a t)").rearrange("p (i t) -> p i t", i=8)
        TT = arena[:, 38:40, :].rearrange("p a t -> p (a t)").rearrange("p (i t) -> p i t", i=8)
        YH = arena[:, 40, :]
        AV = arena[:, 41:43, :].rearrange("p a t -> p (a t)").rearrange("p (i t) -> p i t", i=8)
        WY = arena[:, 43:45, :].rearrange("p a t -> p (a t)").rearrange("p (i t) -> p i t", i=8)
        VTK = arena[:, 45, :].rearrange("p (q f) -> p q f", q=PAIRS)
        MT, NN = arena[:, 41, :], arena[:, 42, :]
        PP, PINV = outs[:, 4, :], outs[:, 5, :]
        AR = [v.rearrange("p a t -> p (a t)").rearrange("p (q w t) -> p q w t", q=PAIRS, w=2)
              for v in (outs[:, 6:8, :], arena[:, 24:26, :])]
        YV, YSQ, QT, BONUS = KK, AA, DEC, R
        LAST = small[:, 32:40]
        BH, KH, SCR = outs[:, 8, :], outs[:, 9, :], outs[:, 10, :]
        KTOK = [outs[:, i, :].rearrange("p (q f) -> p q f", q=PAIRS) for i in (10, 11)]
        HQ, HF, HK, HV, HO, SUF = (arena[:, 4 * i:4 * i + 4, :] for i in range(6))
        QC = arena[:, 24:26, :].rearrange("p a t -> p (a t)").rearrange("p (h t) -> p h t", h=HG)
        KN = arena[:, 26:30, :]
        AT = arena[:, 30:34, :].rearrange("p h (c t) -> p h c t", c=4)
        HVT = arena[:, 34:38, :].rearrange("p h (c t) -> p h c t", c=4)
        HKT = arena[:, 38:42, :].rearrange("p h (c t) -> p h c t", c=4)
        HS = arena[:, 42:46, :].rearrange("p h (c t) -> p h c t", c=4)
        HSCR = outs[:, 8:12, :]
        CKV, KR = arena[:, 2, :], arena[:, 3, :]
        MSQ, MRS = arena[:, 4:7, :], arena[:, 7:9, :]
        WUQ = arena[:, 9:11, :]
        WUK, WUV = arena[:, 11, :], arena[:, 12, :]
        COS, SIN, ANG, RED = (arena[:, i, :] for i in (13, 14, 15, 16))
        WROT = arena[:, 17, :].rearrange("p (k n) -> p k n", k=2)
        RT = arena[:, 18, :]
        WROPE = outs[:, 8, :].rearrange("p (k n) -> p k n", k=2)
        KRR = outs[:, 9, :]
        QH, KHD, VM = arena[:, 20:28, :], arena[:, 28:36, :], arena[:, 36:40, :]
        PRB, PT = arena[:, 40:42, :], arena[:, 42:46, :]
        GATE = mix[:, 0:4, :]
        YT = mix[:, 4:12, :]
        XT2 = mix[:, 20:28, :]
        TMP = PAD
        XTOK2 = mix[:, 12:20, :].rearrange("p a t -> p (a t)").rearrange("p (a d) -> p a d", a=4)
        X1 = outs[:, 0:8, :]
        SQ1 = mix[:, 28:36, :]
        CV = outs[:, 8:10, :]
        CG = outs[:, 10:12, :]

        def mm3(e, o, g, k, m0, m1, rhi, rlo, first, last, ncols):
            hi = whi[:, g % 2, :][:, k * ncols + m0:k * ncols + m1]
            lo = wlo[:, g % 2, :][:, k * ncols + m0:k * ncols + m1]
            e.matmul(o, hi, rhi, start=first, stop=False)
            e.matmul(o, hi, rlo, start=False, stop=False)
            return e.matmul(o, lo, rhi, start=False, stop=last)

        split_no, raw_no = {}, {}
        for i, gr in enumerate(groups):
            n = split_no if gr[0] == "split" else raw_no
            n[i] = len(n)

        EARLY = [v.rearrange("p a t -> p (a t)") for v in
                 [outs[:, 4 * i:4 * i + 4, :] for i in range(3)] + [arena[:, 28 + 4 * i:32 + 4 * i, :] for i in range(4)]]
        def ada_slot(g):
            return EARLY[g] if g < len(EARLY) else wring[:, g % 2, :]

        def ada_landed(g):
            return (sem(f"ada_in{g}"), 16) if g < len(EARLY) else (sem(f"w_landed{g % 2}"), landings[g])

        POOL_ADA = [g for g in raw_no if g in (1, 4) or g >= G_ADA1]
        DVE_ADA = [g for g in raw_no if g not in POOL_ADA]
        landings = {}
        count = [0, 0]
        for g, gr in enumerate(groups):
            count[g % 2] += 16 * len(gr[1]) * (g >= len(EARLY))
            landings[g] = count[g % 2]

        def RESULT(q):
            return wring[:, q // 2, (q % 2) * D:(q % 2 + 1) * D]

        def FREE_AT(n):
            return (n + 1) // 2, n // 2

        used, tiles = [], 0
        for g in split_no:
            if g < G_DOWN:
                tiles += 4 if G_MIX <= g < G_OUT and (g - G_MIX) % 3 == 2 else 2
                used.append((sem("tile_ready"), tiles))
            elif (g - G_DOWN) % 3 < 2:
                used.append((sem("down_part"), 2 * ((g - G_DOWN) // 3) + (g - G_DOWN) % 3 + 1))
            else:
                tiles += 2
                used.append((sem("tile_ready"), tiles))

        before, last_in = {}, {}
        for g, n in split_no.items():
            before[n] = last_in.get(g % 2)
            last_in[g % 2] = n

        block = ctx.enter_context(nc.Block())

        @block.sync
        def _(sp):
            rows = [("ada_b", V_ADA, 48), ("rwkv_mu", V_MU, 14), ("rwkv_w0", V_W0, 4), ("rwkv_a0", V_A0, 4),
                    ("rwkv_k_k", V_KK, 4), ("rwkv_k_a", V_KA, 4), ("rwkv_r_k", V_RK, 4), ("rwkv_ln_w", V_LNW, 4),
                    ("rwkv_ln_b", V_LNB, 4), ("hgrn_lb", V_LB, 4), ("hgrn_norm_w", V_HN, 1),
                    ("mla_q_norm_w", V_QN, 2), ("mla_kv_norm_w", V_KV, 1), ("final_norm_w", V_FIN, 8), ("c", V_C, 8)]
            for name, r0, n in rows:
                sp.dma_start(vrows[r0:r0 + n, :], a[name].rearrange("(r p) -> r p", p=P)).then_inc(sem("ld_vec"), 16)
            cw = a["ffn_conv_w"].rearrange("(r p) -> r p", p=P)
            sp.dma_start(crow[0:88, 0, :], cw[0:88, :]).then_inc(sem("ld_vec"), 16)
            sp.dma_start(crow[0:44, 1, :], cw[88:132, :]).then_inc(sem("ld_vec"), 16)
            sp.dma_start(crow[44:88, 1, :], a["ffn_conv_b"].rearrange("(r p) -> r p", p=P)).then_inc(sem("ld_vec"), 16)
            sp.dma_start(consti[:].rearrange("p a b -> p (a b)"), a["const_i"]).then_inc(sem("ld_const"), 16)

            def load(g):
                kind, parts, nk, n = groups[g]
                if g < len(EARLY):
                    sp.dma_start(EARLY[g].rearrange("p (k n) -> p k n", k=nk), parts[0][0]).then_inc(sem(f"ada_in{g}"), 16)
                    return
                if g - 2 < len(EARLY):
                    pass
                elif g - 2 in split_no:
                    sp.wait_ge(sem("w_lo"), split_no[g - 2] + 1)
                else:
                    sp.wait_ge(sem("ada_used"), raw_no[g - 2] + 1)
                dst = wring[:, g % 2, 0:nk * n].rearrange("p (k n) -> p k n", k=nk)
                for src, off, w in parts:
                    sp.dma_start(dst[:, :, off:off + w], src).then_inc(sem(f"w_landed{g % 2}"), 16)

            for g in range(len(groups)):
                load(g)
                if g == G_RW + 1:
                    sp.wait_ge(sem("vec_turned"), 1)
                    sp.wait_ge(sem("h_split"), 1)
                    sp.dma_start(LW[0:64, :], a["rwkv_w2"][0]).then_inc(sem("ld_lora"), 16)
                    sp.dma_start(LW[64:128, :], a["rwkv_a2"][0]).then_inc(sem("ld_lora"), 16)
                    sp.dma_start(GW, a["rwkv_g2"][0]).then_inc(sem("ld_lora"), 16)
                if g == G_KR:
                    sp.wait_ge(sem("hg_out"), 1)
                    uq = a["mla_w_uq"][0].rearrange("(k p) (h n) -> p k h n", p=P, n=QK)
                    ukv = a["mla_w_ukv"][0].rearrange("p (h n) -> p h n", n=P)
                    by_head = lambda v, n: v.rearrange("p (h n) -> p h n", n=n)
                    for k in range(2):
                        sp.dma_start(by_head(WUQ[:, k, :], NOPE), uq[:, k, :, 0:NOPE]).then_inc(sem("ld_mla"), 16)
                        sp.dma_start(by_head(WROPE[:, k, :], ROPE), uq[:, k, :, NOPE:QK]).then_inc(sem("ld_mla"), 16)
                    sp.dma_start(by_head(WUK, NOPE), ukv[:, :, 0:NOPE]).then_inc(sem("ld_mla"), 16)
                    sp.dma_start(by_head(WUV, NOPE), ukv[:, :, NOPE:P]).then_inc(sem("ld_mla"), 16)
                    sp.dma_start(ANG.bitcast(I32), a["positions"][0].partition_broadcast(P)).then_inc(sem("ld_mla"), 16)
                if g == G_MIX + 13:
                    sp.wait_ge(sem("oc_done"), ML)
                    sp.dma_start(XTOK2, a["x"][0].rearrange("(a p) d -> p a d", p=P)).then_inc(sem("ld_x2"), 16)
            for q in range(4):
                sp.wait_ge(sem("rows_ready"), 2 * (q + 1))
                sp.dma_start(out[0, q * P:(q + 1) * P, :], RESULT(q)).then_inc(sem("stored"), 16)
            sp.wait_ge(sem("stored"), 64)

        @block.gpsimd
        def _(pool):
            pool_step = [0]

            def pool_link(ins):
                pool_step[0] += 1
                ins.then_inc(sem("pool_chain"), 1)
                pool.wait_ge(sem("pool_chain"), pool_step[0])

            def weigh(g):
                w = ada_slot(g)
                pool.wait_ge(*ada_landed(g))
                if g == POOL_ADA[0]:
                    pool.wait_ge(sem("cond_ready"), 1)
                by_k = w.rearrange("p (k n) -> p k n", k=KD)
                pool_link(pool.tensor_tensor(by_k, by_k, cond[:].unsqueeze(2).broadcast_to([P, KD, 256]), ALU.mult))
                for half in (1024, 512, 256):
                    pool_link(pool.tensor_tensor(w[:, 0:half], w[:, 0:half], w[:, half:2 * half], ALU.add))
                pool.sem_inc(sem("ada_pool"), 1)

            pool.memset(PAD[:], 0.0).then_inc(sem("pad_zero"), 1)
            for g in range(len(groups)):
                if g in POOL_ADA:
                    weigh(g)
                if g not in split_no:
                    continue
                n = split_no[g]
                w = groups[g][2] * groups[g][3]
                s = g % 2
                pool.wait_ge(sem("w_hi"), n + 1)
                if before[n] is not None:
                    pool.wait_ge(*used[before[n]])
                pool.tensor_tensor(wlo[:, s, 0:w], wring[:, s, 0:w], whi[:, s, 0:w].bitcast(F32),
                                   ALU.subtract).then_inc(sem("w_lo"), 1)

        @block.tensor
        def _(pe):
            tile_no = [0]

            def bank():
                i = tile_no[0]
                tile_no[0] += 1
                if i >= 2:
                    pe.wait_ge(sem(f"bank_free{i % 2}"), i // 2)
                return ps[i % 2]

            def project(g, cuts, rhi, rlo):
                n = split_no[g]
                pe.wait_ge(sem("w_lo"), n + 1)
                nk, ncols = groups[g][2], groups[g][3]
                for m0, m1 in cuts:
                    o = bank()[0:m1 - m0, :]
                    for k in range(nk):
                        q = mm3(pe, o, g, k, m0, m1, rhi[:, k, :], rlo[:, k, :], k == 0, k == nk - 1, ncols)
                    q.then_inc(sem("tile_ready"), 1)

            PAIR = [(0, P), (P, 2 * P)]

            def fill(j, x0, x1):
                g = G_FILL[j]
                for x in range(x0, x1):
                    m, k = x // KD, x % KD
                    if x == 0:
                        pe.wait_ge(sem("w_lo"), split_no[g] + 1)
                        pe.wait_ge(sem("rw_out"), j)
                    if x == KD:
                        pe.wait_ge(sem("mod_read"), j + 1)
                    if k == 0:
                        fill_bank[0] = bank()
                    q = mm3(pe, fill_bank[0], g, k, P * m, P * (m + 1), hhi[:, k, :], hlo[:, k, :], k == 0, k == KD - 1, 256)
                    if k == KD - 1:
                        q.then_inc(sem("tile_ready"), 1)

            fill_bank = [None]

            pe.wait_ge(sem("ld_const"), 32)
            pe.wait_ge(sem("ld_x"), 16)
            for d in range(KD):
                if d >= 4:
                    pe.wait_ge(sem("xt_copied"), d - 3)
                for t in range(4):
                    q = pe.transpose(ps[2 + d % 4][:, P * t:P * (t + 1)], xtok[:, t, P * d:P * (d + 1)], ident)
                q.then_inc(sem("xt_turned"), 1)
            pe.wait_ge(sem("ld_vec"), 18 * 16)
            pe.transpose(ps[6][:, 0:V_ROWS], vrows[0:V_ROWS, :], ident[0:V_ROWS, 0:V_ROWS])
            pe.transpose(ps[6][:, 128:216], crow[0:88, 0, :], ident[0:88, 0:88])
            pe.transpose(ps[6][:, 256:344], crow[0:88, 1, :], ident[0:88, 0:88]).then_inc(sem("vec_in_psum"), 1)

            def mean_square(src, nk, o, w=None):
                for k in range(nk):
                    q = pe.matmul(o, ones if w is None else w, src[:, k, :], start=k == 0, stop=k == nk - 1)
                return q

            pe.wait_ge(sem("x_squared"), 1)
            pe.wait_ge(sem("vec_turned"), 1)
            mean_square(sqT, KD, ps[6]).then_inc(sem("x_summed"), 1)

            def ada(g, o):
                if g in POOL_ADA:
                    pe.wait_ge(sem("ada_pool"), POOL_ADA.index(g) + 1)
                else:
                    pe.wait_ge(sem("ada_dve"), DVE_ADA.index(g) + 1)
                for m in range(2):
                    c = 2 * raw_no[g] + m
                    q = pe.matmul(o[:, c:c + 1], ada_slot(g)[:, P * m:P * (m + 1)], ones[:, 0:1], start=True, stop=True)
                q.then_inc(sem("ada_used"), 1)

            for g in range(G_ADA0, G_RW):
                ada(g, ps[7])
            pe.wait_ge(sem("h_split"), 1)
            for g in range(G_RW, G_RW + 3):
                project(g, PAIR, hhi, hlo)

            pe.wait_ge(sem("ld_lora"), 48)
            pe.wait_ge(sem("lora_in"), 2)
            for j in range(RW_TILES):
                if j >= 2:
                    pe.wait_ge(sem("lora_read"), 2 * (j - 1))
                pe.matmul(ps[2 + j % 2], LW[0:64, P * j:P * (j + 1)], LORA[0:64, :], start=True, stop=True
                          ).then_inc(sem("lora_out"), 1)
                pe.matmul(ps[4 + j % 2], LW[64:128, P * j:P * (j + 1)], LORA[64:128, :], start=True, stop=True
                          ).then_inc(sem("lora_out"), 1)
            project(G_RW + 3, PAIR, hhi, hlo)
            for j in range(RW_TILES):
                pe.wait_ge(sem("kk_squared"), j + 1)
                if j >= 2:
                    pe.wait_ge(sem("kk_norm_read"), j - 1)
                pe.matmul(ps[6 + j % 2], heads, outs[:, j, :], start=True, stop=True).then_inc(sem("kk_summed"), 1)
            for g in range(G_RW + 4, G_RW + 7):
                project(g, PAIR, hhi, hlo)

            ada_next = iter([g for g in raw_no if g >= G_ADA1])

            def fold_ada(j, i):
                if 5 * j + i >= 16:
                    return
                if i == 0 and j == 0:
                    pe.wait_ge(sem("rw_mixed"), 14)
                if i == 4:
                    pe.wait_ge(sem("bank_free1"), FREE_AT(16 + 2 * j)[1])
                ada(next(ada_next), ps[1])

            def head_mean(j, bank_):
                pe.wait_ge(sem("y_in"), j + 1)
                if j < 3:
                    pe.wait_ge(sem("bank_free0"), FREE_AT(16 + 2 * j)[0])
                pe.matmul(bank_, heads, YV[:, j, :], start=True, stop=True).then_inc(sem("stat"), 1)

            def bonus_sum(j):
                pe.wait_ge(sem("rk_ready"), j + 1)
                pe.matmul(ps[6], heads, BONUS[:, j, :], start=True, stop=True).then_inc(sem("bonus_sum"), 1)

            def head_variance(j, bank_):
                pe.wait_ge(sem("y_centred"), j + 1)
                pe.matmul(bank_, heads, YSQ[:, j, :], start=True, stop=True).then_inc(sem("stat"), 1)

            def output_gate(j, bank_):
                pe.wait_ge(sem("y_rooted"), j + 1)
                pe.matmul(bank_, GW[:, P * j:P * (j + 1)], GL, start=True, stop=True).then_inc(sem("g_out"), 1)

            for j in range(RW_TILES):
                ar = AR[j % 2]
                pe.wait_ge(sem("rw_hats"), j + 1)
                if j == 0:
                    pe.wait_ge(sem("kk_norm_read"), RW_TILES)
                for i in range(8):
                    p, h = i // 2, i % 2
                    b = ps[2 + i % 4]
                    if i >= 4:
                        pe.wait_ge(sem("abr_copied"), 8 * j + i - 3)
                    if j and i == 2:
                        head_mean(j - 1, ps[0])
                    if j and i == 3:
                        bonus_sum(j - 1)
                    if j and i == 6:
                        head_variance(j - 1, ps[0])
                    if i == 4:
                        fold_ada(j, 0)
                    rhs = ar[:, p, :, :].rearrange("p w t -> p (w t)")
                    pe.matmul(b[:, 0:256], PAD[:, h, P * p:P * (p + 1)], rhs, start=True, stop=True)
                    pe.matmul(b[:, 256:512], PAD[:, 2 + h, P * p:P * (p + 1)], rhs, start=True, stop=True
                              ).then_inc(sem("abr_done"), 1)
                def token_major(n, src):
                    if n == 0 and j:
                        pe.wait_ge(sem("bonus_ready"), j)
                    if n >= 2:
                        pe.wait_ge(sem("rw_tildes"), j + 1)
                        pe.wait_ge(sem("tok_copied"), 4 * j + n - 1)
                    for p in range(PAIRS):
                        piece = ar[:, p, 0, :] if src is None else src[:, P * p:P * (p + 1)]
                        q = pe.transpose(ps[6 + n % 2][:, P * p:P * (p + 1)], piece, ident)
                    q.then_inc(sem("tok_turned"), 1)

                token_major(0, None)
                token_major(1, V[:, j, :])
                if j:
                    output_gate(j - 1, ps[0])
                fold_ada(j, 1)

                def turn(l):
                    for half in range(2):
                        pe.wait_ge(sem("t_added"), 2 * (6 * j + l) + half + 1)
                        for i in range(4):
                            q = pe.transpose(ps[2 + half][:, P * i:P * (i + 1)], (TT if l == 0 else TM)[:, 4 * half + i, :], ident)
                        q.then_inc(sem("t_turned"), 1)

                turn(0)
                for l, n in enumerate((2, 4, 8, 16, 32)):
                    if l in (1, 2):
                        fold_ada(j, l + 1)
                    for half in range(2):
                        pe.wait_ge(sem("t_copied"), 2 * (6 * j + l) + half + 1)
                        for i in range(4):
                            x = 4 * half + i
                            first = TM[:, x, :].rearrange("p (b w n) -> p b w n", w=2, n=n)[:, :, 0, :]
                            q = pe.matmul(ps[4 + half][:, 64 * i:64 * (i + 1)], ABR[:, x, 0:P], first, start=True, stop=True)
                        q.then_inc(sem("y_done"), 1)
                    for half in range(2):
                        pe.wait_ge(sem("y_masked"), 2 * (5 * j + l) + half + 1)
                        for i in range(4):
                            x = 4 * half + i
                            q = pe.matmul(ps[4 + half][:, 256 + 64 * i:256 + 64 * (i + 1)], TT[:, x, :], YH[:, 64 * x:64 * (x + 1)],
                                          start=True, stop=True)
                        q.then_inc(sem("ty_done"), 1)
                    turn(l + 1)
                    if l == 1:
                        token_major(2, BH)
                        token_major(3, KH)
                pe.wait_ge(sem("tok_copied"), 4 * j + 3)
                for i in range(8):
                    p, h = i // 2, i % 2
                    q = pe.matmul(ps[6][:, 64 * i:64 * (i + 1)], ABR[:, i, 256:384], VTK[:, p, 64 * h:64 * (h + 1)],
                                  start=True, stop=True)
                q.then_inc(sem("akv_done"), 1)
                pe.wait_ge(sem("t_copied"), 2 * (6 * j + 6))
                pe.wait_ge(sem("akv_copied"), j + 1)
                for half in range(2):
                    for i in range(4):
                        x = 4 * half + i
                        q = pe.matmul(ps[2 + half][:, P * i:P * (i + 1)], TT[:, x, :], AV[:, x, :], start=True, stop=True)
                    q.then_inc(sem("wy_done"), 1)
                pe.wait_ge(sem("tok_copied"), 4 * j + 4)
                pe.wait_ge(sem("wy_copied"), 2 * j + 2)
                for h in range(2):
                    for p in range(PAIRS):
                        for c in range(2):
                            x, rows, b = 2 * p + h, slice(64 * c, 64 * c + 64), ps[4 + c]
                            hs = slice(64 * h, 64 * h + 64)
                            w, y2 = WY[rows, x, 0:64], WY[rows, x, 64:128]
                            pe.matmul(b[hs, 64 * p:64 * p + 64], w, KTOK[0][rows, p, hs], start=True, stop=True)
                            o = b[hs, 256 + 64 * p:320 + 64 * p]
                            pe.matmul(o, KTOK[0][rows, p, hs], y2, start=True, stop=False)
                            q = pe.matmul(o, KTOK[1][rows, p, hs], VTK[rows, p, hs], start=False, stop=True)
                q.then_inc(sem("mn_done"), 1)
                for p in range(PAIRS):
                    for h in range(2):
                        x = 2 * p + h
                        q = pe.matmul(ps[6][64 * h:64 * h + 64, P * p:P * (p + 1)], WY[:, x, 0:64], ABR[:, x, 128:256],
                                      start=True, stop=True)
                q.then_inc(sem("q_done"), 1)
                fill(j, 0, 4)
                for c in range(1, CHUNKS - 1):
                    pe.wait_ge(sem("state_ready"), 8 * j + c + 1)
                    for h in range(2):
                        hs = slice(64 * h, 64 * h + 64)
                        q = pe.matmul(ps[2 + h][hs, 0:64], MT[hs, 64 * c:64 * c + 64], YH[hs, 64 * c:64 * c + 64],
                                      start=True, stop=True)
                    q.then_inc(sem("state_step"), 1)
                    fill(j, 2 * c + 2, 2 * c + 4)
                pe.wait_ge(sem("state_ready"), 8 * j + 8)
                pe.wait_ge(sem("q_ready"), j + 1)
                for p in range(PAIRS):
                    for h in range(2):
                        x, hs = 2 * p + h, slice(64 * h, 64 * h + 64)
                        b = ps[4 + h]
                        pe.matmul(b[hs, P * p:P * (p + 1)], WY[:, x, 64:128], ABR[:, x, 128:256], start=True, stop=False)
                        q = pe.matmul(b[hs, P * p:P * (p + 1)], VTK[:, p, hs], ABR[:, x, 384:512], start=False, stop=True)
                        for c in range(2):
                            o = b[hs, P * p + 64 * c:P * p + 64 * c + 64]
                            ch = 2 * p + c
                            q = pe.matmul(o, YH[hs, 64 * ch:64 * ch + 64], QT[hs, j, 64 * ch:64 * ch + 64],
                                          start=False, stop=True, skip_group_check=True)
                q.then_inc(sem("y_out"), 1)
                fold_ada(j, 4)
            head_mean(3, ps[2])
            bonus_sum(3)
            project(G_HG[3], PAIR, hhi, hlo)
            head_variance(3, ps[3])
            output_gate(3, ps[7])

            for u in range(4, 8):
                project(G_HG[u], PAIR, hhi, hlo)
            for l, n in enumerate((0, 1, 2, 4, 8, 16, 32, 64)):
                pe.wait_ge(sem("hg_factors"), l + 1)
                if n == 0:
                    pe.wait_ge(sem("rw_out"), RW_TILES)
                    for h in range(HG):
                        for c in range(4):
                            t = slice(P * c, P * (c + 1))
                            q = pe.matmul(ps[2 + h][:, t], HK[:, h, t], HQ[:, h, t], start=True, stop=True)
                    q.then_inc(sem("hg_level"), 1)
                    continue
                b0 = 6 if l % 2 else 4
                if l == 2:
                    pe.wait_ge(sem("hg_masked"), 1)
                elif l > 2:
                    pe.wait_ge(sem("hg_masked"), l - 1)
                for h in range(HG):
                    for c in range(4):
                        i = 4 * h + c
                        q = pe.matmul(ps[b0 + i // 8][:, 64 * (i % 8):64 * (i % 8) + 64], KN[:, h, P * c:P * (c + 1)],
                                      QC[:, h, 64 * c:64 * (c + 1)], start=True, stop=True)
                q.then_inc(sem("hg_level"), 1)
            pe.wait_ge(sem("hg_tail"), 1)
            for n in range(8):
                src = (HV if n < 4 else HK)[:, n % 4, :]
                if n >= 2:
                    pe.wait_ge(sem("hg_tok_copied"), n - 1)
                for c in range(4):
                    q = pe.transpose(ps[2 + n % 2][:, P * c:P * (c + 1)], src[:, P * c:P * (c + 1)], ident)
                q.then_inc(sem("hg_tok_turned"), 1)
            pe.wait_ge(sem("hg_masked"), 8)
            pe.wait_ge(sem("hg_tok_copied"), 8)
            for h in range(HG):
                if h >= 2:
                    pe.wait_ge(sem("hg_state"), 3 * (h - 1))
                for c in range(3):
                    q = pe.matmul(ps[2 + h % 2][:, P * c:P * (c + 1)], HKT[:, h, c, :], HVT[:, h, c, :], start=True, stop=True)
                q.then_inc(sem("hg_added"), 1)
            for h in range(HG):
                pe.wait_ge(sem("hg_state"), 3 * (h + 1))
                for c in range(4):
                    o = ps[4 + h][:, P * c:P * (c + 1)]
                    q = pe.matmul(o, HVT[:, h, c, :], AT[:, h, c, :], start=True, stop=c == 0)
                    if c:
                        q = pe.matmul(o, HS[:, h, c, :], HQ[:, h, P * c:P * (c + 1)], start=False, stop=True)
                q.then_inc(sem("hg_o"), 1)
            for h in range(HG):
                pe.wait_ge(sem("hg_squared"), h + 1)
                if h >= 2:
                    pe.wait_ge(sem("hg_rooted"), h - 1)
                pe.matmul(ps[2 + h % 2], ones, HSCR[:, h, :], start=True, stop=True).then_inc(sem("hg_summed"), 1)

            project(G_KR, [(0, P), (P, 192)], hhi, hlo)
            pe.wait_ge(sem("ml_squared"), 1)
            pe.wait_ge(sem("hg_rooted"), 4)
            mean_square(MSQ, 2, ps[2])
            pe.matmul(ps[3], ones, MSQ[:, 2, :], start=True, stop=True).then_inc(sem("ml_summed"), 1)
            pe.wait_ge(sem("ml_normed"), 1)
            pe.wait_ge(sem("ld_mla"), 7 * 16)
            pe.wait_ge(sem("hg_out"), 1)
            for j in range(4):
                if j >= 1:
                    pe.wait_ge(sem("qk_copied"), 4 * j)
                for k in range(2):
                    pe.matmul(ps[2], WUQ[:, k, P * j:P * (j + 1)],
                              CQ[:, k, :], start=k == 0, stop=k == 1)
                pe.matmul(ps[3], WUK[:, P * j:P * (j + 1)], CKV,
                          start=True, stop=True).then_inc(sem("qk_done"), 1)
            pe.wait_ge(sem("rope_weights"), 1)
            for j in range(2):
                if j:
                    pe.wait_ge(sem("rope_done"), 5)
                for w, b in ((WROPE, ps[4]), (WROT, ps[5])):
                    for k in range(2):
                        q = pe.matmul(b, w[:, k, P * j:P * (j + 1)], CQ[:, k, :], start=k == 0, stop=k == 1)
                q.then_inc(sem("qr_done"), 1)
            for t in range(4):
                if t >= 2:
                    pe.wait_ge(sem("vm_copied"), t - 1)
                pe.matmul(ps[6 + t % 2], CKV[:, P * t:P * (t + 1)], WUV, start=True, stop=True
                          ).then_inc(sem("vm_done"), 1)
            pe.wait_ge(sem("qk_copied"), 16)
            pe.wait_ge(sem("rope_done"), 9)
            pe.wait_ge(sem("vm_copied"), 4)
            def score(i):
                h, qb = i // 4, i % 4
                w = P * (qb + 1)
                if i >= 2:
                    pe.wait_ge(sem("prob"), i - 1)
                pe.matmul(ps[2 + i % 2][:, 0:w], QH[0:QK, h, P * qb:P * (qb + 1)], KHD[0:QK, h, 0:w],
                          start=True, stop=True).then_inc(sem("score"), 1)

            def mix_products(x0, x1):
                for x in range(x0, x1):
                    g, block, y = G_MIX + x // 16, x // 48, x % 48
                    if x % 16 == 0:
                        pe.wait_ge(sem("w_lo"), split_no[g] + 1)
                    if y == 32:
                        pe.wait_ge(sem("o_split"), block + 1)
                    nk = KD if y < 32 else 4
                    m, k = x % 16 // nk, x % nk
                    if k == 0:
                        mix_bank[0] = bank()
                    if y < 32:
                        q = mm3(pe, mix_bank[0], g, k, P * m, P * (m + 1), hhi[:, k, :], hlo[:, k, :], k == 0, k == 7, 256)
                    else:
                        q = mm3(pe, mix_bank[0], g, k, P * m, P * (m + 1), ohi[:, k, :], olo[:, k, :], k == 0, k == 3, 512)
                    if k == nk - 1:
                        q.then_inc(sem("tile_ready"), 1)

            mix_bank = [None]
            score(0)
            for i in range(4 * ML):
                h, qb = i // 4, i % 4
                if i + 1 < 4 * ML:
                    score(i + 1)
                mix_products(6 * i, 6 * i + 6)
                pe.wait_ge(sem("prob_scaled"), i + 1)
                if i >= 2:
                    pe.wait_ge(sem("pt_copied"), i - 1)
                for kb in range(qb + 1):
                    q = pe.transpose(ps[4 + i % 2][:, P * kb:P * (kb + 1)], PRB[:, i % 2, P * kb:P * (kb + 1)], ident)
                q.then_inc(sem("prob_turned"), 1)
                if qb < 3:
                    continue
                pe.wait_ge(sem("pt_copied"), i + 1)
                if h >= 2:
                    pe.wait_ge(sem("oc_copied"), h - 1)
                b = ps[6 + h % 2][64 * (h % 2):64 * (h % 2) + 64, :]
                for kb in range(4):
                    q = pe.matmul(b[:, P * kb:T], VM[:, kb, 64 * h:64 * (h + 1)], PT[:, kb, P * kb:T],
                                  start=kb == 0, stop=kb == 3)
                q.then_inc(sem("oc_done"), 1)

            mix_products(192, 208)
            pe.wait_ge(sem("oc_copied"), ML)
            pe.wait_ge(sem("ld_x2"), 16)
            for d in range(KD):
                if d >= 4:
                    pe.wait_ge(sem("xt2_copied"), d - 3)
                for t in range(4):
                    q = pe.transpose(ps[2 + d % 4][:, P * t:P * (t + 1)], XTOK2[:, t, P * d:P * (d + 1)], ident)
                q.then_inc(sem("xt2_turned"), 1)
            mix_products(208, 288)
            pe.wait_ge(sem("y_split"), 1)
            for q_ in range(4):
                project(G_OUT + q_, PAIR, hhi, hlo)

            pe.wait_ge(sem("x1_squared"), 1)
            pe.wait_ge(sem("oc_copied"), ML)
            mean_square(SQ1, KD, ps[6]).then_inc(sem("x1_summed"), 1)
            pe.wait_ge(sem("h2_split"), 1)
            for j in range(NF):
                project(G_UP + j, PAIR, hhi, hlo)
            pe.wait_ge(sem("act_split"), NF)
            for q_ in range(4):
                o = [bank(), bank()]
                for part in range(3):
                    g = G_DOWN + 3 * q_ + part
                    pe.wait_ge(sem("w_lo"), split_no[g] + 1)
                    nk, ncols = groups[g][2], groups[g][3]
                    for m in range(2):
                        for k in range(nk):
                            kk = 8 * part + k
                            q = mm3(pe, o[m], g, k, P * m, P * (m + 1), acthi[:, kk, :], actlo[:, kk, :],
                                    kk == 0, kk == NF - 1, ncols)
                        if part == 2:
                            q.then_inc(sem("tile_ready"), 1)
                    if part < 2:
                        q.then_inc(sem("down_part"), 1)
            pe.wait_ge(sem("x2_squared"), 1)
            mean_square(SQF, KD, ps[6]).then_inc(sem("x2_summed"), 1)
            pe.wait_ge(sem("x2_normed"), 1)
            for t in range(4):
                for half in range(2):
                    i = 2 * t + half
                    if i >= 2:
                        pe.wait_ge(sem("rows_ready"), i - 1)
                    for d in range(4):
                        q = pe.transpose(ps[2 + i % 2][:, P * d:P * (d + 1)], SQF[:, 4 * half + d, P * t:P * (t + 1)], ident)
                    q.then_inc(sem("rows_turned"), 1)

        @block.scalar
        def _(act):
            chain = [0]

            def link(ins):
                chain[0] += 1
                ins.then_inc(sem("act_chain"), 1)
                act.wait_ge(sem("act_chain"), chain[0])

            split_order = list(split_no)
            staged = [0]

            def stage(upto):
                while staged[0] <= min(upto, len(split_order) - 1):
                    n, g = staged[0], split_order[staged[0]]
                    w = groups[g][2] * groups[g][3]
                    act.wait_ge(sem(f"w_landed{g % 2}"), landings[g])
                    if before[n] is not None:
                        act.wait_ge(*used[before[n]])
                        act.wait_ge(sem("w_lo"), before[n] + 1)
                    act.activation(whi[:, g % 2, 0:w], wring[:, g % 2, 0:w], ACT.Copy).then_inc(sem("w_hi"), 1)
                    staged[0] += 1

            tile_no = [0]

            def tile():
                i = tile_no[0]
                tile_no[0] += 1
                act.wait_ge(sem("tile_ready"), i + 1)
                return ps[i % 2], sem(f"bank_free{i % 2}")

            act.dma_start(const[:], a["const_f"]).then_inc(sem("ld_const"), 16)
            act.dma_start(xtok, a["x"][0].rearrange("(a p) d -> p a d", p=P)).then_inc(sem("ld_x"), 16)

            act.wait_ge(sem("vec_in_psum"), 1)
            act.activation(vec[:], ps[6][:, 0:V_ROWS], ACT.Copy)
            act.activation(convv[:, 0, :], ps[6][:, 128:216], ACT.Copy)
            link(act.activation(convv[:, 1, :], ps[6][:, 256:344], ACT.Copy))
            act.activation(small[:, 32:40], col(V_C, 8), ACT.Sigmoid).then_inc(sem("vec_turned"), 1)
            act.wait_ge(sem("xt_copied"), KD)
            act.activation(sqT, xT, ACT.Square).then_inc(sem("x_squared"), 1)
            act.wait_ge(sem("lb_zero"), 1)
            act.activation(small[:, 44:48], small[:, 40:44], ACT.Exp).then_inc(sem("lb_exp"), 1)
            act.wait_ge(sem("x_summed"), 1)
            act.activation(rstd, ps[6][:], ACT.Sqrt, bias=EPS, scale=1.0 / D).then_inc(sem("x_rooted"), 1)
            stage(1)
            for d in range(KD):
                act.wait_ge(sem("h_value"), d + 1)
                act.activation(hhi[:, d, :], sqT[:, d, :], ACT.Copy).then_inc(sem("h_hi"), 1)

            stage(1)
            act.wait_ge(sem("rw_mixed"), 2)
            act.activation(LORA[0:64, :], LORA[0:64, :], ACT.Tanh).then_inc(sem("lora_in"), 1)
            act.activation(GL, GL, ACT.Sigmoid).then_inc(sem("lora_in"), 1)
            stage(3)
            for j in range(RW_TILES):
                act.wait_ge(sem("lora_out"), 2 * j + 2)
                act.activation(DEC[:, j, :], ps[2 + j % 2][:], ACT.Sigmoid, bias=col(V_W0 + j)).then_inc(sem("lora_read"), 1)
                act.activation(AA[:, j, :], ps[4 + j % 2][:], ACT.Sigmoid, bias=col(V_A0 + j)).then_inc(sem("lora_read"), 1)
            stage(5)
            for j in range(RW_TILES):
                act.wait_ge(sem("kk_summed"), j + 1)
                act.activation(outs[:, j, :], ps[6 + j % 2][:], ACT.Sqrt).then_inc(sem("kk_norm_read"), 1)
            stage(6)
            tile_no[0] += 14

            def decays(j):
                if j == 0:
                    act.wait_ge(sem("log_summed"), RW_TILES)
                else:
                    act.wait_ge(sem("rw_tildes"), j)
                act.activation(PP, DEC[:, j, :], ACT.Exp, scale=-E_HALF)
                act.activation(PINV, DEC[:, j, :], ACT.Exp, scale=E_HALF).then_inc(sem("decay_ready"), 1)

            def hgrn_tiles(u):
                h = u // 2
                act.wait_ge(sem("rw_out"), h + 1)
                bk, free = tile()
                if u % 2:
                    act.activation(HV[:, h, :], bk[:], ACT.Copy).then_inc(free, 1)
                    bk, free = tile()
                    act.activation(HO[:, h, :], bk[:], ACT.Sigmoid).then_inc(sem("hg_og"), 1)
                else:
                    act.activation(HQ[:, h, :], bk[:], ACT.Copy).then_inc(free, 1)
                    bk, free = tile()
                    act.activation(HF[:, h, :], bk[:], ACT.Sigmoid)
                    act.activation(HK[:, h, :], bk[:], ACT.Sigmoid, scale=-1.0).then_inc(free, 1)

            decays(0)
            for j in range(RW_TILES):
                def token_major(n):
                    act.wait_ge(sem("tok_turned"), 4 * j + n + 1)
                    src = ps[6 + n % 2][:]
                    if n == 0:
                        dst, src = AV[:, :, 0:64], src.rearrange("p (i f) -> p i f", i=8)
                    else:
                        dst = (VTK, KTOK[0], KTOK[1])[n - 1]
                        src = src.rearrange("p (q f) -> p q f", q=PAIRS)
                    act.activation(dst, src, ACT.Copy).then_inc(sem("tok_copied"), 1)

                token_major(0)
                token_major(1)
                for l in range(6):
                    for half in range(2):
                        act.wait_ge(sem("t_turned"), 2 * (6 * j + l) + half + 1)
                        dst = (TM if l == 0 else TT)[:, 4 * half:4 * half + 4, :]
                        act.activation(dst, ps[2 + half][:].rearrange("p (i t) -> p i t", i=4), ACT.Copy
                                       ).then_inc(sem("t_copied"), 1)
                    if l == 2:
                        token_major(2)
                        token_major(3)
                    if l == 3 and j + 1 < RW_TILES:
                        decays(j + 1)
                    if l == 4:
                        stage(7 + j)
                act.wait_ge(sem("akv_done"), j + 1)
                act.activation(AV[:, :, 64:128], ps[6][:].rearrange("p (i f) -> p i f", i=8), ACT.Copy
                               ).then_inc(sem("akv_copied"), 1)
                for half in range(2):
                    act.wait_ge(sem("wy_done"), 2 * j + half + 1)
                    act.activation(WY[:, 4 * half:4 * half + 4, :], ps[2 + half][:].rearrange("p (i t) -> p i t", i=4),
                                   ACT.Copy).then_inc(sem("wy_copied"), 1)
                if j == 0:
                    for k in range(2):
                        bk, free = tile()
                        act.activation(CQ[:, k, :], bk[:], ACT.Copy).then_inc(free, 1)
                else:
                    hgrn_tiles(j - 1)
                if j == 3:
                    stage(11)
                act.wait_ge(sem("y_out"), j + 1)
                for h in range(2):
                    hs = slice(64 * h, 64 * h + 64)
                    q = act.activation(YV[hs, j, :], ps[4 + h][hs, :], ACT.Copy)
                q.then_inc(sem("y_in"), 1)
                act.wait_ge(sem("stat"), 2 * j + 2)
                act.activation(YSQ[:, j, :], (ps[3] if j == 3 else ps[0])[:], ACT.Sqrt, bias=REPS, scale=1.0 / CH
                               ).then_inc(sem("y_rooted"), 1)

            for u in range(3, 8):
                stage(9 + u)
                hgrn_tiles(u)
            for n in range(8):
                act.wait_ge(sem("hg_tok_turned"), n + 1)
                dst = (HVT if n < 4 else HKT)[:, n % 4, :, :]
                act.activation(dst, ps[2 + n % 2][:].rearrange("p (c t) -> p c t", c=4), ACT.Copy
                               ).then_inc(sem("hg_tok_copied"), 1)
            for h in range(HG):
                act.wait_ge(sem("hg_o"), h + 1)
                if h == 0:
                    act.wait_ge(sem("hg_masked"), 8)
                act.activation(HSCR[:, h, :], ps[4 + h][:], ACT.Square).then_inc(sem("hg_squared"), 1)
            for h in range(HG):
                act.wait_ge(sem("hg_summed"), h + 1)
                act.activation(HSCR[:, h, :], ps[2 + h % 2][:], ACT.Sqrt, bias=EPS, scale=1.0 / P
                               ).then_inc(sem("hg_rooted"), 1)

            stage(16)
            act.wait_ge(sem("hg_out"), 1)
            bk, free = tile()
            stage(17)
            act.activation(CKV, bk[:], ACT.Copy).then_inc(free, 1)
            bk, free = tile()
            act.activation(KR[0:32, :], bk[0:32, :], ACT.Copy)
            act.activation(KRR[0:32, :], bk[32:64, :], ACT.Copy).then_inc(free, 1)
            act.wait_ge(sem("bank_free0"), 17)
            act.wait_ge(sem("bank_free1"), 17)
            act.activation(MSQ[:, 0:2, :], CQ, ACT.Square)
            act.activation(MSQ[:, 2, :], CKV, ACT.Square).then_inc(sem("ml_squared"), 1)
            act.wait_ge(sem("ml_summed"), 1)
            act.activation(MRS[:, 0, :], ps[2][:], ACT.Sqrt, bias=EPS, scale=0.5 / P)
            act.activation(MRS[:, 1, :], ps[3][:], ACT.Sqrt, bias=EPS, scale=1.0 / P).then_inc(sem("ml_rooted"), 1)
            act.wait_ge(sem("angles"), 1)
            act.activation(SIN, SIN, ACT.Sin)
            act.activation(COS, COS, ACT.Sin).then_inc(sem("sines"), 1)
            for j in range(4):
                act.wait_ge(sem("qk_done"), j + 1)
                for i in range(2):
                    rows = slice(64 * i, 64 * i + 64)
                    act.activation(QH[0:64, 2 * j + i, :], ps[2][rows, :], ACT.Copy).then_inc(sem("qk_copied"), 1)
                    act.activation(KHD[0:64, 2 * j + i, :], ps[3][rows, :], ACT.Copy).then_inc(sem("qk_copied"), 1)
            for t in range(4):
                act.wait_ge(sem("vm_done"), t + 1)
                act.activation(VM[:, t, :], ps[6 + t % 2][:], ACT.Copy).then_inc(sem("vm_copied"), 1)

            def prob(i):
                w = P * (i % 4 + 1)
                act.wait_ge(sem("row_max"), i + 1)
                if i >= 2:
                    act.wait_ge(sem("prob_turned"), i - 1)
                act.activation(PRB[:, i % 2, 0:w], ps[2 + i % 2][:, 0:w], ACT.Exp, bias=small[:, 48 + i % 2:49 + i % 2],
                               scale=MLA_SCALE, accum_out=small[:, 50 + i % 2:51 + i % 2]).then_inc(sem("prob"), 1)

            def mix_gates(x0, x1):
                for x in range(x0, x1):
                    block, y = x // 48, x % 48
                    if x % 16 == 0:
                        stage(17 + x // 16 + 1)
                    if y == 8:
                        if block:
                            act.wait_ge(sem("tile_ready"), MIX_TILE + 8 * block)
                        if block == 4:
                            act.wait_ge(sem("o_value"), 1)
                        b = MIX_BLOCKS[block][1]
                        act.activation(ohi[:], outs[:, 4 * b:4 * b + 4, :], ACT.Copy).then_inc(sem("o_hi"), 1)
                    if y < 32 and x % 8 == 7:
                        i = MIX_TILE + 8 * block + y // 8
                        act.wait_ge(sem("tile_ready"), i + 1)
                        if block:
                            act.wait_ge(sem("gates_used"), block)
                        act.activation(GATE[:, y // 8, :], ps[i % 2][:], ACT.Sigmoid).then_inc(sem(f"bank_free{i % 2}"), 1)

            prob(0)
            for i in range(4 * ML):
                h, qb = i // 4, i % 4
                if i + 1 < 4 * ML:
                    prob(i + 1)
                act.wait_ge(sem("prob_turned"), i + 1)
                if qb == 0 and h:
                    act.wait_ge(sem("oc_done"), h)
                act.activation(PT[:, 0:qb + 1, P * qb:P * (qb + 1)],
                               ps[4 + i % 2][:, 0:P * (qb + 1)].rearrange("p (k t) -> p k t", k=qb + 1), ACT.Copy
                               ).then_inc(sem("pt_copied"), 1)
                mix_gates(6 * i, 6 * i + 6)
            mix_gates(192, 288)
            n = 35
            tile_no[0] = MIX_TILE + 48
            act.wait_ge(sem("y_value"), 1)
            act.wait_ge(sem("tile_ready"), tile_no[0])
            act.activation(hhi[:], YT, ACT.Copy).then_inc(sem("y_hi"), 1)
            for q_ in range(4):
                stage(n + 1)
                n += 1
                tile_no[0] += 2
                act.wait_ge(sem("x1_tile"), 2 * q_ + 2)
                for d in (2 * q_, 2 * q_ + 1):
                    q = act.activation(SQ1[:, d, :], X1[:, d, :], ACT.Square)
            q.then_inc(sem("x1_squared"), 1)
            act.wait_ge(sem("x1_summed"), 1)
            act.activation(tail[:, 0, :], ps[6][:], ACT.Sqrt, bias=EPS, scale=1.0 / D).then_inc(sem("x1_rooted"), 1)
            act.wait_ge(sem("h2_value"), 1)
            act.activation(hhi[:], SQ1, ACT.Copy).then_inc(sem("h2_hi"), 1)
            for j in range(NF):
                stage(n + 1)
                n += 1
                tile_no[0] += 2
                act.wait_ge(sem("conv_gate"), j + 1)
                act.activation(tail[:, 1, :], CG[:, j % 2, :], ACT.Sigmoid).then_inc(sem("gate_sig"), 1)
                act.wait_ge(sem("act_value"), j + 1)
                act.activation(acthi[:, j, :], CV[:, j % 2, :], ACT.Copy).then_inc(sem("act_hi"), 1)
            for q_ in range(4):
                for part in range(3):
                    stage(n + 1)
                    n += 1
            act.wait_ge(sem("x2_tile"), KD)
            act.activation(SQF, X1, ACT.Square).then_inc(sem("x2_squared"), 1)
            act.wait_ge(sem("x2_summed"), 1)
            act.activation(tail[:, 0, :], ps[6][:], ACT.Sqrt, bias=EPS, scale=1.0 / D).then_inc(sem("x2_rooted"), 1)

        @block.vector
        def _(dve):
            chain = [0]

            def link(ins):
                chain[0] += 1
                ins.then_inc(sem("dve_chain"), 1)
                dve.wait_ge(sem("dve_chain"), chain[0])

            tile_no = [0]

            def tile():
                i = tile_no[0]
                tile_no[0] += 1
                dve.wait_ge(sem("tile_ready"), i + 1)
                return ps[i % 2], sem(f"bank_free{i % 2}")

            mul, add, sub = ALU.mult, ALU.add, ALU.subtract
            dve.memset(small[:, 0:1], NORM_EPS)
            dve.memset(small[:, 1:2], RWKV_EPS)
            for d in range(KD):
                dve.wait_ge(sem("xt_turned"), d + 1)
                dve.tensor_copy(xT[:, d, :], ps[2 + d % 4][:]).then_inc(sem("xt_copied"), 1)
            dve.wait_ge(sem("vec_turned"), 1)
            dve.tensor_tensor(cond[:], small[:, 32:40], col(V_C, 8), mul).then_inc(sem("cond_ready"), 1)
            dve.tensor_tensor(small[:, 40:44], col(V_LB, 4), col(V_LB, 4), sub).then_inc(sem("lb_zero"), 1)
            dve.wait_ge(sem("lb_exp"), 1)
            link(dve.reciprocal(small[:, 56:60], small[:, 44:48]))
            link(dve.tensor_tensor(small[:, 60:64], small[:, 56:60], small[:, 44:48], mul))
            link(dve.tensor_tensor(LBV, small[:, 60:64], small[:, 60:64], sub))
            link(dve.tensor_scalar(OMLB, LBV, -1.0, 1.0, mul, add))
            link(dve.tensor_scalar(ONE_MU, col(V_MU, 14), -1.0, 1.0, mul, add))
            link(dve.tensor_scalar(small[:, 12:16], col(V_KA, 4), -1.0, 1.0, mul, add))
            for n, g in enumerate(DVE_ADA):
                w = ada_slot(g)
                dve.wait_ge(*ada_landed(g))
                if n == 0:
                    dve.wait_ge(sem("cond_ready"), 1)
                if n == 2:
                    dve.wait_ge(sem("x_rooted"), 1)
                    link(dve.reciprocal(rstd, rstd))
                    dve.tensor_tensor(sqT, xT, rstd.unsqueeze(1).broadcast_to([P, KD, T]), mul)
                for k in range(KD):
                    wk = w[:, 256 * k:256 * (k + 1)]
                    if k == 0:
                        link(dve.tensor_scalar(wk, wk, cond[:, 0:1], None, mul))
                    else:
                        link(dve.scalar_tensor_tensor(w[:, 0:256], wk, cond[:, k:k + 1], w[:, 0:256], mul, add))
                dve.sem_inc(sem("ada_dve"), 1)
            dve.wait_ge(sem("ada_used"), 8)
            link(dve.tensor_tensor(mod[:, 0:16], ps[7][:, 0:16], vec[:, 0:16], add))
            link(dve.tensor_scalar(mod[:, 8:16], mod[:, 8:16], 1.0, None, add))
            for d in range(KD):
                dve.tensor_scalar(sqT[:, d, :], sqT[:, d, :], mod[:, 8 + d:9 + d], mod[:, d:d + 1], mul, add
                                  ).then_inc(sem("h_value"), 1)
            for d in range(KD):
                dve.wait_ge(sem("h_hi"), d + 1)
                dve.wait_ge(sem("h_value"), d + 1)
                q = dve.tensor_tensor(hlo[:, d, :], sqT[:, d, :], hhi[:, d, :].bitcast(F32), sub)
            q.then_inc(sem("h_split"), 1)

            def chunks(v):
                return v.rearrange("p (c t) -> p c t", c=CHUNKS)

            def key_norm(j):
                nrm = outs[:, j, :]
                dve.wait_ge(sem("kk_norm_read"), j + 1)
                link(dve.tensor_scalar(nrm, nrm, 1e-12, None, ALU.max))
                link(dve.reciprocal(nrm, nrm))
                link(dve.tensor_tensor(KK[:, j, :], KK[:, j, :], nrm, mul))
                link(dve.tensor_scalar(nrm, AA[:, j, :], col(V_KA + j), small[:, 12 + j:13 + j], mul, add))
                link(dve.tensor_tensor(K[:, j, :], K[:, j, :], nrm, mul))
                link(dve.tensor_tensor(AA[:, j, :], AA[:, j, :], KK[:, j, :], mul))
                link(dve.tensor_scalar(KK[:, j, :], KK[:, j, :], -1.0, None, mul))

            for n, x in enumerate((12, 13, 4, 5, 6, 7, 0, 1, 2, 3, 8, 9, 10, 11)):
                bk, free = tile()
                dst = LORA if x == 12 else GL if x == 13 else (R, K, V)[x // 4][:, x % 4, :]
                if x == 12:
                    dve.wait_ge(sem("h_split"), 1)
                link(dve.tensor_scalar(dst, bk[:], ONE_MU[:, x:x + 1], None, mul))
                link(dve.scalar_tensor_tensor(dst[:, 1:T], bk[:, 0:T - 1], col(V_MU + x), dst[:, 1:T], mul, add))
                dve.sem_inc(free, 1)
                dve.sem_inc(sem("rw_mixed"), 1)
                if 4 <= x < 8:
                    j = x - 4
                    link(dve.tensor_scalar(KK[:, j, :], K[:, j, :], col(V_KK + j), None, mul))
                    dve.tensor_tensor(outs[:, j, :], KK[:, j, :], KK[:, j, :], mul).then_inc(sem("kk_squared"), 1)
                if x == 0:
                    link(dve.memset(SCR, 1.0))
                    link(dve.memset(chunks(SCR)[:, :, 0:1], 0.0))
                    dve.wait_ge(sem("lora_read"), 8)
                    for j in range(RW_TILES):
                        q = dve.tensor_tensor_scan(DEC[:, j, :], SCR, DEC[:, j, :], 0.0, mul, add)
                        q.then_inc(sem("log_summed"), 1)
                    dve.wait_ge(sem("log_summed"), RW_TILES)
                if x in (2, 8):
                    key_norm(int(x == 8))

            def hats(j):
                ar_ = AR[j % 2]
                dve.wait_ge(sem("decay_ready"), j + 1)
                if j == 0:
                    dve.wait_ge(sem("pad_zero"), 1)
                rr = R[:, j, :].rearrange("p (q t) -> p q t", q=PAIRS)
                pp = PP.rearrange("p (q t) -> p q t", q=PAIRS)
                dve.tensor_tensor(ar_[:, :, 1, :], rr, pp, mul)
                for c in range(2):
                    ar = ar_[:, :, 0, 64 * c:64 * c + 64]
                    kk = KK[:, j, :].rearrange("p (q c t) -> p q c t", q=PAIRS, c=2)[:, :, c, :]
                    pc = PP.rearrange("p (q c t) -> p q c t", q=PAIRS, c=2)[:, :, c, :]
                    dve.tensor_tensor(ar[:, :, 1:64], kk[:, :, 1:64], pc[:, :, 0:63], mul)
                    dve.tensor_copy(ar[:, :, 0:1], kk[:, :, 0:1])
                for h in range(2):
                    hs = slice(64 * h, 64 * h + 64)
                    dve.tensor_tensor(PAD[hs, h, :], AA[hs, j, :], PINV[hs, :], mul)
                    q = dve.tensor_tensor(PAD[hs, 2 + h, :], K[hs, j, :], PINV[hs, :], mul)
                q.then_inc(sem("rw_hats"), 1)

            def centre(j, bank_):
                y = YV[:, j, :]
                dve.wait_ge(sem("y_in"), j + 1)
                dve.wait_ge(sem("stat"), 2 * j + 1)
                link(dve.scalar_tensor_tensor(y, bank_[:], -1.0 / CH, y, mul, add))
                dve.tensor_tensor(YSQ[:, j, :], y, y, mul).then_inc(sem("y_centred"), 1)

            def bonus(j):
                dve.wait_ge(sem("bonus_sum"), j + 1)
                dve.tensor_tensor(BONUS[:, j, :], ps[6][:], V[:, j, :], mul).then_inc(sem("bonus_ready"), 1)

            def finish(j, bank_, step):
                y, root = YV[:, j, :], YSQ[:, j, :]
                if step == 0:
                    dve.wait_ge(sem("y_rooted"), j + 1)
                    link(dve.reciprocal(root, root))
                elif step == 1:
                    link(dve.tensor_tensor(y, y, root, mul))
                    link(dve.tensor_scalar(y, y, col(V_LNW + j), col(V_LNB + j), mul, add))
                else:
                    dve.wait_ge(sem("bonus_ready"), j + 1)
                    link(dve.tensor_tensor(y, y, BONUS[:, j, :], add))
                    dve.wait_ge(sem("g_out"), j + 1)
                    dve.tensor_tensor(outs[:, j, :], y, bank_[:], mul).then_inc(sem("rw_out"), 1)

            last = LAST.unsqueeze(2).broadcast_to([P, CHUNKS, CH])

            def tildes(j):
                dve.wait_ge(sem("rw_hats"), j + 1)
                if j:
                    dve.wait_ge(sem("tok_turned"), 4 * j)
                link(dve.tensor_copy(LAST.unsqueeze(2), chunks(PP)[:, :, 63:64]))
                for h in range(2):
                    hs = slice(64 * h, 64 * h + 64)
                    dve.tensor_tensor(chunks(BH)[hs], chunks(PAD[:, h, :])[hs], last[hs], mul)
                    q = dve.tensor_tensor(chunks(KH)[hs], chunks(PAD[:, 2 + h, :])[hs], last[hs], mul)
                q.then_inc(sem("rw_tildes"), 1)

            def output_gates(h):
                dve.wait_ge(sem("hg_og"), h + 1)
                dve.wait_ge(sem("tile_ready"), 20 + 4 * h)
                dve.tensor_tensor(HO[:, h, :], HO[:, h, :], ps[1][:], mul).then_inc(sem("bank_free1"), 1)

            hats(0)
            for j in range(RW_TILES):
                for i in range(8):
                    dve.wait_ge(sem("abr_done"), 8 * j + i + 1)
                    dve.tensor_tensor(ABR[:, i, :], ps[2 + i % 4][:], cst("rw_mask"), mul).then_inc(sem("abr_copied"), 1)
                    if j and i == 2:
                        centre(j - 1, ps[0])
                    if j and i == 3:
                        bonus(j - 1)
                dve.wait_ge(sem("abr_copied"), 8 * j + 8)
                for half in range(2):
                    x = slice(4 * half, 4 * half + 4)
                    wide = [P, 4, P]
                    link(dve.tensor_tensor(TT[:, x, :], ABR[:, x, 0:P], cst("pair_t").unsqueeze(1).broadcast_to(wide), mul))
                    dve.tensor_tensor(TT[:, x, :], TT[:, x, :], ident.unsqueeze(1).broadcast_to(wide), add
                                      ).then_inc(sem("t_added"), 1)
                for l, n in enumerate((2, 4, 8, 16, 32)):
                    if l == 1:
                        tildes(j)
                    if l >= 2 and j:
                        finish(j - 1, ps[0], l - 2)
                    mask = cst("level")[:, 64 * l:64 * l + 64].unsqueeze(1).broadcast_to([P, 4, 64])
                    for half in range(2):
                        dve.wait_ge(sem("y_done"), 2 * (5 * j + l) + half + 1)
                        dve.tensor_tensor(YH[:, 256 * half:256 * half + 256].rearrange("p (i c) -> p i c", i=4),
                                          ps[4 + half][:, 0:256].rearrange("p (i c) -> p i c", i=4), mask, mul
                                          ).then_inc(sem("y_masked"), 1)
                    for half in range(2):
                        dve.wait_ge(sem("ty_done"), 2 * (5 * j + l) + half + 1)
                        dve.wait_ge(sem("t_copied"), 2 * (6 * j) + 2)
                        first = TM[:, 4 * half:4 * half + 4, :].rearrange("p i (b w n) -> p (i b) w n", w=2, n=n)[:, :, 0, :]
                        dve.tensor_tensor(first, first, ps[4 + half][:, 256:512].rearrange("p (b n) -> p b n", n=n), add
                                          ).then_inc(sem("t_added"), 1)
                if j + 1 < RW_TILES:
                    hats(j + 1)
                c0, c1 = 14 + 10 * j + 2 * (j == 0), min(24 + 10 * j, 48)
                dve.wait_ge(sem("ada_used"), c1 // 2)
                dve.tensor_tensor(mod[:, c0:c1], ps[1][:, c0:c1], vec[:, c0:c1], add).then_inc(sem("mod_read"), 1)
                dve.wait_ge(sem("mod_read"), j + 1)
                dve.wait_ge(sem("mn_done"), j + 1)
                mt = MT.rearrange("p (q c f) -> p q c f", q=PAIRS, c=2)
                nn_ = NN.rearrange("p (q c f) -> p q c f", q=PAIRS, c=2)
                link(dve.tensor_tensor(chunks(MT), cst("eye64").unsqueeze(1).broadcast_to([P, CHUNKS, CH]), last, mul))
                for c in range(2):
                    b = ps[4 + c][:].rearrange("p (w q f) -> p w q f", w=2, q=PAIRS)
                    dve.tensor_tensor(mt[:, :, c, :], mt[:, :, c, :], b[:, 0, :, :], add)
                    link(dve.tensor_copy(nn_[:, :, c, :], b[:, 1, :, :]))
                dve.wait_ge(sem("q_done"), j + 1)
                dve.tensor_tensor(QT[:, j, :].rearrange("p (q t) -> p q t", q=PAIRS),
                                  ps[6][:].rearrange("p (q t) -> p q t", q=PAIRS), AR[j % 2][:, :, 1, :], add).then_inc(sem("q_ready"), 1)
                dve.memset(YH[:, 0:64], 0.0).then_inc(sem("state_ready"), 1)
                dve.tensor_copy(YH[:, 64:128], NN[:, 0:64]).then_inc(sem("state_ready"), 1)
                for c in range(1, CHUNKS - 1):
                    dve.wait_ge(sem("state_step"), 6 * j + c)
                    for h in range(2):
                        hs = slice(64 * h, 64 * h + 64)
                        q = dve.tensor_tensor(YH[hs, 64 * c + 64:64 * c + 128], ps[2 + h][hs, 0:64], NN[hs, 64 * c:64 * c + 64], add)
                    q.then_inc(sem("state_ready"), 1)
                link(dve.tensor_tensor(BONUS[:, j, :], R[:, j, :], K[:, j, :], mul))
                dve.tensor_scalar(BONUS[:, j, :], BONUS[:, j, :], col(V_RK + j), None, mul).then_inc(sem("rk_ready"), 1)
                if j == 2:
                    output_gates(0)
                if j < 2:
                    key_norm(j + 2)
                dve.wait_ge(sem("y_out"), j + 1)

            link(dve.tensor_scalar(mod[:, 32:40], mod[:, 32:40], 1.0, None, add))
            centre(3, ps[2])
            bonus(3)
            for step in range(3):
                finish(3, ps[7], step)
            dve.wait_ge(sem("rw_out"), RW_TILES)

            for h in range(1, HG):
                output_gates(h)
            tile_no[0] = 32
            for h in range(HG):
                link(dve.tensor_scalar(HF[:, h, :], HF[:, h, :], OMLB[:, h:h + 1], LBV[:, h:h + 1], mul, add))
                link(dve.tensor_scalar(HK[:, h, :], HK[:, h, :], OMLB[:, h:h + 1], None, mul))
            link(dve.tensor_scalar(HF, HF, 1e-30, None, ALU.max))
            dve.memset(KN, 0.0)
            dve.memset(SUF, 1.0).then_inc(sem("hg_factors"), 1)
            dve.wait_ge(sem("hg_factors"), 1)

            def halves(v, n):
                return v.rearrange("p h (b w n) -> p (h b) w n", w=2, n=n)

            def masked(l, n):
                b0 = 6 if l % 2 else 4
                dve.wait_ge(sem("hg_level"), l + 1)
                dve.wait_ge(sem("hg_masked"), l)
                for i in range(2):
                    mask = consti[:, l - 1, :].unsqueeze(1).broadcast_to([P, 8, 64]).rearrange("p i (b n) -> p i b n", n=n)
                    at = AT[:, 2 * i:2 * i + 2, :, :].rearrange("p h c (b w n) -> p (h c) b w n", w=2, n=n)[:, :, :, 1, :]
                    q = None
                    src = ps[b0 + i][:].rearrange("p (i b n) -> p i b n", i=8, n=n)
                    q = dve.copy_predicated(at, mask, src)
                q.then_inc(sem("hg_masked"), 1)

            for l, n in enumerate((1, 2, 4, 8, 16, 32, 64)):
                k_, q_, f_, s_ = halves(HK, n), halves(HQ, n), halves(HF, n), halves(SUF, n)
                kn = halves(KN, n)
                if l:
                    dve.wait_ge(sem("hg_level"), l + 1)
                qc = QC.rearrange("p h (b n) -> p (h b) n", n=n)
                dve.tensor_tensor(qc, q_[:, :, 1, :], f_[:, :, 1, :], mul)
                dve.tensor_tensor(kn[:, :, 0, :], k_[:, :, 0, :], s_[:, :, 0, :], mul).then_inc(sem("hg_factors"), 1)
                shape = [P, HG * T // (2 * n), n]
                link(dve.tensor_tensor(s_[:, :, 0, :], s_[:, :, 0, :], f_[:, :, 1, n - 1:n].broadcast_to(shape), mul))
                link(dve.tensor_tensor(f_[:, :, 1, :], f_[:, :, 1, :], f_[:, :, 0, n - 1:n].broadcast_to(shape), mul))
                if l == 0:
                    dve.wait_ge(sem("hg_level"), 1)
                    for h in range(HG):
                        q = dve.tensor_tensor(AT[:, h, :, :], ps[2 + h][:].rearrange("p (c t) -> p c t", c=4),
                                              ident.unsqueeze(1).broadcast_to([P, 4, P]), mul)
                    q.then_inc(sem("hg_masked"), 1)
                    dve.wait_ge(sem("hg_masked"), 1)
                else:
                    masked(l, n // 2)
            masked(7, 64)
            dve.tensor_tensor(HQ, HQ, HF, mul)
            dve.tensor_tensor(HK, HK, SUF, mul).then_inc(sem("hg_tail"), 1)
            for h in range(HG):
                dve.wait_ge(sem("hg_added"), h + 1)
                b = ps[2 + h % 2]
                dve.tensor_copy(HS[:, h, 1, :], b[:, 0:P]).then_inc(sem("hg_state"), 1)
                for c in (1, 2):
                    dve.wait_ge(sem("hg_state"), 3 * h + c)
                    dve.scalar_tensor_tensor(HS[:, h, c + 1, :], HS[:, h, c, :], HF[:, h, P * (c + 1) - 1:P * (c + 1)],
                                             b[:, P * c:P * (c + 1)], mul, add).then_inc(sem("hg_state"), 1)
            for h in range(HG):
                dve.wait_ge(sem("hg_rooted"), h + 1)
                sc = HSCR[:, h, :]
                link(dve.reciprocal(sc, sc))
                link(dve.tensor_tensor(sc, sc, HO[:, h, :], mul))
                q = dve.scalar_tensor_tensor(outs[:, 4 + h, :], ps[4 + h][:], col(V_HN), sc, mul, mul)
            q.then_inc(sem("hg_out"), 1)

            tile_no[0] += 2
            dve.wait_ge(sem("ml_rooted"), 1)
            link(dve.reciprocal(MRS, MRS))
            for k in range(2):
                dve.scalar_tensor_tensor(CQ[:, k, :], CQ[:, k, :], col(V_QN + k), MRS[:, 0, :], mul, mul)
            dve.scalar_tensor_tensor(CKV, CKV, col(V_KV), MRS[:, 1, :], mul, mul).then_inc(sem("ml_normed"), 1)
            dve.wait_ge(sem("ld_mla"), 7 * 16)
            for k in range(2):
                wr = WROPE[:, k, :].rearrange("p (h n) -> p h n", n=ROPE)
                wx = WROT[:, k, :].rearrange("p (h n) -> p h n", n=ROPE)
                dve.tensor_copy(wx[:, :, 0:16], wr[:, :, 16:32])
                q = dve.tensor_copy(wx[:, :, 16:32], wr[:, :, 0:16])
            q.then_inc(sem("rope_weights"), 1)
            magic, c1, c2 = 12582912.0, 6.28125, 0.0019350051879882812
            c3 = 2 * np.pi - c1 - c2
            link(dve.tensor_copy(RED, ANG.bitcast(I32)))
            link(dve.tensor_scalar(ANG, RED, cst("freq"), None, mul))
            for dst, quarter in ((SIN, 0.0), (COS, 0.25)):
                link(dve.tensor_scalar(RED, ANG, float(1 / (2 * np.pi)), quarter, mul, add))
                link(dve.tensor_scalar(RED, RED, magic, None, add))
                link(dve.tensor_scalar(RED, RED, magic, None, sub))
                link(dve.scalar_tensor_tensor(dst, RED, -c1, ANG, mul, add))
                link(dve.scalar_tensor_tensor(dst, RED, -c2, dst, mul, add))
                link(dve.scalar_tensor_tensor(dst, RED, -float(c3), dst, mul, add))
                if quarter:
                    link(dve.tensor_scalar(dst, dst, float(np.pi / 2), None, add))
                link(dve.tensor_scalar(dst, dst, 3.1415925, -3.1415925, ALU.min, ALU.max))
            dve.sem_inc(sem("angles"), 1)
            dve.wait_ge(sem("sines"), 1)
            link(dve.tensor_scalar(SIN, SIN, cst("rsign"), None, mul))
            q4 = slice(0, ROPE)
            link(dve.tensor_tensor(KR[q4, :], KR[q4, :], COS[q4, :], mul))
            link(dve.tensor_tensor(KRR[q4, :], KRR[q4, :], SIN[q4, :], mul))
            for h in range(ML):
                q = dve.tensor_tensor(KHD[NOPE:QK, h, :], KR[q4, :], KRR[q4, :], add)
            q.then_inc(sem("rope_done"), 1)
            for j in range(2):
                dve.wait_ge(sem("qr_done"), j + 1)
                link(dve.tensor_tensor(RT, ps[4][:], COS, mul))
                link(dve.tensor_tensor(RED, ps[5][:], SIN, mul))
                for i in range(4):
                    rows = slice(32 * i, 32 * i + 32)
                    q = dve.tensor_tensor(QH[NOPE:QK, 4 * j + i, :], RT[rows, :], RED[rows, :], add)
                    q.then_inc(sem("rope_done"), 1)
                dve.wait_ge(sem("rope_done"), 4 * j + 5)

            def row_max(i):
                w = P * (i % 4 + 1)
                b, s2 = ps[2 + i % 2], i % 2
                dve.wait_ge(sem("score"), i + 1)
                link(dve.tensor_tensor(b[:, w - P:w], b[:, w - P:w], cst("causal"), add))
                link(dve.reduce_max(small[:, 52 + s2:53 + s2], b[:, 0:w], AX.X))
                dve.tensor_scalar(small[:, 48 + s2:49 + s2], small[:, 52 + s2:53 + s2], -MLA_SCALE, None, mul
                                  ).then_inc(sem("row_max"), 1)

            def mix_gated(x0, x1):
                for x in range(x0, x1):
                    block, y = x // 48, x % 48
                    half, b = MIX_BLOCKS[block]
                    if y == 12:
                        dve.wait_ge(sem("o_hi"), block + 1)
                        dve.tensor_tensor(olo[:], outs[:, 4 * b:4 * b + 4, :], ohi[:].bitcast(F32), sub
                                          ).then_inc(sem("o_split"), 1)
                    if y >= 32 and x % 4 == 3:
                        m = (y - 32) // 4
                        i = MIX_TILE + 8 * block + 4 + m
                        dve.wait_ge(sem("tile_ready"), i + 1)
                        yt = YT[:, 4 * half + m, :]
                        dve.wait_ge(sem("bank_free0"), FREE_AT(i - m)[0])
                        dve.wait_ge(sem("bank_free1"), FREE_AT(i - m)[1])
                        if b == 0:
                            link(dve.tensor_tensor(yt, GATE[:, m, :], ps[i % 2][:], mul))
                        else:
                            link(dve.tensor_tensor(TMP[:, m, :], GATE[:, m, :], ps[i % 2][:], mul))
                            link(dve.tensor_tensor(yt, yt, TMP[:, m, :], add))
                        dve.sem_inc(sem(f"bank_free{i % 2}"), 1)
                        if m == 3:
                            dve.sem_inc(sem("gates_used"), 1)

            row_max(0)
            for i in range(4 * ML):
                if i + 1 < 4 * ML:
                    row_max(i + 1)
                w, s2, h = P * (i % 4 + 1), i % 2, i // 4
                dve.wait_ge(sem("prob"), i + 1)
                link(dve.reciprocal(small[:, 54 + s2:55 + s2], small[:, 50 + s2:51 + s2]))
                dve.tensor_scalar(PRB[:, s2, 0:w], PRB[:, s2, 0:w], small[:, 54 + s2:55 + s2], None, mul
                                  ).then_inc(sem("prob_scaled"), 1)
                if i % 4 == 3:
                    dve.wait_ge(sem("oc_done"), h + 1)
                    rows = slice(64 * (h % 2), 64 * (h % 2) + 64)
                    dve.tensor_copy(outs[rows, 8 + h // 2, :], ps[6 + h % 2][rows, :]).then_inc(sem("oc_copied"), 1)
                mix_gated(6 * i, 6 * i + 6)
            dve.wait_ge(sem("oc_copied"), ML)
            dve.sem_inc(sem("o_value"), 1)

            mix_gated(192, 208)
            for d in range(KD):
                dve.wait_ge(sem("xt2_turned"), d + 1)
                dve.tensor_copy(XT2[:, d, :], ps[2 + d % 4][:]).then_inc(sem("xt2_copied"), 1)
            mix_gated(208, 288)
            tile_no[0] = MIX_TILE + 48
            dve.sem_inc(sem("y_value"), 1)
            dve.wait_ge(sem("y_hi"), 1)
            dve.tensor_tensor(hlo[:], YT, hhi[:].bitcast(F32), sub).then_inc(sem("y_split"), 1)
            for d in range(KD):
                bk, free = tile()
                link(dve.scalar_tensor_tensor(X1[:, d, :], bk[:], mod[:, 16 + d:17 + d], XT2[:, d, :], mul, add))
                dve.sem_inc(free, 1)
                dve.sem_inc(sem("x1_tile"), 1)
            dve.wait_ge(sem("x1_rooted"), 1)
            link(dve.reciprocal(tail[:, 0, :], tail[:, 0, :]))
            for d in range(KD):
                link(dve.tensor_tensor(SQ1[:, d, :], X1[:, d, :], tail[:, 0, :], mul))
                link(dve.tensor_scalar(SQ1[:, d, :], SQ1[:, d, :], mod[:, 32 + d:33 + d], mod[:, 24 + d:25 + d], mul, add))
            dve.sem_inc(sem("h2_value"), 1)
            dve.wait_ge(sem("h2_hi"), 1)
            dve.tensor_tensor(hlo[:], SQ1, hhi[:].bitcast(F32), sub).then_inc(sem("h2_split"), 1)

            for j in range(NF):
                cur = None
                for f, buf in ((j, CV), (NF + j, CG)):
                    bk, free = tile()
                    o = buf[:, j % 2, :]
                    if j >= 2 and f == j:
                        dve.wait_ge(sem("act_hi"), j - 1)
                    link(dve.tensor_scalar(o, bk[:], convv[:, 1, f:f + 1], convv[:, 1, 44 + f:45 + f], mul, add))
                    link(dve.scalar_tensor_tensor(o[:, 1:T], bk[:, 0:T - 1], convv[:, 0, 44 + f:45 + f], o[:, 1:T], mul, add))
                    link(dve.scalar_tensor_tensor(o[:, 2:T], bk[:, 0:T - 2], convv[:, 0, f:f + 1], o[:, 2:T], mul, add))
                    dve.sem_inc(free, 1)
                dve.sem_inc(sem("conv_gate"), 1)
                dve.wait_ge(sem("gate_sig"), j + 1)
                cv, cg = CV[:, j % 2, :], CG[:, j % 2, :]
                link(dve.tensor_tensor(cg, cg, tail[:, 1, :], mul))
                link(dve.tensor_tensor(cv, cv, cg, mul))
                dve.sem_inc(sem("act_value"), 1)
                dve.wait_ge(sem("act_hi"), j + 1)
                dve.tensor_tensor(actlo[:, j, :], cv, acthi[:, j, :].bitcast(F32), sub).then_inc(sem("act_split"), 1)
            for d in range(KD):
                bk, free = tile()
                link(dve.scalar_tensor_tensor(X1[:, d, :], bk[:], mod[:, 40 + d:41 + d], X1[:, d, :], mul, add))
                dve.sem_inc(free, 1)
                dve.sem_inc(sem("x2_tile"), 1)
            dve.wait_ge(sem("x2_rooted"), 1)
            link(dve.reciprocal(tail[:, 0, :], tail[:, 0, :]))
            for d in range(KD):
                q = dve.scalar_tensor_tensor(SQF[:, d, :], X1[:, d, :], col(V_FIN + d), tail[:, 0, :], mul, mul)
            q.then_inc(sem("x2_normed"), 1)
            for t in range(4):
                for half in range(2):
                    i = 2 * t + half
                    dve.wait_ge(sem("rows_turned"), i + 1)
                    dve.tensor_copy(RESULT(t)[:, T * half:T * half + T], ps[2 + i % 2][:]).then_inc(sem("rows_ready"), 1)


_INS = ["x", "c", "positions", "ada_w", "ada_b", "w_in", "rwkv_mu", "rwkv_w0", "rwkv_w2", "rwkv_a0", "rwkv_a2", "rwkv_g2",
        "rwkv_k_k", "rwkv_k_a", "rwkv_r_k", "rwkv_ln_w", "rwkv_ln_b", "hgrn_lb", "hgrn_norm_w", "mla_q_norm_w", "mla_w_uq",
        "mla_kv_norm_w", "mla_w_ukv", "branch_proj_a", "branch_proj_b", "branch_proj_c", "w_out", "ffn_w_up",
        "ffn_conv_w", "ffn_conv_b", "ffn_w_down", "final_norm_w"]
_FLAT = {"c", "ada_b", "rwkv_mu", "rwkv_w0", "rwkv_a0", "rwkv_k_k", "rwkv_k_a", "rwkv_r_k", "rwkv_ln_w", "rwkv_ln_b",
         "hgrn_lb", "hgrn_norm_w", "mla_q_norm_w", "mla_kv_norm_w", "ffn_conv_w", "ffn_conv_b", "final_norm_w"}


def kernel(**inputs):
    import concourse.bacc as bacc
    from concourse.bass_utils import run_bass_kernel_spmd

    nc = bacc.Bacc("TRN2", target_bir_lowering=False, num_devices=1, dynamic_dma_scratch_size=1024)
    arrays = {"const_f": CONST_F, "const_i": CONST_I.reshape(P, 7, CH).reshape(P, 7 * CH)}
    for name in _INS:
        v = np.ascontiguousarray(inputs[name])
        arrays[name] = v.reshape(-1) if name in _FLAT else v
    feed, aps = {}, {}
    for name, v in arrays.items():
        feed["in_" + name] = np.ascontiguousarray(v)
        aps[name] = nc.dram_tensor("in_" + name, v.shape, mybir.dt.from_np(v.dtype), kind="ExternalInput").ap()
    out = nc.dram_tensor("out_y", (1, T, D), F32, kind="ExternalOutput").ap()
    trunk(nc, aps, out)
    r = run_bass_kernel_spmd(nc, [feed], core_ids=[0])
    return r.results[0]["out_y"]
```

```python
from contextlib import ExitStack

import numpy as np

import concourse.bass as bass
from concourse import mybir

F32 = mybir.dt.float32
F32R = mybir.dt.float32r
I32 = mybir.dt.int32
ALU = mybir.AluOpType
ACT = mybir.ActivationFunctionType
AX = mybir.AxisListType

P = 128
T = 512
D = 1024
KD = D // P
FF = 2816
NF = FF // P
RW_TILES = 4
CH = 64
PAIRS = T // P
CHUNKS = T // CH
HG = 4
ML = 8
NOPE, ROPE = 64, 32
QK = NOPE + ROPE
MLA_SCALE = QK ** -0.5
NORM_EPS, RWKV_EPS = 1e-6, 64e-5
RW_COL, HG_COL, ML_COL, GATE_COL = 0, 1792, 3840, 4256
E_HALF = float(np.exp(-0.5))
GROUP = 2048

V_ADA, V_MU, V_W0, V_A0, V_KK, V_KA, V_RK, V_LNW, V_LNB = 0, 48, 62, 66, 70, 74, 78, 82, 86
V_LB, V_HN, V_QN, V_KV, V_FIN, V_C = 90, 94, 95, 97, 98, 106
V_ROWS = 114


def make_constants():
    s = np.arange(P)[:, None]
    t = np.arange(P)[None, :]
    same = (s // CH) == (t // CH)
    strict = (same & (s < t)).astype(np.float32)
    incl = (same & (s <= t)).astype(np.float32)
    c = {"ident": np.eye(P, dtype=np.float32), "rw_mask": np.concatenate([strict, incl, strict, incl], 1)}
    c["pair_t"] = ((s // 2 == t // 2) & (s < t)).astype(np.float32)
    levels = []
    for n in (2, 4, 8, 16, 32):
        first = [x for x in range(P) if (x // n) % 2 == 0]
        levels.append(np.array([[float((tt // (2 * n) == x // (2 * n)) and (tt // n) % 2 == 1) for x in first]
                                for tt in range(P)], np.float32))
    c["level"] = np.concatenate(levels, 1)
    c["ones"] = np.ones((P, P), np.float32)
    c["heads"] = ((s // CH) == (t // CH)).astype(np.float32)
    c["eye64"] = (s % CH == np.arange(CH)[None, :]).astype(np.float32)
    c["causal"] = np.where(t <= s, 0.0, -1e30).astype(np.float32)
    inv = (10000.0 ** (-np.arange(0, ROPE, 2, dtype=np.float32) / ROPE)).astype(np.float32)
    c["freq"] = np.tile(inv, P // 16)[:, None].astype(np.float32)
    c["rsign"] = np.where(np.arange(P) % ROPE < ROPE // 2, -1.0, 1.0)[:, None].astype(np.float32)
    hg = []
    for n in (1, 2, 4, 8, 16, 32, 64):
        second = [x for x in range(P) if (x // n) % 2 == 1]
        hg.append(np.array([[int((ss // (2 * n) == x // (2 * n)) and (ss // n) % 2 == 0) for x in second]
                            for ss in range(P)], np.int32))
    at, off = {}, 0
    for k, v in c.items():
        at[k] = (off, off + v.shape[1])
        off += v.shape[1]
    return np.concatenate(list(c.values()), 1), at, np.concatenate(hg, 1)


CONST_F, CONST_AT, CONST_I = make_constants()


def weight_groups(a):
    g = []
    kt = lambda w: w.rearrange("(k p) n -> p k n", p=P)
    ada, win = kt(a["ada_w"][0]), kt(a["w_in"][0])
    up, down = kt(a["ffn_w_up"][0]), kt(a["ffn_w_down"][0])
    for j in range(8):
        g.append(("raw", [(ada[:, :, 256 * j:256 * (j + 1)], 0, 256)], KD, 256))
    for c0 in (1536, 512, 768, 0, 256, 1024, 1280):
        g.append(("split", [(win[:, :, c0:c0 + 256], 0, 256)], KD, 256))
    def ada_group(j):
        g.append(("raw", [(ada[:, :, 256 * j:256 * (j + 1)], 0, 256)], KD, 256))

    def hgrn_group(u):
        h, part = HG_GROUPS[u]
        c0 = HG_COL + 2 * HG * P * part
        g.append(("split", [(win[:, :, c0 + P * h:c0 + P * (h + 1)], 0, P),
                            (win[:, :, c0 + P * (HG + h):c0 + P * (HG + h + 1)], P, P)], KD, 256))

    for j in range(8, 24):
        if (j - 8) % 5 == 4:
            if j == 12:
                g.append(("split", [(win[:, :, ML_COL:ML_COL + 256], 0, 256)], KD, 256))
            else:
                hgrn_group((j - 8) // 5 - 1)
        ada_group(j)
    for u in range(2, 8):
        hgrn_group(u)
    c0 = ML_COL + 256
    g.append(("split", [(win[:, :, c0:c0 + 160], 0, 160), (win[:, :, c0 + 144:c0 + 160], 160, 16),
                        (win[:, :, c0 + 128:c0 + 144], 176, 16)], KD, 192))
    proj = [kt(a[f"branch_proj_{b}"][0]) for b in "abc"]
    for half, b in MIX_BLOCKS:
        for q in range(2):
            c0 = GATE_COL + b * D + half * 512 + q * 256
            g.append(("split", [(win[:, :, c0:c0 + 256], 0, 256)], KD, 256))
        g.append(("split", [(proj[b][:, :, 512 * half:512 * (half + 1)], 0, 512)], 4, 512))
    wo = kt(a["w_out"][0])
    for q in range(4):
        g.append(("split", [(wo[:, :, 256 * q:256 * (q + 1)], 0, 256)], KD, 256))
    for j in range(NF):
        g.append(("split", [(up[:, :, P * j:P * (j + 1)], 0, P), (up[:, :, FF + P * j:FF + P * (j + 1)], P, P)], KD, 256))
    for q in range(4):
        for k0 in (0, 8, 16):
            nk = min(8, NF - k0)
            g.append(("split", [(down[:, k0:k0 + nk, 256 * q:256 * (q + 1)], 0, 256)], nk, 256))
    return g


G_ADA0, G_RW, G_ADA1, G_KR, G_MIX, G_OUT, G_UP, G_DOWN = 0, 8, 15, 40, 41, 59, 63, 85
MIX_BLOCKS = [(0, 0), (0, 1), (1, 0), (1, 1), (0, 2), (1, 2)]
MIX_TILE = 34
HG_GROUPS = [(0, 0), (0, 1), (1, 0), (2, 0), (1, 1), (3, 0), (2, 1), (3, 1)]
HG_TILE = 16
G_FILL = [19, 25, 31, 34]
G_HG = [25, 31, 34, 35, 36, 37, 38, 39]


def trunk(nc, a, out):
    groups = weight_groups(a)
    ctx = ExitStack()
    with ctx:
        def sb(name, shape, dt=F32, c=ctx):
            return c.enter_context(nc.sbuf_tensor(name, shape, dt))

        sems = {}

        def sem(name):
            if name not in sems:
                sems[name] = ctx.enter_context(nc.semaphore(name))
            return sems[name]

        wring = sb("wring", [P, 2, GROUP])
        whi = sb("whi", [P, 2, GROUP], F32R)
        wlo = sb("wlo", [P, 2, GROUP], F32R)
        hhi = sb("hhi", [P, KD, T], F32R)
        hlo = sb("hlo", [P, KD, T], F32R)
        const = sb("const", [P, CONST_F.shape[1]])
        consti = sb("consti", [P, 7, CH], I32)
        vec = sb("vec", [P, V_ROWS])
        convv = sb("convv", [P, 2, 88])
        mod = sb("mod", [P, 48])
        cond = sb("cond", [P, KD])
        small = sb("small", [P, 64])
        outs = sb("outs", [P, 12, T])
        PAD = sb("padded", [P, 4, T])
        CQ = sb("cq", [P, 2, T])[:]
        scope = ExitStack()
        arena = sb("arena", [P, 46, T], c=scope)
        scope.close()
        scope = ExitStack()
        ohi = sb("ohi", [P, 4, T], F32R, c=scope)
        olo = sb("olo", [P, 4, T], F32R, c=scope)
        mix = sb("mix", [P, 38, T], c=scope)
        scope.close()
        scope = ExitStack()
        tail = sb("tail", [P, 2, T], c=scope)
        acthi = sb("acthi", [P, NF, T], F32R, c=scope)
        actlo = sb("actlo", [P, NF, T], F32R, c=scope)
        scope.close()
        ps = [ctx.enter_context(nc.psum_tensor(f"bank{b}", [P, T], F32))[:] for b in range(8)]

        def cst(name):
            lo, hi = CONST_AT[name]
            return const[:, lo:hi]

        ident = cst("ident")
        ones = cst("ones")
        heads = cst("heads")

        def col(row, n=1):
            return vec[:, row:row + n]

        EPS, REPS = small[:, 0:1], small[:, 1:2]
        LBV, OMLB = small[:, 4:8], small[:, 8:12]
        ONE_MU = small[:, 16:30]

        xtok = arena[:, 0:8, :].rearrange("p a t -> p (a t)").rearrange("p (a d) -> p a d", a=4)
        xT = arena[:, 8:16, :]
        sqT = arena[:, 16:24, :]
        rstd = arena[:, 24, :]
        vrows = arena[:, 25, 0:P]
        crow = arena[:, 26, 0:2 * P].rearrange("p (a b) -> p a b", a=2)
        R, K, V, DEC, AA, KK = (arena[:, 4 * i:4 * i + 4, :] for i in range(6))
        LORA = arena[:, 24, :]
        LW = arena[:, 25, :]
        GL = arena[:, 26, :]
        GW = arena[:, 27, :]
        ABR = arena[:, 28:36, :]
        TM = arena[:, 36:38, :].rearrange("p a t -> p (a t)").rearrange("p (i t) -> p i t", i=8)
        TT = arena[:, 38:40, :].rearrange("p a t -> p (a t)").rearrange("p (i t) -> p i t", i=8)
        YH = arena[:, 40, :]
        AV = arena[:, 41:43, :].rearrange("p a t -> p (a t)").rearrange("p (i t) -> p i t", i=8)
        WY = arena[:, 43:45, :].rearrange("p a t -> p (a t)").rearrange("p (i t) -> p i t", i=8)
        VTK = arena[:, 45, :].rearrange("p (q f) -> p q f", q=PAIRS)
        MT, NN = arena[:, 41, :], arena[:, 42, :]
        PP, PINV = outs[:, 4, :], outs[:, 5, :]
        AR = [v.rearrange("p a t -> p (a t)").rearrange("p (q w t) -> p q w t", q=PAIRS, w=2)
              for v in (outs[:, 6:8, :], arena[:, 24:26, :])]
        YV, YSQ, QT, BONUS = KK, AA, DEC, R
        LAST = small[:, 32:40]
        BH, KH, SCR = outs[:, 8, :], outs[:, 9, :], outs[:, 10, :]
        KTOK = [outs[:, i, :].rearrange("p (q f) -> p q f", q=PAIRS) for i in (10, 11)]
        HQ, HF, HK, HV, HO, SUF = (arena[:, 4 * i:4 * i + 4, :] for i in range(6))
        QC = [arena[:, i, :].rearrange("p (h t) -> p h t", h=2) for i in (24, 25)]
        KN = [arena[:, 26:28, :], arena[:, 28:30, :]]
        AT = arena[:, 30:34, :].rearrange("p h (c t) -> p h c t", c=4)
        HVT = arena[:, 34:38, :].rearrange("p h (c t) -> p h c t", c=4)
        HKT = arena[:, 38:42, :].rearrange("p h (c t) -> p h c t", c=4)
        HS = arena[:, 42:46, :].rearrange("p h (c t) -> p h c t", c=4)
        HSCR = PAD[:, 2:4, :]
        CKV, KR, KRR = arena[:, 0, :], arena[:, 1, :], arena[:, 4, :]
        MSQ, MSK, MRS = arena[:, 12:14, :], arena[:, 12, :], arena[:, 16:18, :]
        WUQ, WUK, WUV = outs[:, 8:10, :], outs[:, 10, :], outs[:, 11, :]
        WROPE, WROT = (arena[:, i, :].rearrange("p (k n) -> p k n", k=2) for i in (5, 13))
        SIN, COS, ANG, RED = (PAD[:, i, :] for i in range(4))
        ROT = arena[:, 6:8, :]
        QH, KHD, VM = arena[:, 20:28, :], arena[:, 28:36, :], arena[:, 36:40, :]
        PRB, PT = arena[:, 40:42, :], arena[:, 42:46, :]
        GATE = mix[:, 0:4, :]
        YT = mix[:, 4:12, :]
        XT2 = mix[:, 20:28, :]
        TMP = PAD
        XTOK2 = mix[:, 12:20, :].rearrange("p a t -> p (a t)").rearrange("p (a d) -> p a d", a=4)
        X1 = outs[:, 0:8, :]
        SQ1 = mix[:, 28:36, :]
        CV = outs[:, 8:10, :]
        CG = outs[:, 10:12, :]

        def mm3(e, o, g, k, m0, m1, rhi, rlo, first, last, ncols):
            hi = whi[:, g % 2, :][:, k * ncols + m0:k * ncols + m1]
            lo = wlo[:, g % 2, :][:, k * ncols + m0:k * ncols + m1]
            e.matmul(o, hi, rhi, start=first, stop=False)
            e.matmul(o, hi, rlo, start=False, stop=False)
            return e.matmul(o, lo, rhi, start=False, stop=last)

        split_no, raw_no = {}, {}
        for i, gr in enumerate(groups):
            n = split_no if gr[0] == "split" else raw_no
            n[i] = len(n)

        EARLY = [v.rearrange("p a t -> p (a t)") for v in
                 [outs[:, 4 * i:4 * i + 4, :] for i in range(3)] + [arena[:, 28 + 4 * i:32 + 4 * i, :] for i in range(4)]]
        def ada_slot(g):
            return EARLY[g] if g < len(EARLY) else wring[:, g % 2, :]

        def ada_landed(g):
            return (sem(f"ada_in{g}"), 16) if g < len(EARLY) else (sem(f"w_landed{g % 2}"), landings[g])

        POOL_ADA = [g for g in raw_no if g in (1, 4) or g >= G_ADA1]
        DVE_ADA = [g for g in raw_no if g not in POOL_ADA]
        landings = {}
        count = [0, 0]
        for g, gr in enumerate(groups):
            count[g % 2] += 16 * len(gr[1]) * (g >= len(EARLY))
            landings[g] = count[g % 2]

        RESULT = [v.rearrange("p a t -> p (a t)").rearrange("p (b n) -> p b n", b=2) for v in (PAD[:], outs[:, 8:12, :])]
        SQUARE, SQUARES, ROOT = CQ, tail[:, 0, :], tail[:, 1, :]
        RSTD = small[:, 44:48]

        def FREE_AT(n):
            return (n + 1) // 2, n // 2

        used, tiles = [], 0
        for g in split_no:
            if g < G_DOWN:
                tiles += 4 if G_MIX <= g < G_OUT and (g - G_MIX) % 3 == 2 else 2
                used.append((sem("tile_ready"), tiles))
            elif (g - G_DOWN) % 3 < 2:
                used.append((sem("down_part"), 2 * ((g - G_DOWN) // 3) + (g - G_DOWN) % 3 + 1))
            else:
                tiles += 2
                used.append((sem("tile_ready"), tiles))

        before, last_in = {}, {}
        for g, n in split_no.items():
            before[n] = last_in.get(g % 2)
            last_in[g % 2] = n

        block = ctx.enter_context(nc.Block())

        @block.sync
        def _(sp):
            rows = [("ada_b", V_ADA, 48), ("rwkv_mu", V_MU, 14), ("rwkv_w0", V_W0, 4), ("rwkv_a0", V_A0, 4),
                    ("rwkv_k_k", V_KK, 4), ("rwkv_k_a", V_KA, 4), ("rwkv_r_k", V_RK, 4), ("rwkv_ln_w", V_LNW, 4),
                    ("rwkv_ln_b", V_LNB, 4), ("hgrn_lb", V_LB, 4), ("hgrn_norm_w", V_HN, 1),
                    ("mla_q_norm_w", V_QN, 2), ("mla_kv_norm_w", V_KV, 1), ("final_norm_w", V_FIN, 8), ("c", V_C, 8)]
            for name, r0, n in rows:
                sp.dma_start(vrows[r0:r0 + n, :], a[name].rearrange("(r p) -> r p", p=P)).then_inc(sem("ld_vec"), 16)
            cw = a["ffn_conv_w"].rearrange("(r p) -> r p", p=P)
            sp.dma_start(crow[0:88, 0, :], cw[0:88, :]).then_inc(sem("ld_vec"), 16)
            sp.dma_start(crow[0:44, 1, :], cw[88:132, :]).then_inc(sem("ld_vec"), 16)
            sp.dma_start(crow[44:88, 1, :], a["ffn_conv_b"].rearrange("(r p) -> r p", p=P)).then_inc(sem("ld_vec"), 16)
            sp.dma_start(consti[:].rearrange("p a b -> p (a b)"), a["const_i"]).then_inc(sem("ld_const"), 16)

            def load(g):
                kind, parts, nk, n = groups[g]
                if g < len(EARLY):
                    sp.dma_start(EARLY[g].rearrange("p (k n) -> p k n", k=nk), parts[0][0]).then_inc(sem(f"ada_in{g}"), 16)
                    return
                if g - 2 < len(EARLY):
                    pass
                elif g - 2 in split_no:
                    sp.wait_ge(sem("w_lo"), split_no[g - 2] + 1)
                else:
                    sp.wait_ge(sem("ada_used"), raw_no[g - 2] + 1)
                dst = wring[:, g % 2, 0:nk * n].rearrange("p (k n) -> p k n", k=nk)
                for src, off, w in parts:
                    sp.dma_start(dst[:, :, off:off + w], src).then_inc(sem(f"w_landed{g % 2}"), 16)

            for g in range(len(groups)):
                load(g)
                if g == G_RW + 1:
                    sp.wait_ge(sem("vec_turned"), 1)
                    sp.wait_ge(sem("h_split"), KD)
                    sp.dma_start(LW[0:64, :], a["rwkv_w2"][0]).then_inc(sem("ld_lora"), 16)
                    sp.dma_start(LW[64:128, :], a["rwkv_a2"][0]).then_inc(sem("ld_lora"), 16)
                    sp.dma_start(GW, a["rwkv_g2"][0]).then_inc(sem("ld_lora"), 16)
                uq = a["mla_w_uq"][0].rearrange("(k p) (h n) -> p k h n", p=P, n=QK)
                ukv = a["mla_w_ukv"][0].rearrange("p (h n) -> p h n", n=P)
                by_head = lambda v, n: v.rearrange("p (h n) -> p h n", n=n)
                if g == G_FILL[3]:
                    sp.wait_ge(sem("rw_tildes"), RW_TILES)
                    sp.wait_ge(sem("abr_done"), 8 * RW_TILES)
                    sp.dma_start(ANG.bitcast(I32), a["positions"][0].partition_broadcast(P)).then_inc(sem("ld_pos"), 16)
                if g == G_FILL[3] + 1:
                    sp.wait_ge(sem("mn_done"), RW_TILES)
                    for k in range(2):
                        sp.dma_start(by_head(WUQ[:, k, :], NOPE), uq[:, k, :, 0:NOPE]).then_inc(sem("ld_mla"), 16)
                    sp.dma_start(by_head(WUK, NOPE), ukv[:, :, 0:NOPE]).then_inc(sem("ld_mla"), 16)
                    sp.dma_start(by_head(WUV, NOPE), ukv[:, :, NOPE:P]).then_inc(sem("ld_mla"), 16)
                if g == G_KR:
                    sp.wait_ge(sem("hg_out"), 1)
                    for k in range(2):
                        sp.dma_start(by_head(WROPE[:, k, :], ROPE), uq[:, k, :, NOPE:QK]).then_inc(sem("ld_rope"), 16)
                if g == G_MIX + 13:
                    sp.wait_ge(sem("oc_done"), ML)
                    sp.dma_start(XTOK2, a["x"][0].rearrange("(a p) d -> p a d", p=P)).then_inc(sem("ld_x2"), 16)
            for q in range(4):
                sp.wait_ge(sem(f"rows_scaled{q // 2}"), q % 2 + 1)
                sp.dma_start(out[0, q * P:(q + 1) * P, :], RESULT[q // 2][:, q % 2, :]).then_inc(sem("stored"), 16)
            sp.wait_ge(sem("stored"), 64)

        @block.gpsimd
        def _(pool):
            pool_step = [0]

            def pool_link(ins):
                pool_step[0] += 1
                ins.then_inc(sem("pool_chain"), 1)
                pool.wait_ge(sem("pool_chain"), pool_step[0])

            def weigh(g):
                w = ada_slot(g)
                pool.wait_ge(*ada_landed(g))
                if g == POOL_ADA[0]:
                    pool.wait_ge(sem("cond_ready"), 1)
                by_k = w.rearrange("p (k n) -> p k n", k=KD)
                pool_link(pool.tensor_tensor(by_k, by_k, cond[:].unsqueeze(2).broadcast_to([P, KD, 256]), ALU.mult))
                for half in (1024, 512, 256):
                    pool_link(pool.tensor_tensor(w[:, 0:half], w[:, 0:half], w[:, half:2 * half], ALU.add))
                pool.sem_inc(sem("ada_pool"), 1)

            pool.memset(PAD[:], 0.0).then_inc(sem("pad_zero"), 1)
            for g in range(len(groups)):
                if g in POOL_ADA:
                    weigh(g)
                if g not in split_no:
                    continue
                n = split_no[g]
                w = groups[g][2] * groups[g][3]
                s = g % 2
                pool.wait_ge(sem("w_hi"), n + 1)
                if before[n] is not None:
                    pool.wait_ge(*used[before[n]])
                pool.tensor_tensor(wlo[:, s, 0:w], wring[:, s, 0:w], whi[:, s, 0:w].bitcast(F32),
                                   ALU.subtract).then_inc(sem("w_lo"), 1)

        @block.tensor
        def _(pe):
            tile_no = [0]

            def bank():
                i = tile_no[0]
                tile_no[0] += 1
                if i >= 2:
                    pe.wait_ge(sem(f"bank_free{i % 2}"), i // 2)
                return ps[i % 2]

            def project(g, cuts, rhi, rlo, ready=None):
                n = split_no[g]
                pe.wait_ge(sem("w_lo"), n + 1)
                nk, ncols = groups[g][2], groups[g][3]
                for m0, m1 in cuts:
                    o = bank()[0:m1 - m0, :]
                    for k in range(nk):
                        if ready and m0 == 0:
                            pe.wait_ge(sem(ready), k + 1)
                        q = mm3(pe, o, g, k, m0, m1, rhi[:, k, :], rlo[:, k, :], k == 0, k == nk - 1, ncols)
                    q.then_inc(sem("tile_ready"), 1)

            PAIR = [(0, P), (P, 2 * P)]

            def part(g, x0, x1, cuts=PAIR):
                for x in range(x0, x1):
                    m, k = x // KD, x % KD
                    m0, m1 = cuts[m]
                    if x == 0:
                        pe.wait_ge(sem("w_lo"), split_no[g] + 1)
                    if k == 0:
                        fill_bank[0] = bank()
                    q = mm3(pe, fill_bank[0][0:m1 - m0, :], g, k, m0, m1, hhi[:, k, :], hlo[:, k, :], k == 0, k == KD - 1,
                            groups[g][3])
                    if k == KD - 1:
                        q.then_inc(sem("tile_ready"), 1)

            def fill(j, x0, x1):
                g = G_FILL[j]
                if x0 == 0:
                    pe.wait_ge(sem("rw_out"), j)
                if x0 == KD:
                    pe.wait_ge(sem("mod_read"), j + 2)
                part(g, x0, x1)

            fill_bank = [None]

            pe.wait_ge(sem("ld_const"), 32)
            pe.wait_ge(sem("ld_x"), 16)
            for d in range(KD):
                if d >= 4:
                    pe.wait_ge(sem("xt_copied"), d - 3)
                for t in range(4):
                    q = pe.transpose(ps[2 + d % 4][:, P * t:P * (t + 1)], xtok[:, t, P * d:P * (d + 1)], ident)
                q.then_inc(sem("xt_turned"), 1)
            pe.wait_ge(sem("ld_vec"), 18 * 16)
            pe.transpose(ps[6][:, 0:V_ROWS], vrows[0:V_ROWS, :], ident[0:V_ROWS, 0:V_ROWS])
            pe.transpose(ps[6][:, 128:216], crow[0:88, 0, :], ident[0:88, 0:88])
            pe.transpose(ps[6][:, 256:344], crow[0:88, 1, :], ident[0:88, 0:88]).then_inc(sem("vec_in_psum"), 1)

            def sum_over_features(src, nk, o):
                for k in range(nk):
                    q = pe.matmul(o, ones, src[:, k, :], start=k == 0, stop=k == nk - 1)
                return q

            pe.wait_ge(sem("x_squared"), 1)
            pe.wait_ge(sem("vec_turned"), 1)
            sum_over_features(sqT, KD, ps[6]).then_inc(sem("x_summed"), 1)

            def ada(g, o):
                if g in POOL_ADA:
                    pe.wait_ge(sem("ada_pool"), POOL_ADA.index(g) + 1)
                else:
                    pe.wait_ge(sem("ada_dve"), DVE_ADA.index(g) + 1)
                for m in range(2):
                    c = 2 * raw_no[g] + m
                    q = pe.matmul(o[:, c:c + 1], ada_slot(g)[:, P * m:P * (m + 1)], ones[:, 0:1], start=True, stop=True)
                q.then_inc(sem("ada_used"), 1)

            for g in range(G_ADA0, G_RW):
                ada(g, ps[7])
            for g in range(G_RW, G_RW + 3):
                project(g, PAIR, hhi, hlo, "h_split" if g == G_RW else None)

            pe.wait_ge(sem("ld_lora"), 48)
            pe.wait_ge(sem("lora_in"), 2)
            for j in range(RW_TILES):
                if j >= 2:
                    pe.wait_ge(sem("lora_read"), 2 * (j - 1))
                pe.matmul(ps[2 + j % 2], LW[0:64, P * j:P * (j + 1)], LORA[0:64, :], start=True, stop=True
                          ).then_inc(sem("lora_out"), 1)
                pe.matmul(ps[4 + j % 2], LW[64:128, P * j:P * (j + 1)], LORA[64:128, :], start=True, stop=True
                          ).then_inc(sem("lora_out"), 1)
            project(G_RW + 3, PAIR, hhi, hlo)
            for j in range(RW_TILES):
                pe.wait_ge(sem("kk_squared"), j + 1)
                if j >= 2:
                    pe.wait_ge(sem("kk_norm_read"), j - 1)
                pe.matmul(ps[6 + j % 2], heads, outs[:, j, :], start=True, stop=True).then_inc(sem("kk_summed"), 1)
            for g in range(G_RW + 4, G_RW + 7):
                project(g, PAIR, hhi, hlo)

            ada_next = iter([g for g in raw_no if g >= G_ADA1])

            def fold_ada(j, i):
                if 5 * j + i >= 16:
                    return
                if i == 0 and j == 0:
                    pe.wait_ge(sem("rw_mixed"), 14)
                if i == 4:
                    pe.wait_ge(sem("bank_free1"), FREE_AT(16 + 2 * j)[1])
                ada(next(ada_next), ps[1])

            def head_mean(j, bank_):
                pe.wait_ge(sem("y_in"), j + 1)
                if j < 3:
                    pe.wait_ge(sem("bank_free0"), FREE_AT(16 + 2 * j)[0])
                pe.matmul(bank_, heads, YV[:, j, :], start=True, stop=True).then_inc(sem("stat"), 1)

            def bonus_sum(j):
                pe.wait_ge(sem("rk_ready"), j + 1)
                pe.matmul(ps[6], heads, BONUS[:, j, :], start=True, stop=True).then_inc(sem("bonus_sum"), 1)

            def head_variance(j, bank_):
                pe.wait_ge(sem("y_centred"), j + 1)
                pe.matmul(bank_, heads, YSQ[:, j, :], start=True, stop=True).then_inc(sem("stat"), 1)

            def output_gate(j, bank_):
                pe.wait_ge(sem("y_rooted"), j + 1)
                pe.matmul(bank_, GW[:, P * j:P * (j + 1)], GL, start=True, stop=True).then_inc(sem("g_out"), 1)

            for j in range(RW_TILES):
                ar = AR[j % 2]
                pe.wait_ge(sem("rw_hats"), j + 1)
                if j == 0:
                    pe.wait_ge(sem("kk_norm_read"), RW_TILES)
                for i in range(8):
                    p, h = i // 2, i % 2
                    b = ps[2 + i % 4]
                    if i >= 4:
                        pe.wait_ge(sem("abr_copied"), 8 * j + i - 3)
                    if j and i == 2:
                        head_mean(j - 1, ps[0])
                    if j and i == 3:
                        bonus_sum(j - 1)
                    if j and i == 6:
                        head_variance(j - 1, ps[0])
                    if i == 4:
                        fold_ada(j, 0)
                    rhs = ar[:, p, :, :].rearrange("p w t -> p (w t)")
                    pe.matmul(b[:, 0:256], PAD[:, h, P * p:P * (p + 1)], rhs, start=True, stop=True)
                    pe.matmul(b[:, 256:512], PAD[:, 2 + h, P * p:P * (p + 1)], rhs, start=True, stop=True
                              ).then_inc(sem("abr_done"), 1)
                def token_major(n, src):
                    if n == 0 and j:
                        pe.wait_ge(sem("bonus_ready"), j)
                    if n >= 2:
                        pe.wait_ge(sem("rw_tildes"), j + 1)
                        pe.wait_ge(sem("tok_copied"), 4 * j + n - 1)
                    for p in range(PAIRS):
                        piece = ar[:, p, 0, :] if src is None else src[:, P * p:P * (p + 1)]
                        q = pe.transpose(ps[6 + n % 2][:, P * p:P * (p + 1)], piece, ident)
                    q.then_inc(sem("tok_turned"), 1)

                token_major(0, None)
                token_major(1, V[:, j, :])
                if j:
                    output_gate(j - 1, ps[0])
                fold_ada(j, 1)

                def turn(l):
                    for half in range(2):
                        pe.wait_ge(sem("t_added"), 2 * (6 * j + l) + half + 1)
                        for i in range(4):
                            q = pe.transpose(ps[2 + half][:, P * i:P * (i + 1)], (TT if l == 0 else TM)[:, 4 * half + i, :], ident)
                        q.then_inc(sem("t_turned"), 1)

                turn(0)
                for l, n in enumerate((2, 4, 8, 16, 32)):
                    if l in (1, 2):
                        fold_ada(j, l + 1)
                    for half in range(2):
                        pe.wait_ge(sem("t_copied"), 2 * (6 * j + l) + half + 1)
                        for i in range(4):
                            x = 4 * half + i
                            first = TM[:, x, :].rearrange("p (b w n) -> p b w n", w=2, n=n)[:, :, 0, :]
                            q = pe.matmul(ps[4 + half][:, 64 * i:64 * (i + 1)], ABR[:, x, 0:P], first, start=True, stop=True)
                        q.then_inc(sem("y_done"), 1)
                    for half in range(2):
                        pe.wait_ge(sem("y_masked"), 2 * (5 * j + l) + half + 1)
                        for i in range(4):
                            x = 4 * half + i
                            q = pe.matmul(ps[4 + half][:, 256 + 64 * i:256 + 64 * (i + 1)], TT[:, x, :], YH[:, 64 * x:64 * (x + 1)],
                                          start=True, stop=True)
                        q.then_inc(sem("ty_done"), 1)
                    turn(l + 1)
                    if l == 1:
                        token_major(2, BH)
                        token_major(3, KH)
                pe.wait_ge(sem("tok_copied"), 4 * j + 3)
                for i in range(8):
                    p, h = i // 2, i % 2
                    q = pe.matmul(ps[6][:, 64 * i:64 * (i + 1)], ABR[:, i, 256:384], VTK[:, p, 64 * h:64 * (h + 1)],
                                  start=True, stop=True)
                q.then_inc(sem("akv_done"), 1)
                pe.wait_ge(sem("t_copied"), 2 * (6 * j + 6))
                pe.wait_ge(sem("akv_copied"), j + 1)
                for half in range(2):
                    for i in range(4):
                        x = 4 * half + i
                        q = pe.matmul(ps[2 + half][:, P * i:P * (i + 1)], TT[:, x, :], AV[:, x, :], start=True, stop=True)
                    q.then_inc(sem("wy_done"), 1)
                pe.wait_ge(sem("tok_copied"), 4 * j + 4)
                pe.wait_ge(sem("wy_copied"), 2 * j + 2)
                for h in range(2):
                    for p in range(PAIRS):
                        for c in range(2):
                            x, rows, b = 2 * p + h, slice(64 * c, 64 * c + 64), ps[4 + c]
                            hs = slice(64 * h, 64 * h + 64)
                            w, y2 = WY[rows, x, 0:64], WY[rows, x, 64:128]
                            pe.matmul(b[hs, 64 * p:64 * p + 64], w, KTOK[0][rows, p, hs], start=True, stop=True)
                            o = b[hs, 256 + 64 * p:320 + 64 * p]
                            pe.matmul(o, KTOK[0][rows, p, hs], y2, start=True, stop=False)
                            q = pe.matmul(o, KTOK[1][rows, p, hs], VTK[rows, p, hs], start=False, stop=True)
                q.then_inc(sem("mn_done"), 1)
                for p in range(PAIRS):
                    for h in range(2):
                        x = 2 * p + h
                        q = pe.matmul(ps[6][64 * h:64 * h + 64, P * p:P * (p + 1)], WY[:, x, 0:64], ABR[:, x, 128:256],
                                      start=True, stop=True)
                q.then_inc(sem("q_done"), 1)
                fill(j, 0, 4)
                for c in range(1, CHUNKS - 1):
                    pe.wait_ge(sem("state_ready"), 8 * j + c + 1)
                    for h in range(2):
                        hs = slice(64 * h, 64 * h + 64)
                        q = pe.matmul(ps[2 + h][hs, 0:64], MT[hs, 64 * c:64 * c + 64], YH[hs, 64 * c:64 * c + 64],
                                      start=True, stop=True)
                    q.then_inc(sem("state_step"), 1)
                    fill(j, 2 * c + 2, 2 * c + 4)
                pe.wait_ge(sem("state_ready"), 8 * j + 8)
                pe.wait_ge(sem("q_ready"), j + 1)
                for p in range(PAIRS):
                    for h in range(2):
                        x, hs = 2 * p + h, slice(64 * h, 64 * h + 64)
                        b = ps[4 + h]
                        pe.matmul(b[hs, P * p:P * (p + 1)], WY[:, x, 64:128], ABR[:, x, 128:256], start=True, stop=False)
                        q = pe.matmul(b[hs, P * p:P * (p + 1)], VTK[:, p, hs], ABR[:, x, 384:512], start=False, stop=True)
                        for c in range(2):
                            o = b[hs, P * p + 64 * c:P * p + 64 * c + 64]
                            ch = 2 * p + c
                            q = pe.matmul(o, YH[hs, 64 * ch:64 * ch + 64], QT[hs, j, 64 * ch:64 * ch + 64],
                                          start=False, stop=True, skip_group_check=True)
                q.then_inc(sem("y_out"), 1)
                fold_ada(j, 4)
            head_mean(3, ps[2])
            bonus_sum(3)

            def hgrn_products(x0, x1):
                for x in range(x0, x1):
                    part(G_HG[3 + x // 16], x % 16, x % 16 + 1)

            hgrn_products(0, 8)
            head_variance(3, ps[3])
            hgrn_products(8, 16)
            output_gate(3, ps[7])

            def level(p, l):
                pe.wait_ge(sem("hg_factors"), 8 * p + l + 1)
                if l == 0:
                    if p:
                        pe.wait_ge(sem("hg_masked"), 8)
                    for h in range(2):
                        for c in range(4):
                            t = slice(P * c, P * (c + 1))
                            q = pe.matmul(ps[4 + 2 * p + h][:, t], HK[:, 2 * p + h, t], HQ[:, 2 * p + h, t], start=True, stop=True)
                else:
                    if p or l > 2:
                        pe.wait_ge(sem("hg_masked"), 8 * p + max(l - 1, 1))
                    for i in range(8):
                        h, c = i // 4, i % 4
                        q = pe.matmul(ps[7 - l % 2][:, 64 * i:64 * i + 64], KN[l % 2][:, h, P * c:P * (c + 1)],
                                      QC[l % 2][:, h, 64 * c:64 * (c + 1)], start=True, stop=True)
                q.then_inc(sem("hg_level"), 1)

            def hgrn_turn(p):
                pe.wait_ge(sem("hg_tail"), p + 1)
                pe.wait_ge(sem("bank_free0"), FREE_AT(HG_TILE + 2 * HG_GROUPS.index((2 * p + 1, 1)) + 1)[0])
                if p:
                    pe.wait_ge(sem("hg_rooted"), 2)
                for n in range(4):
                    src = (HV if n < 2 else HK)[:, 2 * p + n % 2, :]
                    if n >= 2:
                        pe.wait_ge(sem("hg_tok_copied"), 4 * p + n - 1)
                    for c in range(4):
                        q = pe.transpose(ps[2 + n % 2][:, P * c:P * (c + 1)], src[:, P * c:P * (c + 1)], ident)
                    q.then_inc(sem("hg_tok_turned"), 1)

            def hgrn_added(p):
                pe.wait_ge(sem("hg_tok_copied"), 4 * p + 4)
                for h in (2 * p, 2 * p + 1):
                    for c in range(3):
                        q = pe.matmul(ps[2 + h % 2][:, P * c:P * (c + 1)], HKT[:, h, c, :], HVT[:, h, c, :], start=True, stop=True)
                    q.then_inc(sem("hg_added"), 1)

            def hgrn_out(p):
                pe.wait_ge(sem("hg_masked"), 8 * p + 8)
                if p:
                    pe.wait_ge(sem("hg_out"), 1)
                for h in (2 * p, 2 * p + 1):
                    pe.wait_ge(sem("hg_state"), 3 * (h + 1))
                    for c in range(4):
                        o = ps[4 + h % 2][:, P * c:P * (c + 1)]
                        q = pe.matmul(o, HVT[:, h, c, :], AT[:, h, c, :], start=True, stop=c == 0)
                        if c:
                            q = pe.matmul(o, HS[:, h, c, :], HQ[:, h, P * c:P * (c + 1)], start=False, stop=True)
                    q.then_inc(sem("hg_o"), 1)

            def hgrn_squares(p):
                for h in (2 * p, 2 * p + 1):
                    pe.wait_ge(sem("hg_squared"), h + 1)
                    pe.matmul(ps[2 + h % 2], ones, HSCR[:, h % 2, :], start=True, stop=True).then_inc(sem("hg_summed"), 1)

            for l in range(8):
                level(0, l)
                hgrn_products(16 + 4 * l, 20 + 4 * l)
            hgrn_turn(0)
            hgrn_products(48, 52)
            hgrn_added(0)
            hgrn_products(52, 56)
            hgrn_out(0)
            hgrn_products(56, 60)
            hgrn_squares(0)
            def mix_products(x0, x1):
                for x in range(x0, x1):
                    g, block, y = G_MIX + x // 16, x // 48, x % 48
                    if x % 16 == 0:
                        pe.wait_ge(sem("w_lo"), split_no[g] + 1)
                    if y == 32:
                        pe.wait_ge(sem("o_split"), block + 1)
                    nk = KD if y < 32 else 4
                    m, k = x % 16 // nk, x % nk
                    if k == 0:
                        mix_bank[0] = bank()
                    if y < 32:
                        q = mm3(pe, mix_bank[0], g, k, P * m, P * (m + 1), hhi[:, k, :], hlo[:, k, :], k == 0, k == 7, 256)
                    else:
                        q = mm3(pe, mix_bank[0], g, k, P * m, P * (m + 1), ohi[:, k, :], olo[:, k, :], k == 0, k == 3, 512)
                    if k == nk - 1:
                        q.then_inc(sem("tile_ready"), 1)

            mix_bank = [None]
            for l in range(8):
                level(1, l)
                if l == 4:
                    pe.wait_ge(sem("cq_squared"), 1)
                    pe.wait_ge(sem("hg_rooted"), 2)
                    sum_over_features(MSQ, 2, ps[2]).then_inc(sem("cq_summed"), 1)
                hgrn_products(60 + 20 * l // 8, 60 + 20 * (l + 1) // 8)

            def query_parts(j):
                if j == 0:
                    pe.wait_ge(sem("cq_normed"), 1)
                    pe.wait_ge(sem("ld_mla"), 4 * 16)
                    pe.wait_ge(sem("hg_masked"), 16)
                if j >= 2:
                    pe.wait_ge(sem("q_copied"), 2 * (j - 1))
                for k in range(2):
                    q = pe.matmul(ps[6 + j % 2], WUQ[:, k, P * j:P * (j + 1)], CQ[:, k, :], start=k == 0, stop=k == 1)
                q.then_inc(sem("queries_done"), 1)

            KEYS = [(0, P), (P, 192)]
            pe.wait_ge(sem("cq_rooted"), 1)
            hgrn_turn(1)
            query_parts(0)
            part(G_KR, 0, 8, KEYS)
            hgrn_added(1)
            query_parts(1)
            part(G_KR, 8, 16, KEYS)
            query_parts(2)
            hgrn_out(1)
            query_parts(3)
            mix_products(0, 4)
            pe.wait_ge(sem("ckv_squared"), 1)
            pe.wait_ge(sem("q_copied"), 6)
            pe.matmul(ps[6], ones, MSK, start=True, stop=True).then_inc(sem("ckv_summed"), 1)
            mix_products(4, 8)
            hgrn_squares(1)
            mix_products(8, 16)
            pe.wait_ge(sem("ckv_normed"), 1)
            pe.wait_ge(sem("hg_rooted"), 4)
            for j in range(4):
                if j >= 2:
                    pe.wait_ge(sem("k_copied"), 2 * (j - 1))
                pe.matmul(ps[2 + j % 2], WUK[:, P * j:P * (j + 1)], CKV, start=True, stop=True).then_inc(sem("k_done"), 1)
            pe.wait_ge(sem("ckv_rooted"), 1)
            pe.wait_ge(sem("q_copied"), 8)
            for t in range(4):
                if t >= 2:
                    pe.wait_ge(sem("vm_copied"), t - 1)
                pe.matmul(ps[6 + t % 2], CKV[:, P * t:P * (t + 1)], WUV, start=True, stop=True
                          ).then_inc(sem("vm_done"), 1)
            pe.wait_ge(sem("rope_weights"), 1)
            pe.wait_ge(sem("hg_out"), 2)
            for j in range(2):
                if j:
                    mix_products(16, 24)
                    pe.wait_ge(sem("rope_done"), 5)
                for w, b in ((WROPE, ps[4]), (WROT, ps[5])):
                    for k in range(2):
                        q = pe.matmul(b, w[:, k, P * j:P * (j + 1)], CQ[:, k, :], start=k == 0, stop=k == 1)
                q.then_inc(sem("qr_done"), 1)
            mix_products(24, 32)
            pe.wait_ge(sem("k_copied"), 8)
            pe.wait_ge(sem("rope_done"), 9)
            pe.wait_ge(sem("vm_copied"), 4)
            def score(i):
                h, qb = i // 4, i % 4
                w = P * (qb + 1)
                if i >= 2:
                    pe.wait_ge(sem("prob"), i - 1)
                pe.matmul(ps[2 + i % 2][:, 0:w], QH[0:QK, h, P * qb:P * (qb + 1)], KHD[0:QK, h, 0:w],
                          start=True, stop=True).then_inc(sem("score"), 1)

            score(0)
            for i in range(4 * ML):
                h, qb = i // 4, i % 4
                if i + 1 < 4 * ML:
                    score(i + 1)
                mix_products(32 + 5 * i, 37 + 5 * i)
                pe.wait_ge(sem("prob_scaled"), i + 1)
                if i >= 2:
                    pe.wait_ge(sem("pt_copied"), i - 1)
                for kb in range(qb + 1):
                    q = pe.transpose(ps[4 + i % 2][:, P * kb:P * (kb + 1)], PRB[:, i % 2, P * kb:P * (kb + 1)], ident)
                q.then_inc(sem("prob_turned"), 1)
                if qb < 3:
                    continue
                pe.wait_ge(sem("pt_copied"), i + 1)
                if h >= 2:
                    pe.wait_ge(sem("oc_copied"), h - 1)
                b = ps[6 + h % 2][64 * (h % 2):64 * (h % 2) + 64, :]
                for kb in range(4):
                    q = pe.matmul(b[:, P * kb:T], VM[:, kb, 64 * h:64 * (h + 1)], PT[:, kb, P * kb:T],
                                  start=kb == 0, stop=kb == 3)
                q.then_inc(sem("oc_done"), 1)

            mix_products(192, 208)
            pe.wait_ge(sem("oc_copied"), ML)
            pe.wait_ge(sem("ld_x2"), 16)
            for d in range(KD):
                if d >= 4:
                    pe.wait_ge(sem("xt_copied"), KD + d - 3)
                for t in range(4):
                    q = pe.transpose(ps[2 + d % 4][:, P * t:P * (t + 1)], XTOK2[:, t, P * d:P * (d + 1)], ident)
                q.then_inc(sem("xt_turned"), 1)
            mix_products(208, 288)
            for q_ in range(4):
                project(G_OUT + q_, PAIR, hhi, hlo, None if q_ else "y_split")

            pe.wait_ge(sem("squares_added"), 7)
            pe.wait_ge(sem("oc_copied"), ML)
            pe.matmul(ps[6], ones, SQUARES, start=True, stop=True).then_inc(sem("residual_summed"), 1)
            for j in range(NF):
                project(G_UP + j, PAIR, hhi, hlo, None if j else "h2_split")

            def turn_rows(d):
                pe.wait_ge(sem("x2_weighted"), d + 1)
                if d >= 4:
                    pe.wait_ge(sem("rows_copied"), d - 3)
                for t in range(4):
                    q = pe.transpose(ps[2 + d % 4][:, P * t:P * (t + 1)], X1[:, d, P * t:P * (t + 1)], ident)
                q.then_inc(sem("rows_turned"), 1)

            for q_ in range(4):
                o = [bank(), bank()]
                for third in range(3):
                    g = G_DOWN + 3 * q_ + third
                    pe.wait_ge(sem("w_lo"), split_no[g] + 1)
                    nk, ncols = groups[g][2], groups[g][3]
                    if q_ == 0:
                        pe.wait_ge(sem("act_split"), 8 * third + nk)
                    for m in range(2):
                        for k in range(nk):
                            kk = 8 * third + k
                            q = mm3(pe, o[m], g, k, P * m, P * (m + 1), acthi[:, kk, :], actlo[:, kk, :],
                                    kk == 0, kk == NF - 1, ncols)
                        if third == 2:
                            q.then_inc(sem("tile_ready"), 1)
                    if third < 2:
                        q.then_inc(sem("down_part"), 1)
                    if q_ and third == 0:
                        turn_rows(2 * q_ - 2)
                        turn_rows(2 * q_ - 1)
            turn_rows(6)
            turn_rows(7)
            pe.wait_ge(sem("squares_added"), 14)
            for t in range(4):
                q = pe.matmul(ps[6][:, t:t + 1], SQUARES[:, P * t:P * (t + 1)], ones[:, 0:1], start=True, stop=True)
            q.then_inc(sem("residual_summed"), 1)

        @block.scalar
        def _(act):
            chain = [0]

            def link(ins):
                chain[0] += 1
                ins.then_inc(sem("act_chain"), 1)
                act.wait_ge(sem("act_chain"), chain[0])

            split_order = list(split_no)
            staged = [0]

            def stage(upto):
                while staged[0] <= min(upto, len(split_order) - 1):
                    n, g = staged[0], split_order[staged[0]]
                    w = groups[g][2] * groups[g][3]
                    act.wait_ge(sem(f"w_landed{g % 2}"), landings[g])
                    if before[n] is not None:
                        act.wait_ge(*used[before[n]])
                        act.wait_ge(sem("w_lo"), before[n] + 1)
                    act.activation(whi[:, g % 2, 0:w], wring[:, g % 2, 0:w], ACT.Copy).then_inc(sem("w_hi"), 1)
                    staged[0] += 1

            tile_no = [0]

            def tile():
                i = tile_no[0]
                tile_no[0] += 1
                act.wait_ge(sem("tile_ready"), i + 1)
                return ps[i % 2], sem(f"bank_free{i % 2}")

            act.dma_start(const[:], a["const_f"]).then_inc(sem("ld_const"), 16)
            act.dma_start(xtok, a["x"][0].rearrange("(a p) d -> p a d", p=P)).then_inc(sem("ld_x"), 16)

            act.wait_ge(sem("vec_in_psum"), 1)
            act.activation(vec[:], ps[6][:, 0:V_ROWS], ACT.Copy)
            act.activation(convv[:, 0, :], ps[6][:, 128:216], ACT.Copy)
            link(act.activation(convv[:, 1, :], ps[6][:, 256:344], ACT.Copy))
            act.activation(small[:, 32:40], col(V_C, 8), ACT.Sigmoid).then_inc(sem("vec_turned"), 1)
            act.wait_ge(sem("xt_copied"), KD)
            act.activation(sqT, xT, ACT.Square).then_inc(sem("x_squared"), 1)
            act.wait_ge(sem("lb_zero"), 1)
            act.activation(small[:, 44:48], small[:, 40:44], ACT.Exp).then_inc(sem("lb_exp"), 1)
            act.wait_ge(sem("cond_ready"), 1)
            for n, g in enumerate(DVE_ADA):
                if n == 2:
                    act.wait_ge(sem("x_summed"), 1)
                    act.activation(rstd, ps[6][:], ACT.Sqrt, bias=EPS, scale=1.0 / D).then_inc(sem("x_rooted"), 1)
                act.wait_ge(*ada_landed(g))
                for k in range(KD):
                    wk = ada_slot(g)[:, 256 * k:256 * (k + 1)]
                    q = act.activation(wk, wk, ACT.Copy, scale=cond[:, k:k + 1])
                q.then_inc(sem("ada_weighed"), 1)
            stage(0)
            for d in range(KD):
                act.wait_ge(sem("mod_read"), 1)
                act.wait_ge(sem("x_normed"), 1)
                act.activation(sqT[:, d, :], sqT[:, d, :], ACT.Identity, scale=mod[:, 8 + d:9 + d], bias=mod[:, d:d + 1]
                               ).then_inc(sem("h_value"), 1)
                act.wait_ge(sem("h_value"), d + 1)
                act.activation(hhi[:, d, :], sqT[:, d, :], ACT.Copy).then_inc(sem("h_hi"), 1)

            stage(1)
            act.wait_ge(sem("rw_mixed"), 2)
            act.activation(LORA[0:64, :], LORA[0:64, :], ACT.Tanh).then_inc(sem("lora_in"), 1)
            act.activation(GL, GL, ACT.Sigmoid).then_inc(sem("lora_in"), 1)
            stage(3)
            for j in range(RW_TILES):
                act.wait_ge(sem("lora_out"), 2 * j + 2)
                act.activation(DEC[:, j, :], ps[2 + j % 2][:], ACT.Sigmoid, bias=col(V_W0 + j)).then_inc(sem("lora_read"), 1)
                act.activation(AA[:, j, :], ps[4 + j % 2][:], ACT.Sigmoid, bias=col(V_A0 + j)).then_inc(sem("lora_read"), 1)
            stage(5)
            for j in range(RW_TILES):
                act.wait_ge(sem("kk_summed"), j + 1)
                act.activation(outs[:, j, :], ps[6 + j % 2][:], ACT.Sqrt).then_inc(sem("kk_norm_read"), 1)
            stage(6)
            tile_no[0] += 14

            def decays(j):
                if j == 0:
                    act.wait_ge(sem("log_summed"), RW_TILES)
                else:
                    act.wait_ge(sem("rw_tildes"), j)
                act.activation(PP, DEC[:, j, :], ACT.Exp, scale=-E_HALF)
                act.activation(PINV, DEC[:, j, :], ACT.Exp, scale=E_HALF).then_inc(sem("decay_ready"), 1)

            def hgrn_tile(u, m):
                h, part_ = HG_GROUPS[u]
                act.wait_ge(sem("rw_out"), h + 1)
                bk, free = tile()
                if part_ == 0 and m == 0:
                    act.activation(HQ[:, h, :], bk[:], ACT.Copy).then_inc(free, 1)
                elif part_ == 0:
                    act.activation(HF[:, h, :], bk[:], ACT.Sigmoid)
                    act.activation(HK[:, h, :], bk[:], ACT.Sigmoid, scale=-1.0).then_inc(free, 1)
                elif m == 0:
                    act.activation(HV[:, h, :], bk[:], ACT.Copy).then_inc(free, 1)
                else:
                    act.activation(HO[:, h, :], bk[:], ACT.Sigmoid).then_inc(sem("hg_og"), 1)

            decays(0)
            for j in range(RW_TILES):
                def token_major(n):
                    act.wait_ge(sem("tok_turned"), 4 * j + n + 1)
                    src = ps[6 + n % 2][:]
                    if n == 0:
                        dst, src = AV[:, :, 0:64], src.rearrange("p (i f) -> p i f", i=8)
                    else:
                        dst = (VTK, KTOK[0], KTOK[1])[n - 1]
                        src = src.rearrange("p (q f) -> p q f", q=PAIRS)
                    act.activation(dst, src, ACT.Copy).then_inc(sem("tok_copied"), 1)

                token_major(0)
                token_major(1)
                for l in range(6):
                    for half in range(2):
                        act.wait_ge(sem("t_turned"), 2 * (6 * j + l) + half + 1)
                        dst = (TM if l == 0 else TT)[:, 4 * half:4 * half + 4, :]
                        act.activation(dst, ps[2 + half][:].rearrange("p (i t) -> p i t", i=4), ACT.Copy
                                       ).then_inc(sem("t_copied"), 1)
                    if l == 2:
                        token_major(2)
                        token_major(3)
                    if l == 3 and j + 1 < RW_TILES:
                        decays(j + 1)
                    if l == 4:
                        stage(7 + j)
                act.wait_ge(sem("akv_done"), j + 1)
                act.activation(AV[:, :, 64:128], ps[6][:].rearrange("p (i f) -> p i f", i=8), ACT.Copy
                               ).then_inc(sem("akv_copied"), 1)
                for half in range(2):
                    act.wait_ge(sem("wy_done"), 2 * j + half + 1)
                    act.activation(WY[:, 4 * half:4 * half + 4, :], ps[2 + half][:].rearrange("p (i t) -> p i t", i=4),
                                   ACT.Copy).then_inc(sem("wy_copied"), 1)
                if j == 0:
                    for k in range(2):
                        bk, free = tile()
                        act.activation(CQ[:, k, :], bk[:], ACT.Copy).then_inc(free, 1)
                else:
                    hgrn_tile(j - 1, 0)
                    hgrn_tile(j - 1, 1)
                if j == 3:
                    stage(11)
                act.wait_ge(sem("y_out"), j + 1)
                for h in range(2):
                    hs = slice(64 * h, 64 * h + 64)
                    q = act.activation(YV[hs, j, :], ps[4 + h][hs, :], ACT.Copy)
                q.then_inc(sem("y_in"), 1)
                act.wait_ge(sem("stat"), 2 * j + 2)
                act.activation(YSQ[:, j, :], (ps[3] if j == 3 else ps[0])[:], ACT.Sqrt, bias=REPS, scale=1.0 / CH
                               ).then_inc(sem("y_rooted"), 1)

            act.wait_ge(sem("angles"), 1)
            act.activation(SIN, SIN, ACT.Sin)
            act.activation(COS, COS, ACT.Sin).then_inc(sem("sines"), 1)

            def hgrn_token_major(p):
                for n in range(4):
                    act.wait_ge(sem("hg_tok_turned"), 4 * p + n + 1)
                    dst = (HVT if n < 2 else HKT)[:, 2 * p + n % 2, :, :]
                    act.activation(dst, ps[2 + n % 2][:].rearrange("p (c t) -> p c t", c=4), ACT.Copy
                                   ).then_inc(sem("hg_tok_copied"), 1)

            def hgrn_norms(p):
                if p:
                    act.wait_ge(sem("hg_out"), 1)
                for h in (2 * p, 2 * p + 1):
                    act.wait_ge(sem("hg_o"), h + 1)
                    act.activation(HSCR[:, h % 2, :], ps[4 + h % 2][:], ACT.Square).then_inc(sem("hg_squared"), 1)
                for h in (2 * p, 2 * p + 1):
                    act.wait_ge(sem("hg_summed"), h + 1)
                    act.activation(HSCR[:, h % 2, :], ps[2 + h % 2][:], ACT.Sqrt, bias=EPS, scale=1.0 / P
                                   ).then_inc(sem("hg_rooted"), 1)

            for u in (3, 4, 5):
                stage(9 + u)
                hgrn_tile(u, 0)
                hgrn_tile(u, 1)
            hgrn_token_major(0)
            stage(15)
            hgrn_tile(6, 0)
            hgrn_norms(0)
            hgrn_tile(6, 1)
            act.activation(MSQ, CQ, ACT.Square).then_inc(sem("cq_squared"), 1)
            stage(16)
            hgrn_tile(7, 0)
            act.wait_ge(sem("cq_summed"), 1)
            act.wait_ge(sem("hg_out"), 1)
            act.activation(MRS[:, 0, :], ps[2][:], ACT.Sqrt, bias=EPS, scale=0.5 / P).then_inc(sem("cq_rooted"), 1)
            hgrn_tile(7, 1)
            hgrn_token_major(1)

            def mix_gates(x0, x1):
                for x in range(x0, x1):
                    block, y = x // 48, x % 48
                    if x % 16 == 0:
                        stage(17 + x // 16 + 1)
                    if y == 16:
                        if block:
                            act.wait_ge(sem("tile_ready"), MIX_TILE + 8 * block)
                        if block == 4:
                            act.wait_ge(sem("o_value"), 1)
                        b = MIX_BLOCKS[block][1]
                        act.activation(ohi[:], outs[:, 4 * b:4 * b + 4, :], ACT.Copy).then_inc(sem("o_hi"), 1)
                    if y < 32 and x % 8 == 7:
                        i = MIX_TILE + 8 * block + y // 8
                        act.wait_ge(sem("tile_ready"), i + 1)
                        if block:
                            act.wait_ge(sem("gates_used"), block)
                        act.activation(GATE[:, y // 8, :], ps[i % 2][:], ACT.Sigmoid).then_inc(sem(f"bank_free{i % 2}"), 1)

            def copy_queries(j):
                act.wait_ge(sem("queries_done"), j + 1)
                for i in range(2):
                    act.activation(QH[0:64, 2 * j + i, :], ps[6 + j % 2][64 * i:64 * i + 64, :], ACT.Copy
                                   ).then_inc(sem("q_copied"), 1)

            stage(17)
            copy_queries(0)
            bk, free = tile()
            act.activation(CKV, bk[:], ACT.Copy).then_inc(free, 1)
            act.wait_ge(sem("bank_free0"), 17)
            act.activation(MSK, CKV, ACT.Square).then_inc(sem("ckv_squared"), 1)
            copy_queries(1)
            bk, free = tile()
            act.activation(KR[0:32, :], bk[0:32, :], ACT.Copy)
            act.activation(KRR[0:32, :], bk[32:64, :], ACT.Copy).then_inc(free, 1)
            copy_queries(2)
            copy_queries(3)
            act.wait_ge(sem("ckv_summed"), 1)
            act.activation(MRS[:, 1, :], ps[6][:], ACT.Sqrt, bias=EPS, scale=1.0 / P).then_inc(sem("ckv_rooted"), 1)
            hgrn_norms(1)
            mix_gates(0, 16)
            for j in range(4):
                act.wait_ge(sem("k_done"), j + 1)
                for i in range(2):
                    act.activation(KHD[0:64, 2 * j + i, :], ps[2 + j % 2][64 * i:64 * i + 64, :], ACT.Copy
                                   ).then_inc(sem("k_copied"), 1)
            for t in range(4):
                act.wait_ge(sem("vm_done"), t + 1)
                act.activation(VM[:, t, :], ps[6 + t % 2][:], ACT.Copy).then_inc(sem("vm_copied"), 1)
            act.wait_ge(sem("rope_done"), 1)
            mix_gates(16, 32)

            def prob(i):
                w = P * (i % 4 + 1)
                act.wait_ge(sem("row_max"), i + 1)
                if i >= 2:
                    act.wait_ge(sem("prob_turned"), i - 1)
                act.activation(PRB[:, i % 2, 0:w], ps[2 + i % 2][:, 0:w], ACT.Exp, bias=small[:, 48 + i % 2:49 + i % 2],
                               scale=MLA_SCALE, accum_out=small[:, 50 + i % 2:51 + i % 2]).then_inc(sem("prob"), 1)

            prob(0)
            for i in range(4 * ML):
                h, qb = i // 4, i % 4
                if i + 1 < 4 * ML:
                    prob(i + 1)
                act.wait_ge(sem("prob_turned"), i + 1)
                if qb == 0 and h:
                    act.wait_ge(sem("oc_done"), h)
                act.activation(PT[:, 0:qb + 1, P * qb:P * (qb + 1)],
                               ps[4 + i % 2][:, 0:P * (qb + 1)].rearrange("p (k t) -> p k t", k=qb + 1), ACT.Copy
                               ).then_inc(sem("pt_copied"), 1)
                mix_gates(32 + 5 * i, 37 + 5 * i)
            mix_gates(192, 272)
            act.wait_ge(sem("tile_ready"), MIX_TILE + 44)
            for d in range(KD):
                act.wait_ge(sem("y_value"), d + 1)
                act.activation(hhi[:, d, :], YT[:, d, :], ACT.Copy).then_inc(sem("y_hi"), 1)
                if d == 3:
                    mix_gates(272, 288)
            n = 35
            tile_no[0] = MIX_TILE + 48

            def square(d, first):
                act.wait_ge(sem("residual_tile"), first + d + 1)
                if d >= 3:
                    act.wait_ge(sem("squares_added"), first // KD * 7 + d - 2)
                q = act.activation(SQUARES if d == 0 else SQUARE[:, d % 2, :], X1[:, d, :], ACT.Square)
                q.then_inc(sem("squared"), 1)

            for q_ in range(4):
                stage(n + 1)
                n += 1
                tile_no[0] += 2
                for d in (2 * q_, 2 * q_ + 1):
                    square(d, 0)
            act.wait_ge(sem("residual_summed"), 1)
            act.activation(ROOT, ps[6][:], ACT.Sqrt, bias=EPS, scale=1.0 / D).then_inc(sem("residual_rooted"), 1)

            def hi_of_h2(d):
                act.wait_ge(sem("h2_value"), d + 1)
                act.activation(hhi[:, d, :], SQ1[:, d, :], ACT.Copy).then_inc(sem("h2_hi"), 1)

            for d in range(KD):
                act.wait_ge(sem("x1_normed"), d + 1)
                act.activation(SQ1[:, d, :], SQ1[:, d, :], ACT.Identity, scale=mod[:, 32 + d:33 + d],
                               bias=mod[:, 24 + d:25 + d]).then_inc(sem("h2_value"), 1)
                if d:
                    hi_of_h2(d - 1)
            hi_of_h2(KD - 1)

            def weigh_tiles(q_):
                for d in (2 * q_, 2 * q_ + 1):
                    square(d, KD)
                    act.wait_ge(sem("squared"), KD + d + 1)
                    act.activation(X1[:, d, :], X1[:, d, :], ACT.Copy, scale=col(V_FIN + d)).then_inc(sem("x2_weighted"), 1)
                for d in (2 * q_, 2 * q_ + 1):
                    act.wait_ge(sem("rows_turned"), d + 1)
                    for b in range(2):
                        q = act.activation(RESULT[b][:, :, P * d:P * (d + 1)],
                                           ps[2 + d % 4][:, 256 * b:256 * (b + 1)].rearrange("p (b n) -> p b n", b=2), ACT.Copy)
                    q.then_inc(sem("rows_copied"), 1)

            stage(n + 1)
            for j in range(NF):
                n += 1
                tile_no[0] += 2
                act.wait_ge(sem("conv_gate"), j + 1)
                act.activation(tail[:, 1, :], CG[:, j % 2, :], ACT.Sigmoid).then_inc(sem("gate_sig"), 1)
                stage(n + 1)
                act.wait_ge(sem("act_value"), j + 1)
                act.activation(acthi[:, j, :], CV[:, j % 2, :], ACT.Copy).then_inc(sem("act_hi"), 1)
            for q_ in range(5):
                if q_ < 4:
                    for third in range(3):
                        stage(n + 1)
                        n += 1
                        if third == 0 and q_:
                            weigh_tiles(q_ - 1)
                else:
                    weigh_tiles(3)
            act.wait_ge(sem("residual_summed"), 2)
            act.activation(RSTD, ps[6][:, 0:4], ACT.Sqrt, bias=EPS, scale=1.0 / D).then_inc(sem("residual_rooted"), 1)
            act.wait_ge(sem("x2_rstd"), 1)
            act.wait_ge(sem("rows_copied"), KD)
            for t in (2, 3):
                row = RESULT[1][:, t - 2, :]
                act.activation(row, row, ACT.Copy, scale=RSTD[:, t:t + 1]).then_inc(sem("rows_scaled1"), 1)

        @block.vector
        def _(dve):
            chain = [0]

            def link(ins):
                chain[0] += 1
                ins.then_inc(sem("dve_chain"), 1)
                dve.wait_ge(sem("dve_chain"), chain[0])

            tile_no = [0]

            def tile():
                i = tile_no[0]
                tile_no[0] += 1
                dve.wait_ge(sem("tile_ready"), i + 1)
                return ps[i % 2], sem(f"bank_free{i % 2}")

            mul, add, sub = ALU.mult, ALU.add, ALU.subtract
            dve.memset(small[:, 0:1], NORM_EPS)
            dve.memset(small[:, 1:2], RWKV_EPS)
            for d in range(KD):
                dve.wait_ge(sem("xt_turned"), d + 1)
                dve.tensor_copy(xT[:, d, :], ps[2 + d % 4][:]).then_inc(sem("xt_copied"), 1)
            dve.wait_ge(sem("vec_turned"), 1)
            dve.tensor_tensor(cond[:], small[:, 32:40], col(V_C, 8), mul).then_inc(sem("cond_ready"), 1)
            dve.tensor_tensor(small[:, 40:44], col(V_LB, 4), col(V_LB, 4), sub).then_inc(sem("lb_zero"), 1)
            dve.wait_ge(sem("lb_exp"), 1)
            link(dve.reciprocal(small[:, 56:60], small[:, 44:48]))
            link(dve.tensor_tensor(small[:, 60:64], small[:, 56:60], small[:, 44:48], mul))
            link(dve.tensor_tensor(LBV, small[:, 60:64], small[:, 60:64], sub))
            link(dve.tensor_scalar(OMLB, LBV, -1.0, 1.0, mul, add))
            link(dve.tensor_scalar(ONE_MU, col(V_MU, 14), -1.0, 1.0, mul, add))
            link(dve.tensor_scalar(small[:, 12:16], col(V_KA, 4), -1.0, 1.0, mul, add))
            for n, g in enumerate(DVE_ADA):
                w = ada_slot(g)
                if n == 3:
                    dve.wait_ge(sem("x_rooted"), 1)
                    link(dve.reciprocal(rstd, rstd))
                    dve.tensor_tensor(sqT, xT, rstd.unsqueeze(1).broadcast_to([P, KD, T]), mul).then_inc(sem("x_normed"), 1)
                dve.wait_ge(sem("ada_weighed"), n + 1)
                for half in (1024, 512, 256):
                    link(dve.tensor_tensor(w[:, 0:half], w[:, 0:half], w[:, half:2 * half], add))
                dve.sem_inc(sem("ada_dve"), 1)
            dve.wait_ge(sem("ada_used"), 8)
            link(dve.tensor_tensor(mod[:, 0:16], ps[7][:, 0:16], vec[:, 0:16], add))
            dve.tensor_scalar(mod[:, 8:16], mod[:, 8:16], 1.0, None, add).then_inc(sem("mod_read"), 1)
            for d in range(KD):
                dve.wait_ge(sem("h_hi"), d + 1)
                dve.tensor_tensor(hlo[:, d, :], sqT[:, d, :], hhi[:, d, :].bitcast(F32), sub).then_inc(sem("h_split"), 1)

            def chunks(v):
                return v.rearrange("p (c t) -> p c t", c=CHUNKS)

            def key_norm(j):
                nrm = outs[:, j, :]
                dve.wait_ge(sem("kk_norm_read"), j + 1)
                link(dve.tensor_scalar(nrm, nrm, 1e-12, None, ALU.max))
                link(dve.reciprocal(nrm, nrm))
                link(dve.tensor_tensor(KK[:, j, :], KK[:, j, :], nrm, mul))
                link(dve.tensor_scalar(nrm, AA[:, j, :], col(V_KA + j), small[:, 12 + j:13 + j], mul, add))
                link(dve.tensor_tensor(K[:, j, :], K[:, j, :], nrm, mul))
                link(dve.tensor_tensor(AA[:, j, :], AA[:, j, :], KK[:, j, :], mul))
                link(dve.tensor_scalar(KK[:, j, :], KK[:, j, :], -1.0, None, mul))

            for n, x in enumerate((12, 13, 4, 5, 6, 7, 0, 1, 2, 3, 8, 9, 10, 11)):
                bk, free = tile()
                dst = LORA if x == 12 else GL if x == 13 else (R, K, V)[x // 4][:, x % 4, :]
                if x == 12:
                    dve.wait_ge(sem("h_split"), KD)
                link(dve.tensor_scalar(dst, bk[:], ONE_MU[:, x:x + 1], None, mul))
                link(dve.scalar_tensor_tensor(dst[:, 1:T], bk[:, 0:T - 1], col(V_MU + x), dst[:, 1:T], mul, add))
                dve.sem_inc(free, 1)
                dve.sem_inc(sem("rw_mixed"), 1)
                if 4 <= x < 8:
                    j = x - 4
                    link(dve.tensor_scalar(KK[:, j, :], K[:, j, :], col(V_KK + j), None, mul))
                    dve.tensor_tensor(outs[:, j, :], KK[:, j, :], KK[:, j, :], mul).then_inc(sem("kk_squared"), 1)
                if x == 0:
                    link(dve.memset(SCR, 1.0))
                    link(dve.memset(chunks(SCR)[:, :, 0:1], 0.0))
                    dve.wait_ge(sem("lora_read"), 8)
                    for j in range(RW_TILES):
                        q = dve.tensor_tensor_scan(DEC[:, j, :], SCR, DEC[:, j, :], 0.0, mul, add)
                        q.then_inc(sem("log_summed"), 1)
                    dve.wait_ge(sem("log_summed"), RW_TILES)
                if x in (2, 8):
                    key_norm(int(x == 8))

            def hats(j):
                ar_ = AR[j % 2]
                dve.wait_ge(sem("decay_ready"), j + 1)
                if j == 0:
                    dve.wait_ge(sem("pad_zero"), 1)
                rr = R[:, j, :].rearrange("p (q t) -> p q t", q=PAIRS)
                pp = PP.rearrange("p (q t) -> p q t", q=PAIRS)
                dve.tensor_tensor(ar_[:, :, 1, :], rr, pp, mul)
                for c in range(2):
                    ar = ar_[:, :, 0, 64 * c:64 * c + 64]
                    kk = KK[:, j, :].rearrange("p (q c t) -> p q c t", q=PAIRS, c=2)[:, :, c, :]
                    pc = PP.rearrange("p (q c t) -> p q c t", q=PAIRS, c=2)[:, :, c, :]
                    dve.tensor_tensor(ar[:, :, 1:64], kk[:, :, 1:64], pc[:, :, 0:63], mul)
                    dve.tensor_copy(ar[:, :, 0:1], kk[:, :, 0:1])
                for h in range(2):
                    hs = slice(64 * h, 64 * h + 64)
                    dve.tensor_tensor(PAD[hs, h, :], AA[hs, j, :], PINV[hs, :], mul)
                    q = dve.tensor_tensor(PAD[hs, 2 + h, :], K[hs, j, :], PINV[hs, :], mul)
                q.then_inc(sem("rw_hats"), 1)

            def centre(j, bank_):
                y = YV[:, j, :]
                dve.wait_ge(sem("y_in"), j + 1)
                dve.wait_ge(sem("stat"), 2 * j + 1)
                link(dve.scalar_tensor_tensor(y, bank_[:], -1.0 / CH, y, mul, add))
                dve.tensor_tensor(YSQ[:, j, :], y, y, mul).then_inc(sem("y_centred"), 1)

            def bonus(j):
                dve.wait_ge(sem("bonus_sum"), j + 1)
                dve.tensor_tensor(BONUS[:, j, :], ps[6][:], V[:, j, :], mul).then_inc(sem("bonus_ready"), 1)

            def finish(j, bank_, step):
                y, root = YV[:, j, :], YSQ[:, j, :]
                if step == 0:
                    dve.wait_ge(sem("y_rooted"), j + 1)
                    link(dve.reciprocal(root, root))
                elif step == 1:
                    link(dve.tensor_tensor(y, y, root, mul))
                    link(dve.tensor_scalar(y, y, col(V_LNW + j), col(V_LNB + j), mul, add))
                else:
                    dve.wait_ge(sem("bonus_ready"), j + 1)
                    link(dve.tensor_tensor(y, y, BONUS[:, j, :], add))
                    dve.wait_ge(sem("g_out"), j + 1)
                    dve.tensor_tensor(outs[:, j, :], y, bank_[:], mul).then_inc(sem("rw_out"), 1)

            last = LAST.unsqueeze(2).broadcast_to([P, CHUNKS, CH])

            def tildes(j):
                dve.wait_ge(sem("rw_hats"), j + 1)
                if j:
                    dve.wait_ge(sem("tok_turned"), 4 * j)
                link(dve.tensor_copy(LAST.unsqueeze(2), chunks(PP)[:, :, 63:64]))
                for h in range(2):
                    hs = slice(64 * h, 64 * h + 64)
                    dve.tensor_tensor(chunks(BH)[hs], chunks(PAD[:, h, :])[hs], last[hs], mul)
                    q = dve.tensor_tensor(chunks(KH)[hs], chunks(PAD[:, 2 + h, :])[hs], last[hs], mul)
                q.then_inc(sem("rw_tildes"), 1)

            def output_gates(h):
                dve.wait_ge(sem("hg_og"), h + 1)
                dve.wait_ge(sem("tile_ready"), HG_TILE + 2 * HG_GROUPS.index((h, 1)) + 2)
                dve.tensor_tensor(HO[:, h, :], HO[:, h, :], ps[1][:], mul).then_inc(sem("bank_free1"), 1)

            def rotary_angles():
                dve.wait_ge(sem("ld_pos"), 16)
                magic, c1, c2 = 12582912.0, 6.28125, 0.0019350051879882812
                c3 = 2 * np.pi - c1 - c2
                link(dve.tensor_copy(RED, ANG.bitcast(I32)))
                link(dve.tensor_scalar(ANG, RED, cst("freq"), None, mul))
                for dst, quarter in ((SIN, 0.0), (COS, 0.25)):
                    link(dve.tensor_scalar(RED, ANG, float(1 / (2 * np.pi)), quarter, mul, add))
                    link(dve.tensor_scalar(RED, RED, magic, None, add))
                    link(dve.tensor_scalar(RED, RED, magic, None, sub))
                    link(dve.scalar_tensor_tensor(dst, RED, -c1, ANG, mul, add))
                    link(dve.scalar_tensor_tensor(dst, RED, -c2, dst, mul, add))
                    link(dve.scalar_tensor_tensor(dst, RED, -float(c3), dst, mul, add))
                    if quarter:
                        link(dve.tensor_scalar(dst, dst, float(np.pi / 2), None, add))
                    link(dve.tensor_scalar(dst, dst, 3.1415925, -3.1415925, ALU.min, ALU.max))
                dve.sem_inc(sem("angles"), 1)

            hats(0)
            for j in range(RW_TILES):
                for i in range(8):
                    dve.wait_ge(sem("abr_done"), 8 * j + i + 1)
                    dve.tensor_tensor(ABR[:, i, :], ps[2 + i % 4][:], cst("rw_mask"), mul).then_inc(sem("abr_copied"), 1)
                    if j and i == 2:
                        centre(j - 1, ps[0])
                    if j and i == 3:
                        bonus(j - 1)
                dve.wait_ge(sem("abr_copied"), 8 * j + 8)
                for half in range(2):
                    x = slice(4 * half, 4 * half + 4)
                    wide = [P, 4, P]
                    link(dve.tensor_tensor(TT[:, x, :], ABR[:, x, 0:P], cst("pair_t").unsqueeze(1).broadcast_to(wide), mul))
                    dve.tensor_tensor(TT[:, x, :], TT[:, x, :], ident.unsqueeze(1).broadcast_to(wide), add
                                      ).then_inc(sem("t_added"), 1)
                for l, n in enumerate((2, 4, 8, 16, 32)):
                    if l == 1:
                        tildes(j)
                    if l >= 2 and j:
                        finish(j - 1, ps[0], l - 2)
                    mask = cst("level")[:, 64 * l:64 * l + 64].unsqueeze(1).broadcast_to([P, 4, 64])
                    for half in range(2):
                        dve.wait_ge(sem("y_done"), 2 * (5 * j + l) + half + 1)
                        dve.tensor_tensor(YH[:, 256 * half:256 * half + 256].rearrange("p (i c) -> p i c", i=4),
                                          ps[4 + half][:, 0:256].rearrange("p (i c) -> p i c", i=4), mask, mul
                                          ).then_inc(sem("y_masked"), 1)
                    for half in range(2):
                        dve.wait_ge(sem("ty_done"), 2 * (5 * j + l) + half + 1)
                        dve.wait_ge(sem("t_copied"), 2 * (6 * j) + 2)
                        first = TM[:, 4 * half:4 * half + 4, :].rearrange("p i (b w n) -> p (i b) w n", w=2, n=n)[:, :, 0, :]
                        dve.tensor_tensor(first, first, ps[4 + half][:, 256:512].rearrange("p (b n) -> p b n", n=n), add
                                          ).then_inc(sem("t_added"), 1)
                if j + 1 < RW_TILES:
                    hats(j + 1)
                c0, c1 = 14 + 10 * j + 2 * (j == 0), min(24 + 10 * j, 48)
                dve.wait_ge(sem("ada_used"), c1 // 2)
                dve.tensor_tensor(mod[:, c0:c1], ps[1][:, c0:c1], vec[:, c0:c1], add).then_inc(sem("mod_read"), 1)
                dve.wait_ge(sem("mod_read"), j + 2)
                dve.wait_ge(sem("mn_done"), j + 1)
                mt = MT.rearrange("p (q c f) -> p q c f", q=PAIRS, c=2)
                nn_ = NN.rearrange("p (q c f) -> p q c f", q=PAIRS, c=2)
                link(dve.tensor_tensor(chunks(MT), cst("eye64").unsqueeze(1).broadcast_to([P, CHUNKS, CH]), last, mul))
                for c in range(2):
                    b = ps[4 + c][:].rearrange("p (w q f) -> p w q f", w=2, q=PAIRS)
                    dve.tensor_tensor(mt[:, :, c, :], mt[:, :, c, :], b[:, 0, :, :], add)
                    link(dve.tensor_copy(nn_[:, :, c, :], b[:, 1, :, :]))
                dve.wait_ge(sem("q_done"), j + 1)
                dve.tensor_tensor(QT[:, j, :].rearrange("p (q t) -> p q t", q=PAIRS),
                                  ps[6][:].rearrange("p (q t) -> p q t", q=PAIRS), AR[j % 2][:, :, 1, :], add).then_inc(sem("q_ready"), 1)
                dve.memset(YH[:, 0:64], 0.0).then_inc(sem("state_ready"), 1)
                dve.tensor_copy(YH[:, 64:128], NN[:, 0:64]).then_inc(sem("state_ready"), 1)
                for c in range(1, CHUNKS - 1):
                    dve.wait_ge(sem("state_step"), 6 * j + c)
                    for h in range(2):
                        hs = slice(64 * h, 64 * h + 64)
                        q = dve.tensor_tensor(YH[hs, 64 * c + 64:64 * c + 128], ps[2 + h][hs, 0:64], NN[hs, 64 * c:64 * c + 64], add)
                    q.then_inc(sem("state_ready"), 1)
                link(dve.tensor_tensor(BONUS[:, j, :], R[:, j, :], K[:, j, :], mul))
                dve.tensor_scalar(BONUS[:, j, :], BONUS[:, j, :], col(V_RK + j), None, mul).then_inc(sem("rk_ready"), 1)
                if j == 2:
                    output_gates(0)
                if j < 2:
                    key_norm(j + 2)
                if j == 3:
                    rotary_angles()
                dve.wait_ge(sem("y_out"), j + 1)

            link(dve.tensor_scalar(mod[:, 32:40], mod[:, 32:40], 1.0, None, add))
            centre(3, ps[2])
            bonus(3)
            for step in range(3):
                finish(3, ps[7], step)
            dve.wait_ge(sem("rw_out"), RW_TILES)

            def halves(v, n):
                return v.rearrange("p h (b w n) -> p (h b) w n", w=2, n=n)

            def bounds(p):
                done = FREE_AT(HG_TILE + 2 * HG_GROUPS.index((2 * p + 1, 0)) + 2)
                dve.wait_ge(sem("bank_free0"), done[0])
                dve.wait_ge(sem("bank_free1"), done[1])
                for h in (2 * p, 2 * p + 1):
                    link(dve.tensor_scalar(HF[:, h, :], HF[:, h, :], OMLB[:, h:h + 1], LBV[:, h:h + 1], mul, add))
                    link(dve.tensor_scalar(HK[:, h, :], HK[:, h, :], OMLB[:, h:h + 1], None, mul))
                two = slice(2 * p, 2 * p + 2)
                link(dve.tensor_scalar(HF[:, two, :], HF[:, two, :], 1e-30, None, ALU.max))
                if p == 0:
                    dve.memset(KN[0], 0.0)
                    dve.memset(KN[1], 0.0)
                dve.memset(SUF[:, two, :], 1.0).then_inc(sem("hg_factors"), 1)
                dve.wait_ge(sem("hg_factors"), 8 * p + 1)

            def factors(p, l):
                n, two = 2 ** (l - 1), slice(2 * p, 2 * p + 2)
                k_, q_, f_, s_ = (halves(v[:, two, :], n) for v in (HK, HQ, HF, SUF))
                kn = halves(KN[l % 2], n)
                if l >= 3:
                    dve.wait_ge(sem("hg_level"), 8 * p + l - 1)
                elif p:
                    dve.wait_ge(sem("hg_level"), 8)
                qc = QC[l % 2].rearrange("p h (b n) -> p (h b) n", n=n)
                dve.tensor_tensor(qc, q_[:, :, 1, :], f_[:, :, 1, :], mul)
                dve.tensor_tensor(kn[:, :, 0, :], k_[:, :, 0, :], s_[:, :, 0, :], mul).then_inc(sem("hg_factors"), 1)
                shape = [P, 2 * T // (2 * n), n]
                link(dve.tensor_tensor(s_[:, :, 0, :], s_[:, :, 0, :], f_[:, :, 1, n - 1:n].broadcast_to(shape), mul))
                link(dve.tensor_tensor(f_[:, :, 1, :], f_[:, :, 1, :], f_[:, :, 0, n - 1:n].broadcast_to(shape), mul))

            def masked(p, l):
                two = slice(2 * p, 2 * p + 2)
                dve.wait_ge(sem("hg_level"), 8 * p + l + 1)
                if l == 0:
                    for h in range(2):
                        q = dve.tensor_tensor(AT[:, 2 * p + h, :, :],
                                              ps[4 + 2 * p + h][:].rearrange("p (c t) -> p c t", c=4),
                                              ident.unsqueeze(1).broadcast_to([P, 4, P]), mul)
                    q.then_inc(sem("hg_masked"), 1)
                    return
                n = 2 ** (l - 1)
                dve.wait_ge(sem("hg_masked"), 8 * p + l)
                mask = consti[:, l - 1, :].unsqueeze(1).broadcast_to([P, 8, 64]).rearrange("p i (b n) -> p i b n", n=n)
                at = AT[:, two, :, :].rearrange("p h c (b w n) -> p (h c) b w n", w=2, n=n)[:, :, :, 1, :]
                dve.copy_predicated(at, mask, ps[7 - l % 2][:].rearrange("p (i b n) -> p i b n", i=8, n=n)
                                    ).then_inc(sem("hg_masked"), 1)

            def hgrn_decayed(p):
                two = slice(2 * p, 2 * p + 2)
                dve.tensor_tensor(HQ[:, two, :], HQ[:, two, :], HF[:, two, :], mul)
                dve.tensor_tensor(HK[:, two, :], HK[:, two, :], SUF[:, two, :], mul).then_inc(sem("hg_tail"), 1)

            def hgrn_states(p):
                for h in (2 * p, 2 * p + 1):
                    dve.wait_ge(sem("hg_added"), h + 1)
                    b = ps[2 + h % 2]
                    dve.tensor_copy(HS[:, h, 1, :], b[:, 0:P]).then_inc(sem("hg_state"), 1)
                    for c in (1, 2):
                        dve.wait_ge(sem("hg_state"), 3 * h + c)
                        dve.scalar_tensor_tensor(HS[:, h, c + 1, :], HS[:, h, c, :], HF[:, h, P * (c + 1) - 1:P * (c + 1)],
                                                 b[:, P * c:P * (c + 1)], mul, add).then_inc(sem("hg_state"), 1)

            def hgrn_normed(p):
                for h in (2 * p, 2 * p + 1):
                    dve.wait_ge(sem("hg_rooted"), h + 1)
                    sc = HSCR[:, h % 2, :]
                    link(dve.reciprocal(sc, sc))
                    link(dve.tensor_tensor(sc, sc, HO[:, h, :], mul))
                    q = dve.scalar_tensor_tensor(outs[:, 4 + h, :], ps[4 + h % 2][:], col(V_HN), sc, mul, mul)
                q.then_inc(sem("hg_out"), 1)

            bounds(0)
            for l in range(8):
                if l < 7:
                    factors(0, l + 1)
                masked(0, l)
                if l == 4:
                    output_gates(1)
            hgrn_decayed(0)
            bounds(1)
            hgrn_states(0)
            for l in range(8):
                if l < 7:
                    factors(1, l + 1)
                if l == 1:
                    hgrn_normed(0)
                masked(1, l)
                if l == 2:
                    output_gates(2)
                if l == 5:
                    dve.wait_ge(sem("cq_rooted"), 1)
                    link(dve.reciprocal(MRS[:, 0, :], MRS[:, 0, :]))
                    for k in range(2):
                        q = dve.scalar_tensor_tensor(CQ[:, k, :], CQ[:, k, :], col(V_QN + k), MRS[:, 0, :], mul, mul)
                    q.then_inc(sem("cq_normed"), 1)
            output_gates(3)
            hgrn_decayed(1)
            hgrn_states(1)
            tile_no[0] = 32

            tile_no[0] += 2
            dve.wait_ge(sem("ckv_rooted"), 1)
            link(dve.reciprocal(MRS[:, 1, :], MRS[:, 1, :]))
            dve.scalar_tensor_tensor(CKV, CKV, col(V_KV), MRS[:, 1, :], mul, mul).then_inc(sem("ckv_normed"), 1)
            dve.wait_ge(sem("ld_rope"), 2 * 16)
            for k in range(2):
                wr = WROPE[:, k, :].rearrange("p (h n) -> p h n", n=ROPE)
                wx = WROT[:, k, :].rearrange("p (h n) -> p h n", n=ROPE)
                dve.tensor_copy(wx[:, :, 0:16], wr[:, :, 16:32])
                q = dve.tensor_copy(wx[:, :, 16:32], wr[:, :, 0:16])
            q.then_inc(sem("rope_weights"), 1)
            hgrn_normed(1)
            dve.wait_ge(sem("sines"), 1)
            link(dve.tensor_scalar(SIN, SIN, cst("rsign"), None, mul))
            q4 = slice(0, ROPE)
            link(dve.tensor_tensor(KR[q4, :], KR[q4, :], COS[q4, :], mul))
            link(dve.tensor_tensor(KRR[q4, :], KRR[q4, :], SIN[q4, :], mul))
            for h in range(ML):
                q = dve.tensor_tensor(KHD[NOPE:QK, h, :], KR[q4, :], KRR[q4, :], add)
            q.then_inc(sem("rope_done"), 1)
            for j in range(2):
                dve.wait_ge(sem("qr_done"), j + 1)
                link(dve.tensor_tensor(ROT[:, 0, :], ps[4][:], COS, mul))
                link(dve.tensor_tensor(ROT[:, 1, :], ps[5][:], SIN, mul))
                for i in range(4):
                    rows = slice(32 * i, 32 * i + 32)
                    q = dve.tensor_tensor(QH[NOPE:QK, 4 * j + i, :], ROT[rows, 0, :], ROT[rows, 1, :], add)
                    q.then_inc(sem("rope_done"), 1)
                dve.wait_ge(sem("rope_done"), 4 * j + 5)

            def mix_gated(x0, x1):
                for x in range(x0, x1):
                    block, y = x // 48, x % 48
                    half, b = MIX_BLOCKS[block]
                    if y == 24:
                        dve.wait_ge(sem("o_hi"), block + 1)
                        dve.tensor_tensor(olo[:], outs[:, 4 * b:4 * b + 4, :], ohi[:].bitcast(F32), sub
                                          ).then_inc(sem("o_split"), 1)
                    if y >= 32 and x % 4 == 3:
                        m = (y - 32) // 4
                        i = MIX_TILE + 8 * block + 4 + m
                        dve.wait_ge(sem("tile_ready"), i + 1)
                        yt = YT[:, 4 * half + m, :]
                        dve.wait_ge(sem("bank_free0"), FREE_AT(i - m)[0])
                        dve.wait_ge(sem("bank_free1"), FREE_AT(i - m)[1])
                        if b == 0:
                            link(dve.tensor_tensor(yt, GATE[:, m, :], ps[i % 2][:], mul))
                        else:
                            link(dve.tensor_tensor(TMP[:, m, :], GATE[:, m, :], ps[i % 2][:], mul))
                            link(dve.tensor_tensor(yt, yt, TMP[:, m, :], add))
                        dve.sem_inc(sem(f"bank_free{i % 2}"), 1)
                        if b == 2:
                            dve.sem_inc(sem("y_value"), 1)
                        if m == 3:
                            dve.sem_inc(sem("gates_used"), 1)

            mix_gated(0, 32)

            def row_max(i):
                w = P * (i % 4 + 1)
                b, s2 = ps[2 + i % 2], i % 2
                dve.wait_ge(sem("score"), i + 1)
                link(dve.tensor_tensor(b[:, w - P:w], b[:, w - P:w], cst("causal"), add))
                link(dve.reduce_max(small[:, 52 + s2:53 + s2], b[:, 0:w], AX.X))
                dve.tensor_scalar(small[:, 48 + s2:49 + s2], small[:, 52 + s2:53 + s2], -MLA_SCALE, None, mul
                                  ).then_inc(sem("row_max"), 1)

            row_max(0)
            for i in range(4 * ML):
                if i + 1 < 4 * ML:
                    row_max(i + 1)
                w, s2, h = P * (i % 4 + 1), i % 2, i // 4
                dve.wait_ge(sem("prob"), i + 1)
                link(dve.reciprocal(small[:, 54 + s2:55 + s2], small[:, 50 + s2:51 + s2]))
                dve.tensor_scalar(PRB[:, s2, 0:w], PRB[:, s2, 0:w], small[:, 54 + s2:55 + s2], None, mul
                                  ).then_inc(sem("prob_scaled"), 1)
                if i % 4 == 3:
                    dve.wait_ge(sem("oc_done"), h + 1)
                    rows = slice(64 * (h % 2), 64 * (h % 2) + 64)
                    dve.tensor_copy(outs[rows, 8 + h // 2, :], ps[6 + h % 2][rows, :]).then_inc(sem("oc_copied"), 1)
                mix_gated(32 + 5 * i, 37 + 5 * i)
            dve.wait_ge(sem("oc_copied"), ML)
            dve.sem_inc(sem("o_value"), 1)

            mix_gated(192, 208)
            for d in range(KD):
                dve.wait_ge(sem("xt_turned"), KD + d + 1)
                dve.tensor_copy(XT2[:, d, :], ps[2 + d % 4][:]).then_inc(sem("xt_copied"), 1)
            mix_gated(208, 272)

            def split_y(d):
                dve.wait_ge(sem("y_hi"), d + 1)
                dve.tensor_tensor(hlo[:, d, :], YT[:, d, :], hhi[:, d, :].bitcast(F32), sub).then_inc(sem("y_split"), 1)

            for d in range(4):
                split_y(d)
            for m in range(4):
                mix_gated(272 + 4 * m, 276 + 4 * m)
                if m:
                    split_y(3 + m)
            split_y(7)
            tile_no[0] = MIX_TILE + 48

            def add_squares(d, first):
                if d:
                    dve.wait_ge(sem("squared"), first + d + 1)
                    if d > 1:
                        dve.wait_ge(sem("squares_added"), (first // KD) * 7 + d - 1)
                    dve.tensor_tensor(SQUARES, SQUARES, SQUARE[:, d % 2, :], add).then_inc(sem("squares_added"), 1)

            for d in range(KD):
                bk, free = tile()
                link(dve.scalar_tensor_tensor(X1[:, d, :], bk[:], mod[:, 16 + d:17 + d], XT2[:, d, :], mul, add))
                dve.sem_inc(free, 1)
                dve.sem_inc(sem("residual_tile"), 1)
                if d:
                    add_squares(d - 1, 0)
            add_squares(7, 0)
            dve.wait_ge(sem("residual_rooted"), 1)
            link(dve.reciprocal(ROOT, ROOT))

            def split_h2(d):
                dve.wait_ge(sem("h2_hi"), d + 1)
                dve.tensor_tensor(hlo[:, d, :], SQ1[:, d, :], hhi[:, d, :].bitcast(F32), sub).then_inc(sem("h2_split"), 1)

            for d in range(KD):
                dve.tensor_tensor(SQ1[:, d, :], X1[:, d, :], ROOT, mul).then_inc(sem("x1_normed"), 1)
                if d > 1:
                    split_h2(d - 2)
            split_h2(6)
            split_h2(7)

            for j in range(NF):
                for f, buf in ((j, CV), (NF + j, CG)):
                    bk, free = tile()
                    o = buf[:, j % 2, :]
                    if j >= 2 and f == j:
                        dve.wait_ge(sem("act_hi"), j - 1)
                    link(dve.tensor_scalar(o, bk[:], convv[:, 1, f:f + 1], convv[:, 1, 44 + f:45 + f], mul, add))
                    link(dve.scalar_tensor_tensor(o[:, 1:T], bk[:, 0:T - 1], convv[:, 0, 44 + f:45 + f], o[:, 1:T], mul, add))
                    link(dve.scalar_tensor_tensor(o[:, 2:T], bk[:, 0:T - 2], convv[:, 0, f:f + 1], o[:, 2:T], mul, add))
                    dve.sem_inc(free, 1)
                dve.sem_inc(sem("conv_gate"), 1)
                dve.wait_ge(sem("gate_sig"), j + 1)
                cv, cg = CV[:, j % 2, :], CG[:, j % 2, :]
                link(dve.tensor_tensor(cg, cg, tail[:, 1, :], mul))
                link(dve.tensor_tensor(cv, cv, cg, mul))
                dve.sem_inc(sem("act_value"), 1)
                dve.wait_ge(sem("act_hi"), j + 1)
                dve.tensor_tensor(actlo[:, j, :], cv, acthi[:, j, :].bitcast(F32), sub).then_inc(sem("act_split"), 1)
            for d in range(KD):
                bk, free = tile()
                link(dve.scalar_tensor_tensor(X1[:, d, :], bk[:], mod[:, 40 + d:41 + d], X1[:, d, :], mul, add))
                dve.sem_inc(free, 1)
                dve.sem_inc(sem("residual_tile"), 1)
                if d:
                    add_squares(d - 1, KD)
            add_squares(7, KD)
            dve.wait_ge(sem("residual_rooted"), 2)
            dve.reciprocal(RSTD, RSTD).then_inc(sem("x2_rstd"), 1)
            dve.wait_ge(sem("x2_rstd"), 1)
            dve.wait_ge(sem("rows_copied"), KD)
            for t in (0, 1):
                row = RESULT[0][:, t, :]
                dve.tensor_scalar(row, row, RSTD[:, t:t + 1], None, mul).then_inc(sem("rows_scaled0"), 1)


_INS = ["x", "c", "positions", "ada_w", "ada_b", "w_in", "rwkv_mu", "rwkv_w0", "rwkv_w2", "rwkv_a0", "rwkv_a2", "rwkv_g2",
        "rwkv_k_k", "rwkv_k_a", "rwkv_r_k", "rwkv_ln_w", "rwkv_ln_b", "hgrn_lb", "hgrn_norm_w", "mla_q_norm_w", "mla_w_uq",
        "mla_kv_norm_w", "mla_w_ukv", "branch_proj_a", "branch_proj_b", "branch_proj_c", "w_out", "ffn_w_up",
        "ffn_conv_w", "ffn_conv_b", "ffn_w_down", "final_norm_w"]
_FLAT = {"c", "ada_b", "rwkv_mu", "rwkv_w0", "rwkv_a0", "rwkv_k_k", "rwkv_k_a", "rwkv_r_k", "rwkv_ln_w", "rwkv_ln_b",
         "hgrn_lb", "hgrn_norm_w", "mla_q_norm_w", "mla_kv_norm_w", "ffn_conv_w", "ffn_conv_b", "final_norm_w"}


def kernel(**inputs):
    import concourse.bacc as bacc
    from concourse.bass_utils import run_bass_kernel_spmd

    nc = bacc.Bacc("TRN2", target_bir_lowering=False, num_devices=1, dynamic_dma_scratch_size=1024)
    arrays = {"const_f": CONST_F, "const_i": CONST_I.reshape(P, 7, CH).reshape(P, 7 * CH)}
    for name in _INS:
        v = np.ascontiguousarray(inputs[name])
        arrays[name] = v.reshape(-1) if name in _FLAT else v
    feed, aps = {}, {}
    for name, v in arrays.items():
        feed["in_" + name] = np.ascontiguousarray(v)
        aps[name] = nc.dram_tensor("in_" + name, v.shape, mybir.dt.from_np(v.dtype), kind="ExternalInput").ap()
    out = nc.dram_tensor("out_y", (1, T, D), F32, kind="ExternalOutput").ap()
    trunk(nc, aps, out)
    r = run_bass_kernel_spmd(nc, [feed], core_ids=[0])
    return r.results[0]["out_y"]
```
